# Optimizing a Trainium2 kernel written in Bass

```python
import jax, jax.numpy as jnp
from jax import lax
import numpy as np

D_MODEL = 1024
BATCH = 1
SEQ = 512
DEPTH = 2

N_MIXERS = 2
N_A_LAYERS = (DEPTH + 1) // 2
N_B_LAYERS = DEPTH // 2
EPS = 1e-6

HG_HEADS = 6
HG_KDIM = 128
HG_VDIM = 128
HG_CHUNK = 64
HG_F = HG_HEADS * HG_KDIM
HG_V = HG_HEADS * HG_VDIM

MLA_HEADS = 6
MLA_Q_LORA = 384
MLA_KV_LORA = 256
MLA_NOPE = 128
MLA_ROPE = 64
MLA_QK = MLA_NOPE + MLA_ROPE
MLA_VDIM = 128
ROPE_THETA = 10000.0
Q_BLOCK = 128

MEM_LEN = 256
MEM_HEADS = 4
MEM_HDIM = 64
MEM_W = MEM_HEADS * MEM_HDIM

MIX_W = 768
OUT_W = MIX_W + MEM_W
HG_IN_W = 2 * HG_F + 2 * HG_V + MEM_W
MLA_IN_W = MLA_Q_LORA + MLA_KV_LORA + MLA_ROPE + MEM_W

D_FF = 2816
CONV_W = 3


def rms_norm(x, g):
    xf = x.astype(jnp.float32)
    y = xf * lax.rsqrt(jnp.mean(xf * xf, axis=-1, keepdims=True) + EPS)
    return (y * g.astype(jnp.float32)).astype(x.dtype)

def rope_tables(positions):
    half = MLA_ROPE // 2
    inv = ROPE_THETA ** (-jnp.arange(half, dtype=jnp.float32) / half)
    ang = positions.astype(jnp.float32)[..., None] * inv
    return jnp.cos(ang)[:, :, None, :], jnp.sin(ang)[:, :, None, :]

def apply_rope(x, cos, sin):
    half = MLA_ROPE // 2
    xf = x.astype(jnp.float32)
    x1, x2 = xf[..., :half], xf[..., half:]
    return jnp.concatenate([x1 * cos - x2 * sin, x1 * sin + x2 * cos], axis=-1).astype(x.dtype)

def hgrn2_mixer(z, lb, onorm_g):
    B, S, _ = z.shape
    C = HG_CHUNK
    N = S // C
    q, f, i, g = jnp.split(z, [HG_F, 2 * HG_F, 2 * HG_F + HG_V], axis=-1)
    q = jax.nn.silu(q.astype(jnp.float32)) * (HG_KDIM ** -0.5)
    fg = lb + (1.0 - lb) * jax.nn.sigmoid(f.astype(jnp.float32))
    k = 1.0 - fg
    logf = jnp.log(fg)
    v = i.astype(jnp.float32)

    def to_chunks(t, d):
        return t.reshape(B, N, C, HG_HEADS, d).transpose(1, 0, 3, 2, 4)

    qc, kc, lc = to_chunks(q, HG_KDIM), to_chunks(k, HG_KDIM), to_chunks(logf, HG_KDIM)
    vc = to_chunks(v, HG_VDIM)
    causal = jnp.tril(jnp.ones((C, C), dtype=bool))[:, :, None]

    def step(state, xs):
        q_, k_, v_, lf = xs
        b = jnp.cumsum(lf, axis=2)
        o_inter = jnp.einsum('bhtk,bhkv->bhtv', q_ * jnp.exp(b), state)
        diff = b[:, :, :, None, :] - b[:, :, None, :, :]
        decay = jnp.exp(jnp.where(causal, diff, -jnp.inf))
        attn = jnp.einsum('bhtk,bhtsk,bhsk->bhts', q_, decay, k_)
        o = o_inter + jnp.einsum('bhts,bhsv->bhtv', attn, v_)
        b_last = b[:, :, -1, :]
        state = state * jnp.exp(b_last)[..., None] + jnp.einsum(
            'bhsk,bhsv->bhkv', k_ * jnp.exp(b_last[:, :, None, :] - b), v_)
        return state, o

    s0 = jnp.zeros((B, HG_HEADS, HG_KDIM, HG_VDIM), jnp.float32)
    _, o = lax.scan(step, s0, (qc, kc, vc, lc))
    o = o.transpose(1, 0, 3, 2, 4).reshape(B, S, HG_HEADS, HG_VDIM)
    gate = g.astype(jnp.float32).reshape(B, S, HG_HEADS, HG_VDIM)
    o = rms_norm(o, onorm_g) * jax.nn.silu(gate)
    return o.reshape(B, S, HG_V).astype(z.dtype)

def causal_block_attention(q, k, v):
    B, S, H, Dq = q.shape
    nb = S // Q_BLOCK
    scale = Dq ** -0.5
    qb = q.reshape(B, nb, Q_BLOCK, H, Dq).transpose(1, 0, 2, 3, 4)
    kpos = jnp.arange(S)

    def one_block(args):
        qi, idx = args
        s = jnp.einsum('bqhd,bkhd->bhqk', qi, k).astype(jnp.float32) * scale
        qpos = idx * Q_BLOCK + jnp.arange(Q_BLOCK)
        s = jnp.where(kpos[None, :] <= qpos[:, None], s, -jnp.inf)
        p = jax.nn.softmax(s, axis=-1)
        return jnp.einsum('bhqk,bkhd->bqhd', p.astype(v.dtype), v)

    out = lax.map(one_block, (qb, jnp.arange(nb)))
    return out.transpose(1, 0, 2, 3, 4).reshape(B, S, H, v.shape[-1])

def mla_mixer(z, cos, sin, qa_g, kva_g, w_uq, w_ukv, qn_g, kn_g):
    B, S, _ = z.shape
    cq, ckv, kpe = jnp.split(z, [MLA_Q_LORA, MLA_Q_LORA + MLA_KV_LORA], axis=-1)
    q = (rms_norm(cq, qa_g) @ w_uq).reshape(B, S, MLA_HEADS, MLA_QK)
    kv = (rms_norm(ckv, kva_g) @ w_ukv).reshape(B, S, MLA_HEADS, MLA_NOPE + MLA_VDIM)
    k_nope, v = kv[..., :MLA_NOPE], kv[..., MLA_NOPE:]
    k_rope = jnp.broadcast_to(kpe[:, :, None, :], (B, S, MLA_HEADS, MLA_ROPE))
    k = jnp.concatenate([k_nope, k_rope], axis=-1)
    q = rms_norm(q, qn_g)
    k = rms_norm(k, kn_g)
    q = jnp.concatenate([q[..., :MLA_NOPE], apply_rope(q[..., MLA_NOPE:], cos, sin)], axis=-1)
    k = jnp.concatenate([k[..., :MLA_NOPE], apply_rope(k[..., MLA_NOPE:], cos, sin)], axis=-1)
    o = causal_block_attention(q, k, v)
    return o.reshape(B, S, MLA_HEADS * MLA_VDIM)

def memory_attention(qm, mem_n, w_mem_kv, qn_g, kn_g):
    B, S, _ = qm.shape
    M = mem_n.shape[1]
    kv = mem_n @ w_mem_kv
    q = rms_norm(qm.reshape(B, S, MEM_HEADS, MEM_HDIM), qn_g)
    k = rms_norm(kv[..., :MEM_W].reshape(B, M, MEM_HEADS, MEM_HDIM), kn_g)
    v = kv[..., MEM_W:].reshape(B, M, MEM_HEADS, MEM_HDIM)
    s = jnp.einsum('bshd,bmhd->bhsm', q, k).astype(jnp.float32) * (MEM_HDIM ** -0.5)
    p = jax.nn.softmax(s, axis=-1)
    o = jnp.einsum('bhsm,bmhd->bshd', p.astype(v.dtype), v)
    return o.reshape(B, S, MEM_W)

def conv_ffn(h, w_up, conv_w, conv_b, w_down):
    u = h @ w_up
    u = lax.conv_general_dilated(
        u, conv_w[:, None, :].astype(u.dtype), window_strides=(1,),
        padding=[(CONV_W - 1, 0)], dimension_numbers=('NWC', 'WIO', 'NWC'),
        feature_group_count=u.shape[-1]) + conv_b
    a, b = u[..., :D_FF], u[..., D_FF:]
    return (jax.nn.silu(a) * b) @ w_down

def first_inputs(seed: int = 0) -> dict:
    key = jax.random.key(seed)
    ks = jax.random.split(key, 32)
    nrm = lambda k, shape, scale: jax.random.normal(k, shape, jnp.float32) * scale
    gain = lambda k, shape: 1.0 + 0.02 * jax.random.normal(k, shape, jnp.float32)
    offs = jax.random.randint(ks[2], (BATCH, 1), 0, 1024, dtype=jnp.int32)
    positions = offs + jnp.arange(SEQ, dtype=jnp.int32)[None, :]
    return {
        "x": nrm(ks[0], (BATCH, SEQ, D_MODEL), 1.0),
        "mem": nrm(ks[1], (BATCH, MEM_LEN, D_MODEL), 1.0),
        "positions": positions,
        "mix_norm_g": gain(ks[3], (DEPTH, D_MODEL)),
        "ffn_norm_g": gain(ks[4], (DEPTH, D_MODEL)),
        "mem_norm_g": gain(ks[5], (DEPTH, D_MODEL)),
        "w_mem_kv": nrm(ks[6], (DEPTH, D_MODEL, 2 * MEM_W), D_MODEL ** -0.5),
        "mem_q_norm_g": gain(ks[7], (DEPTH, MEM_HDIM)),
        "mem_k_norm_g": gain(ks[8], (DEPTH, MEM_HDIM)),
        "w_out": nrm(ks[9], (DEPTH, OUT_W, D_MODEL), OUT_W ** -0.5),
        "w_up": nrm(ks[10], (DEPTH, D_MODEL, 2 * D_FF), D_MODEL ** -0.5),
        "conv_w": nrm(ks[11], (DEPTH, CONV_W, 2 * D_FF), CONV_W ** -0.5),
        "conv_b": nrm(ks[12], (DEPTH, 2 * D_FF), 0.02),
        "w_down": nrm(ks[13], (DEPTH, D_FF, D_MODEL), D_FF ** -0.5),
        "hg_w_in": nrm(ks[14], (N_A_LAYERS, D_MODEL, HG_IN_W), D_MODEL ** -0.5),
        "hg_lb_logits": nrm(ks[15], (DEPTH + 1, HG_F), 0.5),
        "hg_out_norm_g": gain(ks[16], (N_A_LAYERS, HG_VDIM)),
        "mla_w_in": nrm(ks[17], (N_B_LAYERS, D_MODEL, MLA_IN_W), D_MODEL ** -0.5),
        "mla_qa_norm_g": gain(ks[18], (N_B_LAYERS, MLA_Q_LORA)),
        "mla_kva_norm_g": gain(ks[19], (N_B_LAYERS, MLA_KV_LORA)),
        "mla_w_uq": nrm(ks[20], (N_B_LAYERS, MLA_Q_LORA, MLA_HEADS * MLA_QK), MLA_Q_LORA ** -0.5),
        "mla_w_ukv": nrm(ks[21], (N_B_LAYERS, MLA_KV_LORA, MLA_HEADS * (MLA_NOPE + MLA_VDIM)), MLA_KV_LORA ** -0.5),
        "mla_q_norm_g": gain(ks[22], (N_B_LAYERS, MLA_QK)),
        "mla_k_norm_g": gain(ks[23], (N_B_LAYERS, MLA_QK)),
    }

def first_block(x, mem, positions, mix_norm_g, ffn_norm_g, mem_norm_g, w_mem_kv,
              mem_q_norm_g, mem_k_norm_g, w_out, w_up, conv_w, conv_b, w_down,
              hg_w_in, hg_lb_logits, hg_out_norm_g, mla_w_in, mla_qa_norm_g,
              mla_kva_norm_g, mla_w_uq, mla_w_ukv, mla_q_norm_g, mla_k_norm_g):
    cos, sin = rope_tables(positions)
    lower_bounds = jnp.cumsum(jax.nn.softmax(hg_lb_logits.astype(jnp.float32), axis=0), axis=0)
    for layer in range(DEPTH):
        h = rms_norm(x, mix_norm_g[layer])
        j = layer // N_MIXERS
        if layer % N_MIXERS == 0:
            z = h @ hg_w_in[j]
            y = hgrn2_mixer(z[..., :-MEM_W], lower_bounds[layer], hg_out_norm_g[j])
        else:
            z = h @ mla_w_in[j]
            y = mla_mixer(z[..., :-MEM_W], cos, sin, mla_qa_norm_g[j], mla_kva_norm_g[j],
                          mla_w_uq[j], mla_w_ukv[j], mla_q_norm_g[j], mla_k_norm_g[j])
        m = memory_attention(z[..., -MEM_W:], rms_norm(mem, mem_norm_g[layer]), w_mem_kv[layer],
                             mem_q_norm_g[layer], mem_k_norm_g[layer])
        x = x + jnp.concatenate([y, m], axis=-1) @ w_out[layer]
        x = x + conv_ffn(rms_norm(x, ffn_norm_g[layer]), w_up[layer], conv_w[layer],
                         conv_b[layer], w_down[layer])
    return x


DEPTH_2 = 1

CTX_LEN = 256
GRID_W = 64
W_CONV = 512
W_FNO = 512
N_FGROUPS = 4
N_HEADS = 8
HEAD_DIM = 64
W_ATTN = N_HEADS * HEAD_DIM
WIN_H = 8
WIN_W = 16
Q_BLOCK_W = 16
K_BLOCK_W = 2 * WIN_W
N_BRANCH = 3
NEG_INF = -1e30
D_IN = 4 * W_CONV + 2 * W_FNO + 4 * W_ATTN + N_BRANCH * D_MODEL
KV_LO = 4 * W_CONV + 2 * W_FNO + W_ATTN
KV_HI = KV_LO + 2 * W_ATTN


def rmsnorm(x, g):
    xf = x.astype(jnp.float32)
    y = xf * lax.rsqrt(jnp.mean(xf * xf, axis=-1, keepdims=True) + EPS)
    return (y * g.astype(jnp.float32)).astype(x.dtype)

def split_proj(p):
    sizes = (W_CONV,) * 4 + (W_FNO,) * 2 + (W_ATTN,) * 4 + (D_MODEL,) * N_BRANCH
    points = np.cumsum(sizes)[:-1].tolist()
    return jnp.split(p, points, axis=-1)

def heads(t):
    return t.reshape(t.shape[0], t.shape[1], N_HEADS, HEAD_DIM)

def short_conv(u, w_conv, b_conv):
    up = jnp.pad(u, ((0, 0), (1, 1), (0, 0)))
    return up[:, :-2] * w_conv[0] + up[:, 1:-1] * w_conv[1] + up[:, 2:] * w_conv[2] + b_conv

def fourier_mix(u):
    b, l, w = u.shape
    ug = u.reshape(b, l, N_FGROUPS, w // N_FGROUPS).astype(jnp.float32)
    y = jnp.fft.fft2(ug, axes=(1, 3), norm='ortho').real
    return y.reshape(b, l, w).astype(u.dtype)

def context_attention(q, k, v):
    s = jnp.einsum('bqhd,bkhd->bhqk', q, k).astype(jnp.float32) * (HEAD_DIM ** -0.5)
    p = jax.nn.softmax(s, axis=-1).astype(v.dtype)
    o = jnp.einsum('bhqk,bkhd->bqhd', p, v)
    return o.reshape(o.shape[0], o.shape[1], W_ATTN)

def neighbourhood_attention(q, k, v, k_ctx, v_ctx, rpb):
    b, s, h, dh = q.shape
    rows = s // GRID_W
    kh = min(WIN_H, rows)
    n_cb = GRID_W // Q_BLOCK_W
    scale = HEAD_DIM ** -0.5
    q = q.reshape(b, rows, n_cb, Q_BLOCK_W, h, dh)
    k = k.reshape(b, rows, GRID_W, h, dh)
    v = v.reshape(b, rows, GRID_W, h, dh)
    qcol = np.arange(GRID_W).reshape(n_cb, Q_BLOCK_W)
    kcs = np.clip(np.arange(n_cb) * Q_BLOCK_W - WIN_W // 2, 0, GRID_W - K_BLOCK_W)
    kcol = kcs[:, None] + np.arange(K_BLOCK_W)[None, :]
    cs = np.clip(qcol - WIN_W // 2, 0, GRID_W - WIN_W)
    col_ok = (kcol[:, None, :] >= cs[..., None]) & (kcol[:, None, :] < cs[..., None] + WIN_W)
    dc_idx = np.clip(kcol[:, None, :] - qcol[..., None] + WIN_W - 1, 0, 2 * WIN_W - 2)
    rpb_col = rpb[:, :, dc_idx]
    mask = col_ok[:, :, None, :]

    def row_block(r):
        rs = jnp.clip(r - kh // 2, 0, rows - kh)
        qr = lax.dynamic_index_in_dim(q, r, axis=1, keepdims=False)
        kb = lax.dynamic_slice_in_dim(k, rs, kh, axis=1)[:, :, kcol]
        vb = lax.dynamic_slice_in_dim(v, rs, kh, axis=1)[:, :, kcol]
        dr_idx = rs + jnp.arange(kh) - r + (WIN_H - 1)
        bias = jnp.take(rpb_col, dr_idx, axis=1).transpose(0, 2, 3, 1, 4).astype(jnp.float32)
        s_loc = jnp.einsum('bnqhd,binchd->bhnqic', qr, kb).astype(jnp.float32) * scale + bias
        s_loc = jnp.where(mask, s_loc, NEG_INF)
        s_ctx = jnp.einsum('bnqhd,bkhd->bhnqk', qr, k_ctx).astype(jnp.float32) * scale
        n_loc = kh * K_BLOCK_W
        sc = jnp.concatenate([s_loc.reshape(b, h, n_cb, Q_BLOCK_W, n_loc), s_ctx], axis=-1)
        p = jax.nn.softmax(sc, axis=-1).astype(v.dtype)
        p_loc = p[..., :n_loc].reshape(b, h, n_cb, Q_BLOCK_W, kh, K_BLOCK_W)
        p_ctx = p[..., n_loc:]
        return (jnp.einsum('bhnqic,binchd->bnqhd', p_loc, vb)
                + jnp.einsum('bhnqk,bkhd->bnqhd', p_ctx, v_ctx))

    o = lax.map(row_block, jnp.arange(rows))
    return o.transpose(1, 0, 2, 3, 4, 5).reshape(b, s, W_ATTN)

def merge_branches(pieces, attn_o, w_conv, b_conv, w_br_a, w_br_f, w_br_c, w_out):
    a_x, a_b, a_c, a_z, f_u, f_z, _q, _k, _v, c_z, g_a, g_f, g_c = pieces
    silu, sig = jax.nn.silu, jax.nn.sigmoid
    y_a = (a_b * short_conv(a_c * a_x, w_conv, b_conv) * silu(a_z)) @ w_br_a
    y_f = (fourier_mix(f_u) * silu(f_z)) @ w_br_f
    y_c = (attn_o * silu(c_z)) @ w_br_c
    return (sig(g_a) * y_a + sig(g_f) * y_f + sig(g_c) * y_c) @ w_out

def hybrid_layer(x, ctx, c, c_ctx, norm_g, w_ada, b_ada, w_in, b_in, w_conv, b_conv,
                 rpb, w_br_a, w_br_f, w_br_c, w_out, update_ctx):
    mod_l = jax.nn.silu(c) @ w_ada + b_ada
    mod_c = jax.nn.silu(c_ctx) @ w_ada + b_ada
    sh_l, sc_l, gt_l = jnp.split(mod_l[:, None, :], 3, axis=-1)
    sh_c, sc_c, gt_c = jnp.split(mod_c, 3, axis=-1)
    h_lat = rmsnorm(x, norm_g) * (1.0 + sc_l) + sh_l
    h_ctx = rmsnorm(ctx, norm_g) * (1.0 + sc_c) + sh_c

    pl = split_proj(h_lat @ w_in + b_in)
    if update_ctx:
        pc = split_proj(h_ctx @ w_in + b_in)
        k_c, v_c = pc[7], pc[8]
    else:
        k_c, v_c = jnp.split(h_ctx @ w_in[:, KV_LO:KV_HI] + b_in[KV_LO:KV_HI], 2, axis=-1)
    k_c, v_c = heads(k_c), heads(v_c)

    o_lat = neighbourhood_attention(heads(pl[6]), heads(pl[7]), heads(pl[8]), k_c, v_c, rpb)
    x_new = x + gt_l * merge_branches(pl, o_lat, w_conv, b_conv, w_br_a, w_br_f, w_br_c, w_out)
    if update_ctx:
        o_ctx = context_attention(heads(pc[6]), k_c, v_c)
        ctx = ctx + gt_c * merge_branches(pc, o_ctx, w_conv, b_conv, w_br_a, w_br_f, w_br_c, w_out)
    return x_new, ctx

def second_inputs(seed: int = 0) -> dict:
    key = jax.random.key(seed)
    ks = jax.random.split(key, 17)
    f32 = jnp.float32
    nrm = lambda k, shape, s: jax.random.normal(k, shape, f32) * s
    return {
        'x': nrm(ks[0], (BATCH, SEQ, D_MODEL), 1.0),
        'c': nrm(ks[1], (BATCH, D_MODEL), 1.0),
        'ctx': nrm(ks[2], (BATCH, CTX_LEN, D_MODEL), 1.0),
        'c_ctx': nrm(ks[3], (D_MODEL,), 1.0),
        'norm_g': 1.0 + nrm(ks[4], (DEPTH_2, D_MODEL), 0.05),
        'w_ada': nrm(ks[5], (DEPTH_2, D_MODEL, 3 * D_MODEL), 0.5 * D_MODEL ** -0.5),
        'b_ada': nrm(ks[6], (DEPTH_2, 3 * D_MODEL), 0.01),
        'w_in': nrm(ks[7], (DEPTH_2, D_MODEL, D_IN), D_MODEL ** -0.5),
        'b_in': nrm(ks[8], (DEPTH_2, D_IN), 0.01),
        'w_conv': nrm(ks[9], (DEPTH_2, 3, W_CONV), 3 ** -0.5),
        'b_conv': nrm(ks[10], (DEPTH_2, W_CONV), 0.01),
        'rpb': nrm(ks[11], (DEPTH_2, N_HEADS, 2 * WIN_H - 1, 2 * WIN_W - 1), 0.1),
        'w_br_a': nrm(ks[12], (DEPTH_2, W_CONV, D_MODEL), W_CONV ** -0.5),
        'w_br_f': nrm(ks[13], (DEPTH_2, W_FNO, D_MODEL), W_FNO ** -0.5),
        'w_br_c': nrm(ks[14], (DEPTH_2, W_ATTN, D_MODEL), W_ATTN ** -0.5),
        'w_out': nrm(ks[15], (DEPTH_2, D_MODEL, D_MODEL), D_MODEL ** -0.5),
        'final_g': 1.0 + nrm(ks[16], (D_MODEL,), 0.05),
    }

def second_block(x, c, ctx, c_ctx, norm_g, w_ada, b_ada, w_in, b_in, w_conv, b_conv,
              rpb, w_br_a, w_br_f, w_br_c, w_out, final_g):
    for l in range(DEPTH_2):
        x, ctx = hybrid_layer(x, ctx, c, c_ctx, norm_g[l], w_ada[l], b_ada[l], w_in[l], b_in[l],
                              w_conv[l], b_conv[l], rpb[l], w_br_a[l], w_br_f[l], w_br_c[l],
                              w_out[l], update_ctx=(l < DEPTH_2 - 1))
    return rmsnorm(x, final_g)


def setup_inputs(seed=0):
    out = dict(first_inputs(seed))
    for name, value in second_inputs(seed + 1).items():
        if name != "x":
            out[name + "_2"] = value
    return out


def reference(
    x, mem, positions, mix_norm_g, ffn_norm_g, mem_norm_g, w_mem_kv, mem_q_norm_g, mem_k_norm_g,
    w_out, w_up, conv_w, conv_b, w_down, hg_w_in, hg_lb_logits, hg_out_norm_g, mla_w_in,
    mla_qa_norm_g, mla_kva_norm_g, mla_w_uq, mla_w_ukv, mla_q_norm_g, mla_k_norm_g, c_2, ctx_2,
    c_ctx_2, norm_g_2, w_ada_2, b_ada_2, w_in_2, b_in_2, w_conv_2, b_conv_2, rpb_2, w_br_a_2,
    w_br_f_2, w_br_c_2, w_out_2, final_g_2,
):
    x = first_block(
        x, mem, positions, mix_norm_g, ffn_norm_g, mem_norm_g, w_mem_kv, mem_q_norm_g,
        mem_k_norm_g, w_out, w_up, conv_w, conv_b, w_down, hg_w_in, hg_lb_logits, hg_out_norm_g,
        mla_w_in, mla_qa_norm_g, mla_kva_norm_g, mla_w_uq, mla_w_ukv, mla_q_norm_g,
        mla_k_norm_g,
    )
    return second_block(
        x, c_2, ctx_2, c_ctx_2, norm_g_2, w_ada_2, b_ada_2, w_in_2, b_in_2, w_conv_2, b_conv_2,
        rpb_2, w_br_a_2, w_br_f_2, w_br_c_2, w_out_2, final_g_2,
    )


_drawn_inputs = setup_inputs


def setup_inputs(seed=0):
    import zlib

    import numpy as np

    out = dict(_drawn_inputs(seed))
    spreads = {}
    factors = {'mix_norm_g': 3.416,
     'ffn_norm_g': 2.847,
     'mem_norm_g': 8.0,
     'mem_q_norm_g': 8.0,
     'mem_k_norm_g': 8.0,
     'conv_b': 2.941,
     'hg_lb_logits': 2.729,
     'hg_out_norm_g': 4.768,
     'mla_qa_norm_g': 8.0,
     'mla_kva_norm_g': 8.0,
     'mla_q_norm_g': 8.0,
     'mla_k_norm_g': 8.0,
     'ctx_2': 8.0,
     'c_ctx_2': 3.944,
     'norm_g_2': 5.454,
     'b_ada_2': 8.0,
     'b_in_2': 8.0,
     'b_conv_2': 64.0,
     'rpb_2': 200.0,
     'w_br_c_2': 2.769}
    for name, (base, spread) in spreads.items():
        noise = np.random.default_rng([zlib.crc32(name.encode()), seed]).standard_normal(out[name].shape)
        drawn = base * np.exp(spread * noise) if base else spread * noise
        out[name] = __import__('jax').numpy.asarray(drawn.astype(out[name].dtype))
    for name, factor in factors.items():
        out[name] = (out[name] * factor).astype(out[name].dtype)
    return out
```

```python
from contextlib import ExitStack

import numpy as np
import concourse.bass as bass
from concourse import mybir
from concourse.alu_op_type import AluOpType as ALU

F32, F32R, U32, I32 = mybir.dt.float32, mybir.dt.float32r, mybir.dt.uint32, mybir.dt.int32
ACT = mybir.ActivationFunctionType
AX = mybir.AxisListType.X

P, T, D, KC = 128, 512, 1024, 8
NMEM = 256
FF = 2816
FC = FF // P
HH = 6
SLOT = 2048
DSLOT = 11 * P
EPS = 1e-6
NEG = -1e30
KCS = [0, 8, 24, 32]

S_M = 0
S_Z0 = S_M + 4
S_O0 = S_Z0 + 13
S_U0 = S_O0 + 4
S_D0 = S_U0 + 22
S_Z1 = S_D0 + 16
S_UQ = S_Z1 + 4
S_UKV = S_UQ + 3
S_O1 = S_UKV + 3
S_U1 = S_O1 + 4
S_D1 = S_U1 + 22
S_QKV = S_D1 + 16
S_GC = S_QKV + 8
S_BC = S_GC + 4
S_A = S_BC + 2
S_GA = S_A + 8
S_BA = S_GA + 4
S_F = S_BA + 2
S_GF = S_F + 4
S_BF = S_GF + 4
S_O2 = S_BF + 2
NS = S_O2 + 4
NADA = 12

VEC = [("mix0", 8), ("mix1", 8), ("ffn0", 8), ("ffn1", 8), ("mem0", 8), ("mem1", 8),
       ("cw0", 132), ("cw1", 132), ("cb0", 44), ("cb1", 44), ("bin", 64), ("bada", 24), ("ng2", 8),
       ("fin", 8), ("wc2", 12), ("bc2", 4), ("cc", 16), ("lb", 18), ("hgo", 1), ("qa", 3), ("kva", 2),
       ("qnn", 1), ("qnr", 1), ("knn", 1), ("knr", 1), ("mq0", 1), ("mq1", 1), ("mk0", 1), ("mk1", 1)]
VOFF, _n = {}, 0
for _name, _c in VEC:
    VOFF[_name] = _n
    _n += _c
NV = _n

CON = [("ones", 128), ("ident", 128), ("b64", 128), ("rot", 128), ("causal", 128), ("winmask", 128),
       ("scan", 512), ("lvl", 448), ("inv", 1), ("e1", 1), ("e64", 1), ("e192", 1)]
COFF, _n = {}, 0
for _name, _c in CON:
    COFF[_name] = _n
    _n += _c
NC = _n

TWO_PI = 2 * np.pi
C1 = 6.28125
C2 = float(np.float32(TWO_PI - C1))
C3 = float(np.float32(TWO_PI - C1 - C2))
MAGIC = 12582912.0


class Chain:

    def __init__(self, eng, sem):
        self.eng, self.sem, self.n = eng, sem, 0

    def __call__(self, ins):
        self.n += 1
        ins.then_inc(self.sem, 1)
        self.eng.wait_ge(self.sem, self.n)


def build(nc, dr, out):
    KB = 1024
    base = 16512
    RAW, WHI, WLO, HR, XT, CONST, SCR, WORK = (base + KB * k for k in (0, 16, 32, 48, 80, 96, 106, 118))

    def at(name, off, shape, dt=F32):
        return nc.alloc_sbuf_tensor_at(name, shape, dt, offset=off)

    wraw = at("wraw", RAW, [P, 2, SLOT])
    whi = at("whi", WHI, [P, 2, SLOT], F32R)
    wlo = at("wlo", WLO, [P, 2, SLOT], F32R)
    ada = at("ada", WHI, [P, 4, SLOT])
    hh = at("hh", HR, [P, KC, T], F32R)
    hl = at("hl", HR + 16 * KB, [P, KC, T], F32R)
    xT = at("xT", XT, [P, KC, T])
    con = at("con", CONST, [P, NC])
    vec = at("vec", CONST + 4 * ((NC + 7) // 8 * 8), [P, NV])
    so = CONST + 4 * ((NC + 7) // 8 * 8) + 4 * ((NV + 7) // 8 * 8)
    small = at("small", so, [P, 176])
    assert so + 176 * 4 <= SCR, so + 176 * 4 - SCR
    scr = at("scr", SCR, [P, 4, T])
    km1 = at("km1", SCR + 8 * KB, [P, 2, NMEM])
    vm1 = at("vm1", SCR + 10 * KB, [P, 2, NMEM])
    sqacc, rstd = scr[:, 0, :], scr[:, 1, :]
    tb = [scr[:, 2, :], scr[:, 3, :]]

    def w(name, kb, shape, dt=F32):
        return at(name, WORK + int(kb * KB), shape, dt)

    xtok = w("xtok", 0, [P, 4, D])
    mtok = w("mtok", 16, [P, 2, D])
    memT = w("memT", 24, [P, KC, NMEM])
    mh = [w(f"mh{l}", 32 + 16 * l, [P, KC, NMEM], F32R) for l in range(2)]
    ml = [w(f"ml{l}", 40 + 16 * l, [P, KC, NMEM], F32R) for l in range(2)]
    msq = w("msq", 64, [P, 3, NMEM])
    sqx = w("sqx", 76, [P, T])
    hq, hk, hb, hgate = (w(n, k, [P, HH, T]) for n, k in (("hq", 0), ("hk", 12), ("hb", 24), ("hgate", 36)))
    hv = w("hv", 48, [P, 4, HH * P])
    hA = w("hA", 60, [P, HH, T])
    qm0 = w("qm0", 72, [P, 2, T])
    km0 = w("km0", 84, [P, 2, NMEM])
    vm0 = w("vm0", 86, [P, 2, NMEM])
    hE = at("hE", HR, [P, HH, T])
    hKL = at("hKL", HR + 12 * KB, [P, HH, T])
    hQL = at("hQL", HR + 24 * KB, [P, HH, T // 2])
    hkT = w("hkT", 12, [P, HH, 3, P])
    hS = w("hS", 24, [P, 3, HH, P])
    gh = w("gh", 0, [P, FC, T], F32R)
    gl = w("gl", 44, [P, FC, T], F32R)
    pr0, pt0 = w("pr0", 0, [P, 3, T]), [w("pt00", 12, [P, 4, T]), w("pt01", 24, [P, 4, T])]
    z1 = w("z1", 0, [P, 8, T])
    mqn, mqr, mkn, mkr = (w("mqn", 16, [P, HH, T]), w("mqr", 28, [P, 3, T]), w("mkn", 34, [P, HH, T]),
                          w("mkr", 46, [P, 3, T]))
    mv = w("mv", 52, [P, 4, HH * P])
    cosT, sinT = w("cosT", 64, [P, T]), w("sinT", 66, [P, T])
    pr1, pt1 = w("pr1", 68, [P, 3, T]), [w("pt10", 0, [P, 4, T]), w("pt11", 74, [P, 4, T])]
    kr0 = w("kr0", 82, [P, T])
    rtmp = w("rtmp", 84, [P, 2, T])
    posi = w("posi", 68, [P, T], I32)
    posf = w("posf", 70, [P, 2, T])
    sqr = w("sqr", 0, [P, 2, T])
    wq, wk, wcz, wvr = (w(n, k, [P, 4, T]) for n, k in (("wq", 0), ("wk", 8), ("wcz", 16), ("wvr", 24)))
    vtok = w("vtok", 32, [P, 8, T])
    wkc, wvc, vct = w("wkc", 48, [P, 4, NMEM]), w("wvc", 52, [P, 4, NMEM]), w("vct", 56, [P, 2, T])
    wbias = w("wbias", 60, [P, 8, 8, 48])
    wbm = w("wbm", 72, [P, 4, NMEM])
    pr2 = w("pr2", 76, [P, 3, T])
    ptw = w("ptw", 24, [P, 4, 4, P])
    vtmp = w("vtmp", 76, [P, 2, D])
    ctok = w("ctok", 76, [P, 2, D])
    ctxT = w("ctxT", 16, [P, KC, NMEM])
    ch, cl = w("ch", 32, [P, KC, NMEM], F32R), w("cl", 40, [P, KC, NMEM], F32R)
    csq = w("csq", 84, [P, 3, NMEM])
    bh, bl = w("bh", 0, [P, 4, T], F32R), w("bl", 8, [P, 4, T], F32R)
    mm_ = w("mm_", 32, [P, KC, T])
    sig = w("sig", 48, [P, KC, T])
    atmp = w("atmp", 16, [P, 2, T])
    az = w("az", 20, [P, 2, T])
    acc2 = w("acc2", 24, [P, 2, T])
    btmp = w("btmp", 28, [P, 2, T])
    fu, fz = w("fu", 16, [P, 4, T]), w("fz", 24, [P, 4, T])
    xc = w("xc", 64, [P, 4, 4, 256])
    dft = w("dft", 48, [P, 8, T])
    dcc = w("dcc", 80, [P, 256])
    yT = w("yT", 0, [P, KC, T])
    ytok = w("ytok", 16, [P, 4, D])

    ps = nc.alloc_psum_tensor("ps", [P, 8, T], F32)

    def cc(name, a=0, n=None):
        return con[:, COFF[name] + a:COFF[name] + a + (n or dict(CON)[name])]

    def vv(name, j=0, n=1):
        return vec[:, VOFF[name] + j:VOFF[name] + j + n]

    nmx, sm, rc = small[:, 0:4], small[:, 4:8], small[:, 8:12]
    lbt, oml = small[:, 12:18], small[:, 18:24]
    lbx = small[:, 24:48]
    cs = small[:, 48:64]
    mod = small[:, 64:112]
    gsc = small[:, 112:128]

    with ExitStack() as ctx:
        def sem(name):
            return ctx.enter_context(nc.semaphore(name))

        raw_ready = [sem("raw_ready0"), sem("raw_ready1")]
        hi_ready, lo_ready = sem("hi_ready"), sem("lo_ready")
        used = sem("used")
        emptied = sem("emptied")
        x_in, c_in, m_in = sem("x_in"), sem("c_in"), sem("m_in")
        tr, ev = sem("tr"), sem("ev")
        sq_ready, sq_added, sum_ready, rstd_ready = sem("sq_ready"), sem("sq_added"), sem("sum_ready"), sem("rstd_ready")
        msq_ready, msq_added = sem("msq_ready"), sem("msq_added")
        t_ready, thi_ready, split_done = sem("t_ready"), sem("thi_ready"), sem("split_done")
        yn_ready, hn_sq, hn_mm, hn_rstd, hn_done = (sem(n) for n in ("yn_ready", "hn_sq", "hn_mm", "hn_rstd", "hn_done"))
        ch_act, ch_dve = sem("ch_act"), sem("ch_dve")
        f_acc, f_tap, f_conv, f_silu, f_g, f_hi, f_lo = (sem(n) for n in ("f_acc", "f_tap", "f_conv", "f_silu", "f_g", "f_hi", "f_lo"))
        g_act, g_dve = sem("g_act"), sem("g_dve")
        lv_d, lv_e, lv_k, lv_q, lv_mm, lv_cp = (sem(n) for n in ("lv_d", "lv_e", "lv_k", "lv_q", "lv_mm", "lv_cp"))
        st_k, st_tr, st_tc, st_kv, st_s = (sem(n) for n in ("st_k", "st_tr", "st_tc", "st_kv", "st_s"))
        ho_mm, ho_cp = sem("ho_mm"), sem("ho_cp")
        ada_in = [sem(f"ada_in{i}") for i in range(4)]
        ada_used, ada_cs, mod_ready = sem("ada_used"), sem("ada_cs"), sem("mod_ready")
        sc_ready, mx_ready, ex_ready, pn_ready, tp_ready, pt_ready, pv_done, o_read = (
            sem(n) for n in ("sc_ready", "mx_ready", "ex_ready", "pn_ready", "tp_ready", "pt_ready", "pv_done", "o_read"))
        bm_ready = sem("bm_ready")
        pos_in, rp_d, rp_a, rot_mm, rot_rd, kq_ready = (sem(n) for n in ("pos_in", "rp_d", "rp_a", "rot_mm", "rot_rd", "kq_ready"))
        q_act, q_dve = sem("q_act"), sem("q_dve")
        ctx_in, b_in, dft_in = sem("ctx_in"), sem("b_in"), sem("dft_in")
        vt_c, vt_tr, vt_ev = sem("vt_c"), sem("vt_tr"), sem("vt_ev")
        df_mm, df_ev = sem("df_mm"), sem("df_ev")
        d1_done = sem("d1_done")
        y_tr, y_ev, out_done = sem("y_tr"), sem("y_ev"), sem("out_done")
        block = ctx.enter_context(nc.Block())


        Q_MEM = 0
        Q_H0 = Q_MEM + 16
        Q_Y0 = Q_H0 + 8
        Q_F0 = Q_Y0 + 8
        Q_H1 = Q_F0 + 8
        Q_C1 = Q_H1 + 8
        Q_Y1 = Q_C1 + 5
        Q_F1 = Q_Y1 + 8
        Q_H2 = Q_F1 + 8
        Q_CTX = Q_H2 + 8
        Q_BC = Q_CTX + 8
        Q_BA = Q_BC + 4
        Q_BF = Q_BA + 4
        Q_M2 = Q_BF + 4
        A_M0, A_MLA, A_M1, A_W = 0, 16, 40, 56
        G_M0, G_MLA, G_M1, G_W = 0, 2, 8, 10
        H_KM, H_HG, H_QM0, H_C1, H_Q1, H_K1, H_QM1 = 0, 2, 8, 10, 12, 18, 24
        HN_IN = [1, 1] + [1] * 6 + [1, 1] + [3, 2] + [2] * 6 + [2] * 6 + [1, 1]
        HN_AT = [sum(HN_IN[:i]) for i in range(len(HN_IN) + 1)]

        def sqbuf(i):
            return sqacc if i % 2 == 0 else sqx[:]

        def units(kind, layer=0):
            if kind == "mem":
                return [(2, h // 2, h % 2 == 1 and tt == 3) for h in range(4) for tt in range(4)]
            if kind == "mla":
                return [(i + 1, h, i == 3) for h in range(HH) for i in range(4)]
            return [(4, cb * 4 + h // 2, h % 2 == 1) for cb in range(4) for h in range(8)]

        @block.sync
        def _(sp):
            sp.dma_start(xtok[:], dr["x"].rearrange("a (t p) d -> p (a t) d", p=P)).then_inc(x_in, 16)

            def load(s, src):
                if s >= 2:
                    sp.wait_ge(lo_ready, s - 1)
                wd = src.shape[1]
                sp.dma_start(wraw[:, s % 2, 0:wd], src).then_inc(raw_ready[s % 2], 16)

            def load_many(s0, n, dram):
                wd = dram.shape[2]
                i0 = 0
                while s0 + i0 < 2 or (n - i0) % 2:
                    load(s0 + i0, dram[i0])
                    i0 += 1
                with sp.Fori(0, (n - i0) // 2) as i:
                    for u in range(2):
                        s = s0 + i0 + u
                        src = dram[bass.ds(2 * i + (i0 + u), 1), :, :].rearrange("a p n -> (a p) n")
                        sp.wait_ge(lo_ready, 2 * i + (s - 1))
                        sp.dma_start(wraw[:, s % 2, 0:wd], src).then_inc(raw_ready[s % 2], 16)

            load_many(0, S_O0, dr["w0"])
            sp.wait_ge(used, S_O0)
            for a in range(NADA):
                if a >= 4:
                    sp.wait_ge(ada_used, a - 3)
                sp.dma_start(ada[:, a % 4, :], dr["wada"][a]).then_inc(ada_in[a % 4], 16)
            for s0, dram in ((S_O0, "w0b"), (S_D0, "wd0"), (S_Z1, "w1"), (S_D1, "wd1"), (S_QKV, "w2")):
                load_many(s0, dr[dram].shape[0], dr[dram])
            for tt in range(4):
                sp.wait_ge(y_ev, 2 * tt + 2)
                sp.dma_start(out[0, tt * P:(tt + 1) * P, :], ytok[:, tt, :]).then_inc(out_done, 16)
            sp.wait_ge(out_done, 64)

        @block.tensor
        def _(pe):
            mm = nc.tensor.matmul

            def three(o, wsl, asl, K, moving_w=False):
                for k in range(K):
                    for n, (a, b) in enumerate(((0, 0), (0, 1), (1, 0))):
                        l, r = (wsl(a, k), asl(b, k)) if not moving_w else (asl(b, k), wsl(a, k))
                        last = mm(o, l, r, start=(k == 0 and n == 0), stop=(k == K - 1 and n == 2))
                return last

            def wv(par, cols, width=256, off=0, n=P):
                return lambda a, k: (whi, wlo)[a][:, par, k * cols + off:k * cols + off + n]

            def hv_(k0=0):
                return lambda a, k: (hh, hl)[a][:, k0 + k, :]

            def slot_loop(S, n, body, lead=1):
                pe.wait_ge(emptied, S)
                i0 = n % 2
                if i0:
                    pe.wait_ge(lo_ready, S + 1)
                    body(S % 2).then_inc(used, 1)
                m = (n - i0) // 2
                if m == 0:
                    return
                if m == 1:
                    for u in range(2):
                        s = S + i0 + u
                        pe.wait_ge(emptied, max(s - lead, S))
                        pe.wait_ge(lo_ready, s + 1)
                        body(s % 2).then_inc(used, 1)
                    return
                with pe.Fori(0, m) as i:
                    for u in range(2):
                        s = S + i0 + u
                        pe.wait_ge(emptied, 2 * i + (s - lead))
                        pe.wait_ge(lo_ready, 2 * i + (s + 1))
                        body(s % 2).then_inc(used, 1)

            def plain(par, act=None, K=8):
                a = act or hv_()
                for b in range(2):
                    last = three(ps[:, 2 * par + b, :], wv(par, 256, off=b * P), a, K)
                return last

            pe.wait_ge(c_in, 32)
            pe.wait_ge(m_in, 16)
            for n in range(4):
                if n >= 2:
                    pe.wait_ge(ev, n - 1)
                for j in range(4):
                    k, mt = 2 * n + j // 2, j % 2
                    last = nc.tensor.transpose(ps[:, 4 + n % 2, j * P:(j + 1) * P], mtok[:, mt, k * P:(k + 1) * P], cc("ident"))
                last.then_inc(tr, 1)
            pe.wait_ge(x_in, 16)
            for n in range(8):
                if n == 2:
                    pe.wait_ge(msq_added, 8)
                    mm(ps[:, 6, 0:NMEM], cc("ones"), msq[:, 2, :], start=True, stop=True).then_inc(sum_ready, 1)
                pe.wait_ge(ev, n + 3)
                for tt in range(4):
                    last = nc.tensor.transpose(ps[:, 4 + n % 2, tt * P:(tt + 1) * P], xtok[:, tt, n * P:(n + 1) * P], cc("ident"))
                last.then_inc(tr, 1)
            def norm_sum(n):
                pe.wait_ge(sq_added, 8 * n + 8)
                mm(ps[:, 7, :], cc("ones"), sqacc, start=True, stop=True).then_inc(sum_ready, 1)

            norm_sum(0)

            def mem_proj(l):
                def act(a, k):
                    return (mh, ml)[a][l][:, k, :]
                s = S_M + 2 * l
                pe.wait_ge(split_done, Q_MEM + 8 * l + 8)
                pe.wait_ge(lo_ready, s + 1)
                for b in range(2):
                    last = three(ps[:, 2 * (s % 2), b * NMEM:(b + 1) * NMEM], wv(s % 2, 256, off=b * P), act, 8)
                last.then_inc(used, 1)
                s += 1
                pe.wait_ge(lo_ready, s + 1)
                for mt in range(2):
                    last = three(ps[:, 2 * (s % 2), mt * NMEM:(mt + 1) * NMEM], wv(s % 2, 256, n=256),
                                 lambda a, k: act(a, k)[:, mt * P:(mt + 1) * P], 8, moving_w=True)
                last.then_inc(used, 1)

            mem_proj(0)
            pe.wait_ge(emptied, 2)
            mem_proj(1)

            def hn_sums(r, mats):
                if r >= 2:
                    pe.wait_ge(hn_rstd, r - 1)
                for j, m in enumerate(mats):
                    i = HN_AT[r] + j
                    pe.wait_ge(hn_sq, i + 1)
                    lhs, rhs = m(i)
                    mm(ps[:, 4 + r % 2, :], lhs, rhs, start=(j == 0), stop=(j == len(mats) - 1)).then_inc(hn_mm, 1)

            def whole(name):
                return lambda i: (cc(name), sqbuf(i))

            for l in range(2):
                hn_sums(H_KM + l, [whole("b64")])

            pe.wait_ge(split_done, Q_H0 + 8)
            slot_loop(S_Z0, 6, plain)
            def tok_major(par):
                for tt in range(4):
                    last = three(ps[:, 2 * par + tt // 2, (tt % 2) * 256:(tt % 2) * 256 + 256], wv(par, 256, n=256),
                                 lambda a, k: (hh, hl)[a][:, k, tt * P:(tt + 1) * P], 8, moving_w=True)
                return last
            slot_loop(S_Z0 + 6, 3, tok_major)
            slot_loop(S_Z0 + 9, 4, plain)

            def ada_slot(a):
                if a == 0:
                    pe.wait_ge(ada_cs, 1)
                pe.wait_ge(ada_in[a % 4], 16 * (a // 4 + 1))
                for b in range(2):
                    n = 2 * a + b
                    for k in range(8):
                        last = mm(ps[:, 7, 2 * n:2 * n + 2], ada[:, a % 4, k * 256 + b * P:k * 256 + (b + 1) * P],
                                  cs[:, 2 * k:2 * k + 2], start=(k == 0), stop=(k == 7))
                last.then_inc(ada_used, 1)

            for hf in range(2):
                pe.wait_ge(g_dve, 3)
                if hf == 0:
                    pe.wait_ge(emptied, S_O0)
                for h in range(3 * hf, 3 * hf + 3):
                    for c in range(4):
                        last = mm(ps[:, h, c * P:(c + 1) * P], hk[:, h, c * P:(c + 1) * P], hq[:, h, c * P:(c + 1) * P],
                                  start=True, stop=True)
                last.then_inc(lv_mm, 1)
            for j in range(14):
                hf, l = j % 2, j // 2
                pe.wait_ge(lv_k, j + 1)
                pe.wait_ge(lv_q, j + 1)
                pe.wait_ge(lv_cp, j + 1)
                for h3 in range(3):
                    h = 3 * hf + h3
                    for c in range(4):
                        o = h3 * 256 + c * 64
                        last = mm(ps[:, 3 * hf + o // 512, o % 512:o % 512 + 64], hKL[:, h, c * P:(c + 1) * P],
                                  hQL[:, h, c * 64:(c + 1) * 64], start=True, stop=True)
                last.then_inc(lv_mm, 1)
                if 1 <= j <= NADA:
                    ada_slot(j - 1)
            pe.wait_ge(st_k, 1)
            pe.wait_ge(lv_cp, 16)
            for n in range(HH):
                if n >= 2:
                    pe.wait_ge(st_tc, n - 1)
                for c in range(3):
                    last = nc.tensor.transpose(ps[:, n % 2, c * P:(c + 1) * P], hKL[:, n, c * P:(c + 1) * P], cc("ident"))
                last.then_inc(st_tr, 1)
            for n in range(HH):
                pe.wait_ge(st_tc, n + 1)
                if n >= 2:
                    pe.wait_ge(st_s, n - 1)
                for c in range(3):
                    last = mm(ps[:, 2 + n % 2, c * P:(c + 1) * P], hkT[:, n, c, :], hv[:, c, n * P:(n + 1) * P],
                              start=True, stop=True)
                last.then_inc(st_kv, 1)
            for h in range(HH):
                pe.wait_ge(st_s, HH)
                if h >= 2:
                    pe.wait_ge(ho_cp, h - 1)
                for c in range(4):
                    t = slice(c * P, (c + 1) * P)
                    last = mm(ps[:, h % 2, t], hv[:, c, h * P:(h + 1) * P], hA[:, h, t], start=True, stop=(c == 0))
                    if c:
                        last = mm(ps[:, h % 2, t], hS[:, c - 1, h, :], hq[:, h, t], start=False, stop=True)
                last.then_inc(ho_mm, 1)
                if h >= 1:
                    hn_sums(H_HG + h - 1, [whole("ones")])
            hn_sums(H_HG + 5, [whole("ones")])
            for j in range(2):
                hn_sums(H_QM0 + j, [whole("b64")])

            def attention(kind, U0, G0, scores, pv, ready=None):
                us = units(kind)
                for n in range(len(us) + 3):
                    if n < len(us):
                        u = U0 + n
                        if n < 3:
                            if n == 0 and ready:
                                ready()
                        if u >= 3:
                            pe.wait_ge(ex_ready, u - 2)
                        scores(n, 4 + u % 3).then_inc(sc_ready, 1)
                    if 2 <= n < len(us) + 2:
                        u = U0 + n - 2
                        pe.wait_ge(pn_ready, u + 1)
                        if u >= 2:
                            pe.wait_ge(pt_ready, u - 1)
                        b = (7, 3)[u % 2]
                        for j in range(us[n - 2][0]):
                            last = nc.tensor.transpose(ps[:, b, j * P:(j + 1) * P], prs[kind][:, u % 3, j * P:(j + 1) * P], cc("ident"))
                        last.then_inc(tp_ready, 1)
                    if n >= 3 and us[n - 3][2]:
                        g = G0 + us[n - 3][1]
                        pe.wait_ge(pt_ready, U0 + n - 2)
                        if g >= 2:
                            pe.wait_ge(*OREAD[g - 2])
                        pv(us[n - 3][1], g % 2).then_inc(pv_done, 1)

            OREAD = [(t_ready, q + 1) for q in (*range(Q_Y0 + 6, Q_Y0 + 8), *range(Q_Y1, Q_Y1 + 8))] + [(o_read, n + 1) for n in range(16)]
            prs = {"mem": pr0, "mla": pr1, "win": pr2}

            def mem_attention(l, q, kmm, vmm):
                def scores(n, b):
                    h, tt = n // 4, n % 4
                    r = slice(64 * (h % 2), 64 * (h % 2) + 64)
                    return mm(ps[:, b, 0:NMEM], q[r, h // 2, tt * P:(tt + 1) * P], kmm[r, h // 2, :], start=True, stop=True)

                def pv(g, b):
                    for h in (2 * g, 2 * g + 1):
                        for c in range(2):
                            last = mm(ps[64 * (h % 2):64 * (h % 2) + 64, b, :], vmm[:, c, h * 64:(h + 1) * 64],
                                      pts[l][h % 2][:, c, :], start=(c == 0), stop=(c == 1))
                    return last
                prs["mem"] = (pr0, pr1)[l]
                r = (H_QM0, H_QM1)[l]
                attention("mem", (A_M0, A_M1)[l], (G_M0, G_M1)[l], scores, pv, lambda: pe.wait_ge(hn_done, r + 2))

            pts = [pt0, pt1]
            pe.wait_ge(mod_ready, 1)
            mem_attention(0, qm0, km0, vm0)
            pe.wait_ge(split_done, Q_Y0 + 8)
            slot_loop(S_O0, 4, plain)
            norm_sum(1)

            def ffn(S_U, S_D, q, layer):
                pe.wait_ge(split_done, q + 8)
                slot_loop(S_U, 22, plain)
                pe.wait_ge(f_lo, 22 * layer + 22)
                pe.wait_ge(emptied, S_D)
                with pe.Fori(0, 4) as i:
                    for n in range(2):
                        s = S_D + 2 * n
                        pe.wait_ge(emptied, 4 * i + (s - 2))
                        for hf in range(2):
                            pe.wait_ge(lo_ready, 4 * i + (s + hf + 1))
                            par = (s + hf) % 2
                            for k in range(11):
                                for m, (a, b) in enumerate(((0, 0), (0, 1), (1, 0))):
                                    last = mm(ps[:, n, :], (whi, wlo)[a][:, par, k * P:(k + 1) * P],
                                              (gh, gl)[b][:, 11 * hf + k, :],
                                              start=(hf == 0 and k == 0 and m == 0), stop=(hf == 1 and k == 10 and m == 2))
                            last.then_inc(used, 1)

            ffn(S_U0, S_D0, Q_F0, 0)
            norm_sum(2)

            pe.wait_ge(split_done, Q_H1 + 8)
            slot_loop(S_Z1, 4, plain)
            hn_sums(H_C1, [whole("ones")] * 3)
            hn_sums(H_C1 + 1, [whole("ones")] * 2)
            pe.wait_ge(split_done, Q_C1 + 3)

            def uq(par):
                for b in range(3):
                    last = three(ps[:, b, :], wv(par, 384, off=b * P), hv_(), 3)
                return last
            slot_loop(S_UQ, 3, uq, lead=0)
            pe.wait_ge(split_done, Q_C1 + 5)

            def ukv(par):
                for b in range(2):
                    three(ps[:, b, :], wv(par, 512, off=b * P), hv_(3), 2)
                for tt in range(4):
                    last = three(ps[:, 2 + tt // 2, (tt % 2) * 256:(tt % 2) * 256 + 256], wv(par, 512, off=256, n=256),
                                 lambda a, k: (hh, hl)[a][:, 3 + k, tt * P:(tt + 1) * P], 2, moving_w=True)
                return last
            slot_loop(S_UKV, 3, ukv, lead=0)
            def half(h, rhs):
                r = slice(64 * (h % 2), 64 * (h % 2) + 64)
                return lambda i: (con[r, COFF["ones"]:COFF["ones"] + P], rhs[r, :])
            for h in range(HH):
                hn_sums(H_Q1 + h, [whole("ones"), half(h, sqr[:, 0, :])])
                if h % 2 == 1:
                    pe.wait_ge(hn_done, H_Q1 + h + 1)
                    if h > 1:
                        pe.wait_ge(rot_rd, h // 2)
                    mm(ps[:, 6, :], cc("rot"), mqr[:, h // 2, :], start=True, stop=True).then_inc(rot_mm, 1)
            pe.wait_ge(kq_ready, 1)
            pe.wait_ge(rot_rd, 3)
            mm(ps[:, 6, :], cc("rot"), z1[:, 5, :], start=True, stop=True).then_inc(rot_mm, 1)
            for h in range(HH):
                hn_sums(H_K1 + h, [whole("ones"), half(0, sqr[:, 1, :])])
            for j in range(2):
                hn_sums(H_QM1 + j, [whole("b64")])

            def mla_scores(n, b):
                h, i = n // 4, n % 4
                r = slice(64 * (h % 2), 64 * (h % 2) + 64)
                wd = (i + 1) * P
                t = slice(i * P, (i + 1) * P)
                mm(ps[:, b, 0:wd], mqn[:, h, t], mkn[:, h, 0:wd], start=True, stop=False)
                mm(ps[:, b, wd - P:wd], cc("ident"), cc("causal"), start=False, stop=False)
                return mm(ps[:, b, 0:wd], mqr[r, h // 2, t], mkr[r, h // 2, 0:wd], start=False, stop=True)

            def mla_pv(h, b):
                for i in range(4):
                    t = slice(i * P, (i + 1) * P)
                    for j in range(i + 1):
                        last = mm(ps[:, b, t], mv[:, j, h * P:(h + 1) * P], pt1[h % 2][:, j, t], start=(j == 0), stop=(j == i))
                return last

            attention("mla", A_MLA, G_MLA, mla_scores, mla_pv, lambda: pe.wait_ge(hn_done, H_QM1 + 2))
            mem_attention(1, z1[:, 6:8, :], km1, vm1)
            pe.wait_ge(split_done, Q_Y1 + 8)
            slot_loop(S_O1, 4, plain)
            norm_sum(3)
            ffn(S_U1, S_D1, Q_F1, 1)
            norm_sum(4)

            pe.wait_ge(ctx_in, 16)
            for n in range(4):
                if n >= 2:
                    pe.wait_ge(ev, 12 + n - 1)
                for j in range(4):
                    k, mt = 2 * n + j // 2, j % 2
                    last = nc.tensor.transpose(ps[:, 4 + n % 2, j * P:(j + 1) * P], ctok[:, mt, k * P:(k + 1) * P], cc("ident"))
                last.then_inc(tr, 1)
            pe.wait_ge(split_done, Q_H2 + 8)
            slot_loop(S_QKV, 2, plain)
            pe.wait_ge(msq_added, 16)
            mm(ps[:, 6, 0:NMEM], cc("ones"), csq[:, 2, :], start=True, stop=True).then_inc(sum_ready, 1)
            pe.wait_ge(split_done, Q_CTX + 8)

            def kv(par):
                for b in range(2):
                    three(ps[:, 4 + par, b * NMEM:(b + 1) * NMEM], wv(par, 256, off=b * P),
                          lambda a, k: (ch, cl)[a][:, k, :], 8)
                return plain(par)
            slot_loop(S_QKV + 2, 4, kv)
            pe.wait_ge(emptied, S_QKV + 6)
            for j in range(4):
                pe.wait_ge(vt_c, j + 1)
                for q in range(2):
                    n = 3 * j + q
                    if n >= 3:
                        pe.wait_ge(vt_ev, n - 2)
                    for i in range(4):
                        last = nc.tensor.transpose(ps[:, 4 + q, i * P:(i + 1) * P], vtmp[:, j % 2, (4 * q + i) * P:(4 * q + i + 1) * P], cc("ident"))
                    last.then_inc(vt_tr, 1)
                if j >= 1:
                    pe.wait_ge(vt_ev, 3 * j)
                for i in range(2):
                    last = nc.tensor.transpose(ps[:, 6, i * P:(i + 1) * P], wvc[:, j, i * P:(i + 1) * P], cc("ident"))
                last.then_inc(vt_tr, 1)
            slot_loop(S_QKV + 6, 2, plain)

            def win_scores(n, b):
                cb, h = n // 8, n % 8
                r = slice(64 * (h % 2), 64 * (h % 2) + 64)
                q = wq[r, h // 2, cb * P:(cb + 1) * P]
                ks = wk[r, h // 2, :].rearrange("p (r c) -> p r c", c=64)[:, :, KCS[cb]:KCS[cb] + 32]
                mm(ps[:, b, 0:256].rearrange("p (r c) -> p r c", c=32), q, ks, start=True, stop=True)
                return mm(ps[:, b, 256:512], q, wkc[r, h // 2, :], start=True, stop=True)

            def win_pv(g, b):
                cb, hp = g // 4, g % 4
                for h in (2 * hp, 2 * hp + 1):
                    u = A_W + cb * 8 + h
                    for c in range(4):
                        v = vtok[:, 2 * cb + c, h * 64:(h + 1) * 64] if c < 2 else vct[:, c - 2, h * 64:(h + 1) * 64]
                        last = mm(ps[64 * (h % 2):64 * (h % 2) + 64, b, 0:P], v, ptw[:, u % 4, c, :],
                                  start=(c == 0), stop=(c == 3))
                return last

            def win_ready():
                pe.wait_ge(vt_ev, 12)
                pe.wait_ge(emptied, S_GC)

            attention("win", A_W, G_W, win_scores, win_pv, win_ready)
            pe.wait_ge(o_read, 16)
            slot_loop(S_GC, 4, plain)

            def branch(S, q):
                pe.wait_ge(split_done, q + 4)
                for s in (S, S + 1):
                    pe.wait_ge(emptied, max(S, s - 1))
                    pe.wait_ge(lo_ready, s + 1)
                    for b in range(4):
                        last = three(ps[:, 4 * (s % 2) + b, :], wv(s % 2, 512, off=b * P),
                                     lambda a, k: (bh, bl)[a][:, k, :], 4)
                    last.then_inc(used, 1)
            branch(S_BC, Q_BC)
            slot_loop(S_A, 8, plain)
            slot_loop(S_GA, 4, plain)
            branch(S_BA, Q_BA)
            slot_loop(S_F, 4, plain)
            pe.wait_ge(emptied, S_GF)
            pe.wait_ge(dft_in, 32)
            for n in range(8):
                g, q = n // 2, n % 2
                if n >= 2:
                    pe.wait_ge(df_ev, n - 1)
                for i in range(2):
                    tt = 2 * q + i
                    last = mm(ps[:, 4 + n % 2, i * 256:(i + 1) * 256], fu[:, g, tt * P:(tt + 1) * P], dcc[:], start=True, stop=True)
                last.then_inc(df_mm, 1)
            for g in range(4):
                pe.wait_ge(df_ev, 8)
                if g >= 2:
                    pe.wait_ge(t_ready, Q_BF + g - 1)
                for tt in range(4):
                    for i in range(2):
                        last = mm(ps[:, 6 + g % 2, :], xc[:, tt, g, i * P:(i + 1) * P], dft[:, 4 * i + tt, :],
                                  start=(tt == 0 and i == 0), stop=(tt == 3 and i == 1))
                last.then_inc(df_mm, 1)
            slot_loop(S_GF, 4, plain)
            branch(S_BF, Q_BF)
            pe.wait_ge(split_done, Q_M2 + 8)
            slot_loop(S_O2, 4, plain)
            norm_sum(5)
            pe.wait_ge(yn_ready, 1)
            for n in range(8):
                tt, q = n // 2, n % 2
                if n >= 2:
                    pe.wait_ge(y_ev, n - 1)
                for i in range(4):
                    k = 4 * q + i
                    last = nc.tensor.transpose(ps[:, n % 2, i * P:(i + 1) * P], yT[:, k, tt * P:(tt + 1) * P], cc("ident"))
                last.then_inc(y_tr, 1)

        @block.gpsimd
        def _(pool):
            def lo(s, i=None):
                n = s + 1 if i is None else 2 * i + (s + 1)
                pool.wait_ge(hi_ready, n)
                nc.gpsimd.tensor_tensor(wlo[:, s % 2, :], wraw[:, s % 2, :], whi[:, s % 2, :].bitcast(F32),
                                        ALU.subtract).then_inc(lo_ready, 1)

            def lo_many(s0, n):
                if n % 2:
                    lo(s0)
                s0 += n % 2
                if n < 2:
                    return
                with pool.Fori(0, n // 2) as i:
                    for u in range(2):
                        lo(s0 + u, i)

            lo_many(0, S_O0)
            for j in range(14):
                hf = j % 2
                pool.wait_ge(lv_e, j + 1)
                if j >= 2:
                    pool.wait_ge(lv_mm, j + 1)
                nc.gpsimd.tensor_tensor(hKL[:, 3 * hf:3 * hf + 3, :], hk[:, 3 * hf:3 * hf + 3, :],
                                        hE[:, 3 * hf:3 * hf + 3, :], ALU.mult).then_inc(lv_k, 1)
            lo_many(S_O0, S_GC - S_O0)
            for n in range(32):
                cb, h = n // 8, n % 8
                if n == 0:
                    pool.wait_ge(b_in, 128)
                if n >= 4:
                    pool.wait_ge(mx_ready, A_W + n - 3)
                off = (0, -8, -8, -16)[cb] + 16
                nc.gpsimd.tensor_tensor(wbm[:, n % 4, :].rearrange("p (r c) -> p r c", c=32), wbias[:, :, h, off:off + 32],
                                        cc("winmask", 32 * cb, 32).unsqueeze(1).to_broadcast([P, 8, 32]),
                                        ALU.add).then_inc(bm_ready, 1)
            lo_many(S_GC, NS - S_GC)

        @block.scalar
        def _(act):
            A = nc.scalar.activation
            link = Chain(act, ch_act)
            state = {"conv": 0, "q": 0, "ada": False}

            act.dma_start(con[:], dr["con"]).then_inc(c_in, 16)
            act.dma_start(vec[:], dr["vec"]).then_inc(c_in, 16)
            act.dma_start(mtok[:], dr["mem"].rearrange("a (t p) d -> p (a t) d", p=P)).then_inc(m_in, 16)
            nc.scalar.preload_act_table_set("natural_log_exp_and_others")

            def conv(s, i=None, step=2):
                k = 0 if i is None else i
                h = step // 2
                if s >= 2 or i is not None:
                    act.wait_ge(used, k * step + (s - 1))
                act.wait_ge(raw_ready[s % 2], k * (16 * h) + 16 * (s // 2 + 1))
                A(whi[:, s % 2, :], wraw[:, s % 2, :], ACT.Copy).then_inc(hi_ready, 1)

            def conv_upto(n):
                while state["conv"] <= min(n, NS - 1):
                    conv(state["conv"])
                    state["conv"] += 1

            def hi(dst, src=None, wd=T):
                q = state["q"]
                act.wait_ge(t_ready, q + 1)
                A(dst, (src if src is not None else tb[q % 2])[:, 0:wd], ACT.Copy).then_inc(thi_ready, 1)
                state["q"] += 1

            def squares(n, wait):
                for k in range(8):
                    wait(k)
                    i = 8 * n + k
                    if i >= 2:
                        act.wait_ge(sq_added, i - 1)
                    A(tb[k % 2], xT[:, k, :], ACT.Square).then_inc(sq_ready, 1)

            def rnorm(i, src, dst, scale, eps):
                act.wait_ge(sum_ready, i + 1)
                link(A(dst, src, ACT.Ln, bias=eps, scale=scale))
                A(dst, dst, ACT.Exp, scale=-0.5).then_inc(rstd_ready, 1)

            act.wait_ge(c_in, 32)
            conv_upto(0)
            conv_upto(1)
            for n in range(8):
                act.wait_ge(ev, n // 2 + 1)
                if n >= 2:
                    act.wait_ge(msq_added, n - 1)
                A(msq[:, n % 2, :], memT[:, n, :], ACT.Square).then_inc(msq_ready, 1)
            rnorm(0, ps[:, 6, 0:NMEM], msq[:, 2, :], 1.0 / D, cc("e1"))
            squares(0, lambda k: act.wait_ge(ev, 4 + k + 1))
            for l in range(2):
                for k in range(8):
                    hi(mh[l][:, k, :], wd=NMEM)
            rnorm(1, ps[:, 7, :], rstd, 1.0 / D, cc("e1"))
            for k in range(8):
                hi(hh[:, k, :])
            conv_upto(2)

            def hn_sq_(r, tiles):
                for j, (wait, x) in enumerate(tiles):
                    i = HN_AT[r] + j
                    if wait:
                        wait()
                    if i >= 2:
                        act.wait_ge(hn_mm, i - 1)
                    A(sqbuf(i), x, ACT.Square).then_inc(hn_sq, 1)

            def hn_ln(r, scale, eps):
                act.wait_ge(hn_mm, HN_AT[r + 1])
                if r >= 1:
                    act.wait_ge(hn_done, r)
                link(A(rstd, ps[:, 4 + r % 2, :], ACT.Ln, bias=eps, scale=scale))
                A(rstd, rstd, ACT.Exp, scale=-0.5).then_inc(hn_rstd, 1)

            conv_upto(3)
            for l in range(2):
                conv_upto(S_M + 2 * l + 3)
                hn_sq_(H_KM + l, [(lambda: act.wait_ge(emptied, 2 * l + 1), (km0, km1)[l][:].rearrange("p a b -> p (a b)"))])
                hn_ln(H_KM + l, 1.0 / 64, cc("e1"))
            for s in range(S_Z0, S_O0):
                conv_upto(s)
            act.wait_ge(emptied, S_Z0 + 3)
            A(cs, vv("cc", 0, 16), ACT.Silu).then_inc(ada_cs, 1)
            A(hq[:], hq[:], ACT.Silu).then_inc(g_act, 1)
            act.wait_ge(emptied, S_Z0 + 13)
            A(hgate[:], hgate[:], ACT.Silu).then_inc(g_act, 1)
            A(hk[:], hk[:], ACT.Sigmoid).then_inc(g_act, 1)
            nc.scalar.preload_act_table_set("natural_log_exp_and_others")
            act.wait_ge(g_dve, 1)
            A(lbx[:, 0:18], lbx[:, 0:18], ACT.Exp).then_inc(g_act, 1)
            act.wait_ge(g_dve, 2)
            A(hE[:], hb[:], ACT.Ln).then_inc(g_act, 1)
            for j in range(14):
                hf = j % 2
                act.wait_ge(lv_d, j + 1)
                A(hE[:, 3 * hf:3 * hf + 3, :], hE[:, 3 * hf:3 * hf + 3, :], ACT.Exp).then_inc(lv_e, 1)
            act.wait_ge(lv_d, 15)
            A(hE[:], hE[:], ACT.Exp).then_inc(lv_e, 1)
            act.wait_ge(st_k, 1)
            A(hE[:], hb[:], ACT.Exp).then_inc(lv_e, 1)
            act.wait_ge(ada_used, NADA)
            conv_upto(S_O0)
            conv_upto(S_O0 + 1)
            for n in range(HH):
                act.wait_ge(st_tr, n + 1)
                A(hkT[:, n, :, :], ps[:, n % 2, 0:3 * P].rearrange("p (c k) -> p c k", k=P), ACT.Copy).then_inc(st_tc, 1)
            for h in range(HH):
                hn_sq_(H_HG + h, [(lambda: act.wait_ge(ho_cp, h + 1), hA[:, h, :])])
                hn_ln(H_HG + h, 1.0 / P, cc("e1"))
                if h >= 1:
                    hi(hh[:, h - 1, :])
            hi(hh[:, 5, :])
            for j in range(2):
                hn_sq_(H_QM0 + j, [(None, qm0[:, j, :])])
                hn_ln(H_QM0 + j, 1.0, cc("e64"))

            def attention(kind, U0, G0, prb, evac, pvbuf, chunk=None):
                us = units(kind)
                for n in range(len(us) + 4):
                    if n < len(us):
                        u = U0 + n
                        wd = us[n][0] * P
                        act.wait_ge(mx_ready, u + 1)
                        if u >= 3:
                            act.wait_ge(tp_ready, u - 2)
                        A(prb[:, u % 3, 0:wd], ps[:, 4 + u % 3, 0:wd], ACT.Exp, bias=nmx[:, u % 4:u % 4 + 1],
                          accum_out=sm[:, u % 4:u % 4 + 1]).then_inc(ex_ready, 1)
                    if 2 <= n < len(us) + 2:
                        m = n - 2
                        u = U0 + m
                        act.wait_ge(tp_ready, u + 1)
                        w_ = pvbuf(m)
                        if w_:
                            act.wait_ge(pv_done, w_)
                        dst, src = evac(m, ps[:, (7, 3)[u % 2], :])
                        A(dst, src, ACT.Copy).then_inc(pt_ready, 1)
                    if chunk is not None and n >= 4 and us[n - 4][2]:
                        hi(hh[:, chunk + us[n - 4][1], :])

            def mem_att(l):
                def evac(m, b):
                    h, tt = m // 4, m % 4
                    return (pt0, pt1)[l][h % 2][:, 0:2, tt * P:(tt + 1) * P], b[:, 0:256].rearrange("p (c t) -> p c t", t=P)
                G = (G_M0, G_M1)[l]
                attention("mem", (A_M0, A_M1)[l], G, (pr0, pr1)[l], evac, lambda m: G + 1 if m >= 8 else G, 6)

            mem_att(0)

            def out_proj(S, n):
                conv_upto(S + 1)
                conv_upto(S + 2)
                for j in range(4):
                    conv_upto(S + j + 1)
                    act.wait_ge(emptied, S + j + 1)
                    for k in (2 * j, 2 * j + 1):
                        i = 8 * n + k
                        act.wait_ge(sq_added, i - 1)
                        A(tb[k % 2], xT[:, k, :], ACT.Square).then_inc(sq_ready, 1)

            out_proj(S_O0, 1)
            nc.scalar.preload_act_table_set("natural_log_exp_and_others")
            rnorm(2, ps[:, 7, :], rstd, 1.0 / D, cc("e1"))
            for k in range(8):
                hi(hh[:, k, :])

            def ffn_up(S, layer):
                cw, cb = VOFF[f"cw{layer}"], VOFF[f"cb{layer}"]
                b0 = 22 * layer
                assert state["conv"] == S + 1
                with act.Fori(0, 11) as i:
                    for u in range(2):
                        s = S + u
                        par = s % 2
                        conv(s + 1, i)
                        act.wait_ge(used, 2 * i + (s + 1))
                        act.wait_ge(f_lo, 2 * i + b0)
                        for ab in range(2):
                            col = cb + 22 * ab + u
                            wc = cw + 88 + 22 * ab + u
                            A(scr[:, 2 * u + ab, :], ps[:, 2 * par + ab, :], ACT.Identity, bias=vec[:, bass.ds(2 * i + col, 1)],
                              scale=vec[:, bass.ds(2 * i + wc, 1)]).then_inc(f_acc, 1)
                        act.wait_ge(f_conv, 2 * i + (b0 + u + 1))
                        A(scr[:, 2 * u, :], scr[:, 2 * u, :], ACT.Silu).then_inc(f_silu, 1)
                        act.wait_ge(f_g, 2 * i + (b0 + u + 1))
                        A(gh[:].rearrange("p c t -> p (c t)")[:, bass.ds((2 * i + u) * T, T)], scr[:, 2 * u, :],
                          ACT.Copy).then_inc(f_hi, 1)
                state["conv"] = S + 23

            def ffn_down(S, n):
                for k in range(8):
                    for j in (1, 2):
                        conv_upto(S + 2 * k + j)
                    act.wait_ge(emptied, S + 2 * k + 2)
                    i = 8 * n + k
                    act.wait_ge(sq_added, i - 1)
                    A(tb[k % 2], xT[:, k, :], ACT.Square).then_inc(sq_ready, 1)

            ffn_up(S_U0, 0)
            ffn_down(S_D0, 2)
            act.wait_ge(used, S_Z1)
            act.dma_start(posi[:], bass.AP(tensor=dr["pos"].tensor, offset=0, ap=[[0, P], [1, T]])).then_inc(pos_in, 16)
            nc.scalar.preload_act_table_set("natural_log_exp_and_others")
            rnorm(3, ps[:, 7, :], rstd, 1.0 / D, cc("e1"))
            for k in range(8):
                hi(hh[:, k, :])
            conv_upto(S_Z1 + 1)
            for j, dst in enumerate((sinT, cosT)):
                act.wait_ge(rp_d, j + 1)
                A(dst[:], posf[:, j, :], ACT.Sin).then_inc(rp_a, 1)
            nc.scalar.preload_act_table_set("natural_log_exp_and_others")
            for s in range(S_Z1 + 1, S_UQ + 1):
                conv_upto(s)
            hn_sq_(H_C1, [(lambda j=j: act.wait_ge(emptied, S_Z1 + j // 2 + 1), z1[:, j, :]) for j in range(3)])
            hn_sq_(H_C1 + 1, [(lambda j=j: act.wait_ge(emptied, S_Z1 + 3), z1[:, 3 + j, :]) for j in range(2)])
            hn_ln(H_C1, 1.0 / 384, cc("e1"))
            for j in range(3):
                hi(hh[:, j, :])
            hn_ln(H_C1 + 1, 1.0 / 256, cc("e1"))
            for j in range(3, 5):
                hi(hh[:, j, :])
            for s in range(S_UQ, S_O1 + 1):
                conv_upto(s)
            conv_upto(S_O1 + 1)
            act.wait_ge(emptied, S_O1)
            act.wait_ge(split_done, Q_C1 + 5)
            for h in range(HH):
                hn_sq_(H_Q1 + h, [(None, mqn[:, h, :])])
                r = slice(64 * (h % 2), 64 * (h % 2) + 64)
                act.wait_ge(hn_mm, HN_AT[H_Q1 + h])
                A(sqr[r, 0, :], mqr[r, h // 2, :], ACT.Square).then_inc(hn_sq, 1)
                hn_ln(H_Q1 + h, 1.0, cc("e192"))
            for h in range(HH):
                hn_sq_(H_K1 + h, [(None, mkn[:, h, :])])
                act.wait_ge(hn_mm, HN_AT[H_K1 + h])
                A(sqr[0:64, 1, :], posf[0:64, 0, :], ACT.Square).then_inc(hn_sq, 1)
                hn_ln(H_K1 + h, 1.0 / 192, cc("e1"))
            for j in range(2):
                hn_sq_(H_QM1 + j, [(None, z1[:, 6 + j, :])])
                hn_ln(H_QM1 + j, 1.0, cc("e64"))

            def mla_evac(m, b):
                h, i = m // 4, m % 4
                n = i + 1
                return pt1[h % 2][:, 0:n, i * P:(i + 1) * P], b[:, 0:n * P].rearrange("p (c t) -> p c t", t=P)
            act.wait_ge(hn_done, H_QM1 + 2)
            attention("mla", A_MLA, G_MLA, pr1, mla_evac, lambda m: G_MLA + m // 4 - 1 if m >= 8 else G_MLA, 0)
            act.wait_ge(pv_done, G_MLA + 6)
            mem_att(1)
            out_proj(S_O1, 3)
            rnorm(4, ps[:, 7, :], rstd, 1.0 / D, cc("e1"))
            for k in range(8):
                hi(hh[:, k, :])
            ffn_up(S_U1, 1)
            ffn_down(S_D1, 4)

            nc.scalar.preload_act_table_set("natural_log_exp_and_others")
            act.wait_ge(used, S_QKV)
            act.dma_start(ctok[:], dr["ctx"].rearrange("a (t p) d -> p (a t) d", p=P)).then_inc(ctx_in, 16)
            for r in range(8):
                act.dma_start(wbias[r * 16:r * 16 + 16, :, :, :].rearrange("p a b c -> p (a b) c"),
                              dr["rpb"][:, (7 - r) * 8:(7 - r) * 8 + 64, :]).then_inc(b_in, 16)
            rnorm(5, ps[:, 7, :], rstd, 1.0 / D, cc("e1"))
            for k in range(8):
                hi(hh[:, k, :])
            for n in range(8):
                act.wait_ge(ev, 12 + n // 2 + 1)
                act.wait_ge(msq_added, 8 + n - 1)
                A(csq[:, n % 2, :], ctxT[:, n, :], ACT.Square).then_inc(msq_ready, 1)
            conv_upto(S_QKV + 1)
            conv_upto(S_QKV + 2)
            rnorm(6, ps[:, 6, 0:NMEM], csq[:, 2, :], 1.0 / D, cc("e1"))
            for k in range(8):
                hi(ch[:, k, :], wd=NMEM)
            for s in range(S_QKV + 3, S_QKV + 7):
                conv_upto(s)
            for j in range(4):
                act.wait_ge(emptied, S_QKV + 6)
                if j >= 2:
                    act.wait_ge(vt_tr, 3 * (j - 2) + 2)
                for cb in range(4):
                    src = wvr[:, j, :].rearrange("p (r c) -> p r c", c=64)[:, :, KCS[cb]:KCS[cb] + 32]
                    last = A(vtmp[:, j % 2, cb * 256:(cb + 1) * 256].rearrange("p (r c) -> p r c", c=32), src, ACT.Copy)
                last.then_inc(vt_c, 1)
            conv_upto(S_QKV + 7)
            conv_upto(S_QKV + 8)
            act.wait_ge(emptied, S_QKV + 8)
            A(wcz[:], wcz[:], ACT.Silu).then_inc(q_act, 1)
            nc.scalar.preload_act_table_set("natural_log_exp_and_others")
            conv_upto(S_GC)
            act.wait_ge(vt_ev, 12)

            def win_evac(m, b):
                return ptw[:, (A_W + m) % 4, :, :], b.rearrange("p (c t) -> p c t", t=P)
            attention("win", A_W, G_W, pr2, win_evac, lambda m: G_W + m // 2 - 1 if m >= 4 else G_W)
            conv_upto(S_GC + 1)
            for j in range(4):
                hi(bh[:, j, :])

            def gates(S, n0):
                for j in range(4):
                    conv_upto(S + j + 1)
                    act.wait_ge(emptied, S + j + 1)
                    A(sig[:, 2 * j:2 * j + 2, :], sig[:, 2 * j:2 * j + 2, :], ACT.Sigmoid).then_inc(q_act, 1)
                conv_upto(S + 5)
            gates(S_GC, 1)
            conv_upto(S_A)
            for j in range(4):
                conv_upto(S_A + 2 * j + 1)
                conv_upto(S_A + 2 * j + 2)
                act.wait_ge(emptied, S_A + 2 * j + 2)
                A(az[:, j % 2, :], az[:, j % 2, :], ACT.Silu).then_inc(q_act, 1)
                hi(bh[:, j, :])
            gates(S_GA, 9)
            conv_upto(S_F)
            for s in range(S_F, S_F + 5):
                conv_upto(s)
            act.wait_ge(emptied, S_F + 1)
            act.dma_start(dft[:], dr["dft"].rearrange("a (t p) d -> p (a t) d", p=P)).then_inc(dft_in, 16)
            act.dma_start(dcc[:], dr["dcc"]).then_inc(dft_in, 16)
            act.wait_ge(emptied, S_F + 4)
            A(fz[:], fz[:], ACT.Silu).then_inc(q_act, 1)
            for g in range(4):
                hi(bh[:, g, :])
            gates(S_GF, 14)
            conv_upto(S_BF + 1)
            conv_upto(S_BF + 2)
            for k in range(8):
                hi(hh[:, k, :])
            out_proj(S_O2, 5)
            nc.scalar.preload_act_table_set("natural_log_exp_and_others")
            rnorm(7, ps[:, 7, :], rstd, 1.0 / D, cc("e1"))

        @block.vector
        def _(dve):
            V = nc.vector
            TT, TS, STT = V.tensor_tensor, V.tensor_scalar, V.scalar_tensor_tensor
            link = Chain(dve, ch_dve)
            state = {"q": 0, "pend": None}

            def flush():
                if state["pend"] is None:
                    return
                q, src, dh, dl = state["pend"]
                dve.wait_ge(thi_ready, q + 1)
                TT(dl, src, dh.bitcast(F32), ALU.subtract).then_inc(split_done, 1)
                state["pend"] = None

            def split(emit, dh, dl, src=None, wd=T):
                q = state["q"]
                t = (src if src is not None else tb[q % 2])[:, 0:wd]
                if q >= 2:
                    dve.wait_ge(split_done, q - 1)
                emit(t).then_inc(t_ready, 1)
                state["q"] += 1
                flush()
                state["pend"] = (q, t, dh, dl)

            def add_sq(n, k):
                i = 8 * n + k
                dve.wait_ge(sq_ready, i + 1)
                if k:
                    dve.wait_ge(sq_added, i)
                    TT(sqacc, sqacc, tb[k % 2], ALU.add).then_inc(sq_added, 1)
                else:
                    V.tensor_copy(sqacc, tb[k % 2]).then_inc(sq_added, 1)
                if k == 7:
                    dve.wait_ge(sq_added, i + 1)

            def add_msq(buf, n, k):
                i = 8 * n + k
                dve.wait_ge(msq_ready, i + 1)
                if k:
                    dve.wait_ge(msq_added, i)
                    TT(buf[:, 2, :], buf[:, 2, :], buf[:, k % 2, :], ALU.add).then_inc(msq_added, 1)
                else:
                    V.tensor_copy(buf[:, 2, :], buf[:, k % 2, :]).then_inc(msq_added, 1)

            for n in range(4):
                dve.wait_ge(tr, n + 1)
                V.tensor_copy(memT[:, 2 * n:2 * n + 2, :].rearrange("p a b -> p (a b)"), ps[:, 4 + n % 2, :]).then_inc(ev, 1)
            for k in range(8):
                add_msq(msq, 0, k)
            for n in range(8):
                dve.wait_ge(tr, 4 + n + 1)
                V.tensor_copy(xT[:, n, :], ps[:, 4 + n % 2, :]).then_inc(ev, 1)
                if n >= 1:
                    add_sq(0, n - 1)
            add_sq(0, 7)
            dve.wait_ge(rstd_ready, 1)
            for l in range(2):
                for k in range(8):
                    split(lambda t: STT(out=t, in0=memT[:, k, :], scalar=vv(f"mem{l}", k), in1=msq[:, 2, :],
                                        op0=ALU.mult, op1=ALU.mult), mh[l][:, k, :], ml[l][:, k, :], wd=NMEM)
            flush()

            def norm_h(i, g):
                dve.wait_ge(rstd_ready, i)
                for k in range(8):
                    split(lambda t: STT(out=t, in0=xT[:, k, :], scalar=vv(g, k), in1=rstd, op0=ALU.mult, op1=ALU.mult),
                          hh[:, k, :], hl[:, k, :])
                flush()

            norm_h(2, "mix0")

            def empty(s):
                dve.wait_ge(used, s + 1)

            def bank(s, b):
                return ps[:, 2 * (s % 2) + b, :]

            def copy(dst, src):
                return TS(dst, src, 1.0, None, ALU.mult)

            for l in range(2):
                empty(2 * l)
                V.tensor_copy((km0, km1)[l][:].rearrange("p a b -> p (a b)"), bank(2 * l, 0)).then_inc(emptied, 1)
                empty(2 * l + 1)
                V.tensor_copy((vm0, vm1)[l][:].rearrange("p a b -> p (a b)"), bank(2 * l + 1, 0)).then_inc(emptied, 1)

            def hn_apply(r, ops):
                dve.wait_ge(hn_rstd, r + 1)
                for n, (dst, src, g) in enumerate(ops):
                    ins = STT(out=dst, in0=src, scalar=g, in1=rstd, op0=ALU.mult, op1=ALU.mult)
                ins.then_inc(hn_done, 1)

            for l in range(2):
                kk = (km0, km1)[l][:].rearrange("p a b -> p (a b)")
                hn_apply(H_KM + l, [(kk, kk, vv(f"mk{l}"))])

            for s in range(S_Z0, S_O0):
                j = s - S_Z0
                empty(s)
                if 6 <= j < 9:
                    for q in range(2):
                        last = V.tensor_copy(hv[:, 2 * q:2 * q + 2, (j - 6) * 256:(j - 5) * 256],
                                             bank(s, q).rearrange("p (a b) -> p a b", b=256))
                else:
                    dst, n = (hq, 0) if j < 3 else (hk, 6) if j < 6 else (hgate, 18) if j < 12 else (qm0, 24)
                    for b in range(2):
                        last = V.tensor_copy(dst[:, 2 * j + b - n, :], bank(s, b))
                last.then_inc(emptied, 1)

            l3 = vv("lb", 0, 18).rearrange("p (r h) -> p r h", h=HH)
            mxl, e3, sl = lbx[:, 18:24], lbx[:, 0:18].rearrange("p (r h) -> p r h", h=HH), lbt
            link(TT(mxl, l3[:, 0, :], l3[:, 1, :], ALU.max))
            link(TT(mxl, mxl, l3[:, 2, :], ALU.max))
            TT(e3, l3, mxl.unsqueeze(1).to_broadcast([P, 3, HH]), ALU.subtract).then_inc(g_dve, 1)
            dve.wait_ge(g_act, 4)
            link(TT(sl, e3[:, 0, :], e3[:, 1, :], ALU.add))
            link(TT(sl, sl, e3[:, 2, :], ALU.add))
            link(V.reciprocal(sl, sl))
            link(TT(lbt, e3[:, 0, :], sl, ALU.mult))
            link(TS(oml, lbt, -1.0, 1.0, ALU.mult, ALU.add))
            for h in range(HH):
                last = TS(hb[:, h, :], hk[:, h, :], oml[:, h:h + 1], lbt[:, h:h + 1], ALU.mult, ALU.add)
            last.then_inc(g_dve, 1)
            dve.wait_ge(g_dve, 2)
            TS(hk[:], hb[:], -1.0, 1.0, ALU.mult, ALU.add).then_inc(g_dve, 1)
            dve.wait_ge(g_act, 5)
            dve.wait_ge(g_dve, 3)
            for h in range(HH):
                last = V.tensor_tensor_scan(hb[:, h, :], cc("scan"), hE[:, h, :], 0.0, ALU.mult, ALU.add)
            last.then_inc(g_dve, 1)

            SC = float(P) ** -0.5
            dve.wait_ge(g_dve, 4)

            def lv_diff(j):
                hf, l = j % 2, j // 2
                h = 64 >> l
                if j >= 2:
                    dve.wait_ge(lv_k, j - 1)
                    dve.wait_ge(lv_q, j - 1)
                G = 3 * T // (2 * h)
                b = hb[:, 3 * hf:3 * hf + 3, :].rearrange("p a t -> p (a t)").rearrange("p (g t) -> p g t", t=2 * h)
                e = hE[:, 3 * hf:3 * hf + 3, :].rearrange("p a t -> p (a t)").rearrange("p (g t) -> p g t", t=2 * h)
                mid = b[:, :, h - 1:h].to_broadcast([P, G, h])
                TT(e[:, :, h:2 * h], b[:, :, h:2 * h], mid, ALU.subtract)
                TT(e[:, :, 0:h], mid, b[:, :, 0:h], ALU.subtract).then_inc(lv_d, 1)

            for hf in range(2):
                dve.wait_ge(lv_mm, hf + 1)
                for h in range(3 * hf, 3 * hf + 3):
                    last = STT(out=hA[:, h, :].rearrange("p (c t) -> p c t", t=P), in0=ps[:, h, :].rearrange("p (c t) -> p c t", t=P),
                               scalar=SC, in1=cc("ident").unsqueeze(1).to_broadcast([P, 4, P]), op0=ALU.mult, op1=ALU.mult)
                last.then_inc(lv_cp, 1)
            lv_diff(0)
            for j in range(14):
                hf, l = j % 2, j // 2
                h = 64 >> l
                if j < 13:
                    lv_diff(j + 1)
                dve.wait_ge(lv_e, j + 1)
                if j >= 2:
                    dve.wait_ge(lv_mm, j + 1)
                rt = lambda x: x[:, 3 * hf:3 * hf + 3, :].rearrange("p a t -> p (a t)").rearrange("p (g t) -> p g t", t=2 * h)[:, :, h:2 * h]
                STT(out=hQL[:, 3 * hf:3 * hf + 3, :].rearrange("p a t -> p (a t)").rearrange("p (g t) -> p g t", t=h),
                    in0=rt(hq), scalar=SC, in1=rt(hE), op0=ALU.mult, op1=ALU.mult).then_inc(lv_q, 1)

                def copies(j):
                    hf, l = j % 2, j // 2
                    h = 64 >> l
                    dve.wait_ge(lv_mm, j + 3)
                    dve.wait_ge(lv_cp, 2)
                    n = 64 // h
                    msk = cc("lvl", 64 * l, 64).bitcast(U32)
                    for h3 in range(3):
                        hd = 3 * hf + h3
                        o = h3 * 256
                        for c in range(4):
                            src = ps[:, 3 * hf + o // 512, o % 512 + 64 * c:o % 512 + 64 * c + 64].rearrange("p (g t) -> p g t", t=h)
                            dst = hA[:, hd, c * P:(c + 1) * P].rearrange("p (g t) -> p g t", t=2 * h)[:, :, h:2 * h]
                            last = V.copy_predicated(dst, msk.rearrange("p (g t) -> p g t", t=h), src)
                    last.then_inc(lv_cp, 1)
                if j >= 1:
                    copies(j - 1)
            copies(13)
            b4 = hb[:].rearrange("p a t -> p (a t)").rearrange("p (g t) -> p g t", t=P)
            e4 = hE[:].rearrange("p a t -> p (a t)").rearrange("p (g t) -> p g t", t=P)
            dve.wait_ge(lv_k, 14)
            dve.wait_ge(lv_q, 14)
            TT(e4, b4[:, :, P - 1:P].to_broadcast([P, 24, P]), b4, ALU.subtract).then_inc(lv_d, 1)
            dve.wait_ge(lv_e, 15)
            TT(hKL[:], hk[:], hE[:], ALU.mult).then_inc(st_k, 1)
            dve.wait_ge(lv_e, 16)
            link(STT(out=hq[:], in0=hq[:], scalar=SC, in1=hE[:], op0=ALU.mult, op1=ALU.mult))
            for n in range(HH):
                dve.wait_ge(st_kv, n + 1)
                for c in range(3):
                    kvp = ps[:, 2 + n % 2, c * P:(c + 1) * P]
                    if c == 0:
                        ins = copy(hS[:, 0, n, :], kvp)
                    else:
                        ins = STT(out=hS[:, c, n, :], in0=hS[:, c - 1, n, :], scalar=hE[:, n, c * P + P - 1:c * P + P], in1=kvp,
                                  op0=ALU.mult, op1=ALU.add)
                    if c < 2:
                        link(ins)
                ins.then_inc(st_s, 1)
            dve.wait_ge(ada_used, NADA)
            link(TT(mod.rearrange("p (n c) -> p n c", c=2), ps[:, 7, 0:48].rearrange("p (n c) -> p n c", c=2),
                    vv("bada", 0, 24).unsqueeze(2).to_broadcast([P, 24, 2]), ALU.add))
            TS(gsc, mod[:, 16:32], 1.0, None, ALU.add).then_inc(mod_ready, 1)
            dve.wait_ge(mod_ready, 1)
            link(TT(gsc.rearrange("p (n c) -> p n c", c=2), gsc.rearrange("p (n c) -> p n c", c=2),
                    vv("ng2", 0, 8).unsqueeze(2).to_broadcast([P, 8, 2]), ALU.mult))

            def gated(h):
                split(lambda t: TT(t, hA[:, h, :], hgate[:, h, :], ALU.mult), hh[:, h, :], hl[:, h, :])
            for h in range(HH):
                dve.wait_ge(ho_mm, h + 1)
                V.tensor_copy(hA[:, h, :], ps[:, h % 2, :]).then_inc(ho_cp, 1)
                if h >= 1:
                    hn_apply(H_HG + h - 1, [(hA[:, h - 1, :], hA[:, h - 1, :], vv("hgo"))])
                    dve.wait_ge(hn_done, H_HG + h)
                    gated(h - 1)
            hn_apply(H_HG + 5, [(hA[:, 5, :], hA[:, 5, :], vv("hgo"))])
            dve.wait_ge(hn_done, H_HG + 6)
            gated(5)
            flush()
            for j in range(2):
                hn_apply(H_QM0 + j, [(qm0[:, j, :], qm0[:, j, :], vv("mq0"))])

            def attention(kind, U0, G0, prb, consume):
                us = units(kind)
                for n in range(len(us) + 4):
                    if n < len(us):
                        u = U0 + n
                        wd = us[n][0] * P
                        dve.wait_ge(sc_ready, u + 1)
                        if kind == "win":
                            dve.wait_ge(bm_ready, n + 1)
                            b = ps[:, 4 + u % 3, 0:256]
                            link(TT(b, b, wbm[:, n % 4, :], ALU.add))
                        V.tensor_reduce(nmx[:, u % 4:u % 4 + 1], ps[:, 4 + u % 3, 0:wd], AX, ALU.max,
                                        negate=True).then_inc(mx_ready, 1)
                    if 1 <= n < len(us) + 1:
                        u = U0 + n - 1
                        wd = us[n - 1][0] * P
                        dve.wait_ge(ex_ready, u + 1)
                        link(V.reciprocal(rc[:, u % 4:u % 4 + 1], sm[:, u % 4:u % 4 + 1]))
                        x = prb[:, u % 3, 0:wd]
                        TS(x, x, rc[:, u % 4:u % 4 + 1], None, ALU.mult).then_inc(pn_ready, 1)
                    if n >= 4 and us[n - 4][2]:
                        g = us[n - 4][1]
                        dve.wait_ge(pv_done, G0 + g + 1)
                        consume(g, (G0 + g) % 2)

            def take(c):
                def f(g, b):
                    split(lambda t: copy(t, ps[:, b, :]), hh[:, c + g, :], hl[:, c + g, :])
                return f

            attention("mem", A_M0, G_M0, pr0, take(6))
            flush()

            def out_proj(S, n, gate=None):
                for j in range(4):
                    s = S + j
                    empty(s)
                    for b in range(2):
                        x = xT[:, 2 * j + b, :]
                        if gate is None:
                            last = TT(x, x, bank(s, b), ALU.add)
                        else:
                            last = STT(out=x, in0=bank(s, b), scalar=gate(2 * j + b), in1=x, op0=ALU.mult, op1=ALU.add)
                    last.then_inc(emptied, 1)
                    for k in (2 * j - 2, 2 * j - 1):
                        if k >= 0:
                            add_sq(n, k)
                add_sq(n, 6)
                add_sq(n, 7)

            out_proj(S_O0, 1)
            norm_h(3, "ffn0")

            def ffn_up(S, layer):
                cw = VOFF[f"cw{layer}"]
                b0 = 22 * layer
                with dve.Fori(0, 11) as i:
                    for u in range(2):
                        s = S + u
                        par = s % 2
                        n = 2 * b0 + 2 * u
                        a, b = scr[:, 2 * u, :], scr[:, 2 * u + 1, :]
                        pa, pb = ps[:, 2 * par, :], ps[:, 2 * par + 1, :]

                        def tap(dst, src, d, col, sm_):
                            STT(out=dst[:, d:T], in0=src[:, 0:T - d], scalar=vec[:, bass.ds(2 * i + col, 1)], in1=dst[:, d:T],
                                op0=ALU.mult, op1=ALU.add).then_inc(sm_, 1)
                        dve.wait_ge(f_acc, 4 * i + (n + 1))
                        tap(a, pa, 1, cw + 44 + u, f_tap)
                        dve.wait_ge(f_acc, 4 * i + (n + 2))
                        tap(b, pb, 1, cw + 44 + 22 + u, f_tap)
                        dve.wait_ge(f_tap, 4 * i + (n + 1))
                        tap(a, pa, 2, cw + u, f_conv)
                        dve.wait_ge(f_tap, 4 * i + (n + 2))
                        tap(b, pb, 2, cw + 22 + u, emptied)
                        dve.wait_ge(f_silu, 2 * i + (b0 + u + 1))
                        dve.wait_ge(emptied, 2 * i + (s + 1))
                        TT(a, a, b, ALU.mult).then_inc(f_g, 1)
                        dve.wait_ge(f_hi, 2 * i + (b0 + u + 1))
                        sl_ = bass.ds((2 * i + u) * T, T)
                        TT(gl[:].rearrange("p c t -> p (c t)")[:, sl_], a,
                           gh[:].rearrange("p c t -> p (c t)")[:, sl_].bitcast(F32), ALU.subtract).then_inc(f_lo, 1)

            def ffn_down(S, n):
                dve.wait_ge(f_lo, 22 * (n // 2))
                for k in range(8):
                    empty(S + 2 * k + 1)
                    x = xT[:, k, :]
                    TT(x, x, ps[:, k % 2, :], ALU.add).then_inc(emptied, 2)
                    if k:
                        add_sq(n, k - 1)
                add_sq(n, 7)

            ffn_up(S_U0, 0)
            ffn_down(S_D0, 2)

            norm_h(4, "mix1")
            dve.wait_ge(pos_in, 16)
            link(V.tensor_copy(rtmp[:, 0, :], posi[:]))
            ang = rtmp[:, 0, :]
            link(TS(ang, ang, cc("inv"), None, ALU.mult))
            for j in range(2):
                n_, r_ = rtmp[:, 1, :], posf[:, j, :]
                link(TS(n_, ang, 1.0 / TWO_PI, 0.25 * j, ALU.mult, ALU.add))
                link(TS(n_, n_, MAGIC, -MAGIC, ALU.add, ALU.add))
                link(STT(out=r_, in0=n_, scalar=-C1, in1=ang, op0=ALU.mult, op1=ALU.add))
                link(STT(out=r_, in0=n_, scalar=-C2, in1=r_, op0=ALU.mult, op1=ALU.add))
                link(STT(out=r_, in0=n_, scalar=-C3, in1=r_, op0=ALU.mult, op1=ALU.add))
                if j:
                    link(TS(r_, r_, float(np.pi / 2), None, ALU.add))
                TS(r_, r_, 3.1415925, -3.1415925, ALU.min, ALU.max).then_inc(rp_d, 1)
            for s in range(S_Z1, S_UQ):
                empty(s)
                for b in range(2):
                    last = V.tensor_copy(z1[:, 2 * (s - S_Z1) + b, :], bank(s, b))
                last.then_inc(emptied, 1)
            for r, (c0, nn, g) in enumerate(((0, 3, "qa"), (3, 2, "kva"))):
                dve.wait_ge(hn_rstd, H_C1 + r + 1)
                for j in range(nn):
                    split(lambda t: STT(out=t, in0=z1[:, c0 + j, :], scalar=vv(g, j), in1=rstd, op0=ALU.mult, op1=ALU.mult),
                          hh[:, c0 + j, :], hl[:, c0 + j, :])
                flush()
                dve.wait_ge(split_done, state["q"])
                dve.sem_inc(hn_done, 1)
            dve.wait_ge(rp_a, 2)
            link(V.tensor_copy(posf[:, 0, :], z1[:, 5, :]))
            TS(z1[:, 5, :], z1[:, 5, :], vv("knr"), None, ALU.mult).then_inc(kq_ready, 1)
            for s in range(S_UQ, S_UKV):
                p = s - S_UQ
                empty(s)
                V.tensor_copy(mqn[:, 2 * p, :], ps[:, 0, :])
                V.tensor_copy(mqn[:, 2 * p + 1, :], ps[:, 1, :])
                V.tensor_copy(mqr[:, p, :], ps[:, 2, :]).then_inc(emptied, 1)
            for s in range(S_UKV, S_O1):
                p = s - S_UKV
                empty(s)
                V.tensor_copy(mkn[:, 2 * p, :], ps[:, 0, :])
                V.tensor_copy(mkn[:, 2 * p + 1, :], ps[:, 1, :])
                for q in range(2):
                    last = V.tensor_copy(mv[:, 2 * q:2 * q + 2, p * 256:(p + 1) * 256],
                                         ps[:, 2 + q, :].rearrange("p (a b) -> p a b", b=256))
                last.then_inc(emptied, 1)

            def rope(x, r):
                dve.wait_ge(rot_mm, r + 1)
                TT(rtmp[:, 0, :], ps[:, 6, :], sinT[:], ALU.mult).then_inc(rot_rd, 1)
                link(TT(rtmp[:, 1, :], x, cosT[:], ALU.mult))
                dve.wait_ge(rot_rd, r + 1)

            for h in range(HH):
                r = slice(64 * (h % 2), 64 * (h % 2) + 64)
                dve.wait_ge(hn_rstd, H_Q1 + h + 1)
                STT(out=mqr[r, h // 2, :], in0=mqr[r, h // 2, :], scalar=vv("qnr")[r, :], in1=scr[r, 1, :], op0=ALU.mult, op1=ALU.mult)
                STT(out=mqn[:, h, :], in0=mqn[:, h, :], scalar=vv("qnn"), in1=rstd, op0=ALU.mult, op1=ALU.mult).then_inc(hn_done, 1)
                if h % 2 == 1:
                    rope(mqr[:, h // 2, :], h // 2)
                    link(TT(mqr[:, h // 2, :], rtmp[:, 0, :], rtmp[:, 1, :], ALU.add))
            rope(z1[:, 5, :], 3)
            link(TT(kr0[:], rtmp[:, 0, :], rtmp[:, 1, :], ALU.add))
            for h in range(HH):
                r = slice(64 * (h % 2), 64 * (h % 2) + 64)
                dve.wait_ge(hn_rstd, H_K1 + h + 1)
                TT(mkr[r, h // 2, :], kr0[r, :], scr[r, 1, :], ALU.mult)
                STT(out=mkn[:, h, :], in0=mkn[:, h, :], scalar=vv("knn"), in1=rstd, op0=ALU.mult, op1=ALU.mult).then_inc(hn_done, 1)
            for j in range(2):
                hn_apply(H_QM1 + j, [(z1[:, 6 + j, :], z1[:, 6 + j, :], vv("mq1"))])
            attention("mla", A_MLA, G_MLA, pr1, take(0))
            flush()
            attention("mem", A_M1, G_M1, pr1, take(6))
            flush()
            out_proj(S_O1, 3)
            norm_h(5, "ffn1")
            ffn_up(S_U1, 1)
            ffn_down(S_D1, 4)

            def norm_mod(i, src, rs, K, c, dh, dl, wd):
                dve.wait_ge(rstd_ready, i)
                for k in range(8):
                    def emit(t):
                        link(STT(out=t, in0=src[:, k, :], scalar=gsc[:, 2 * k + c:2 * k + c + 1], in1=rs, op0=ALU.mult, op1=ALU.mult))
                        return TS(t, t, mod[:, 2 * k + c:2 * k + c + 1], None, ALU.add)
                    split(emit, dh[:, k, :], dl[:, k, :], wd=wd)
                flush()

            norm_mod(6, xT, rstd, 8, 0, hh, hl, T)
            for n in range(4):
                dve.wait_ge(tr, 12 + n + 1)
                V.tensor_copy(ctxT[:, 2 * n:2 * n + 2, :].rearrange("p a b -> p (a b)"), ps[:, 4 + n % 2, :]).then_inc(ev, 1)
            for k in range(8):
                add_msq(csq, 1, k)

            def bcol(n):
                return vv("bin", n)
            B_AX, B_AB, B_AC, B_AZ, B_FU, B_FZ, B_Q, B_K, B_V, B_CZ, B_GA, B_GF, B_GC = 0, 4, 8, 12, 16, 20, 24, 28, 32, 36, 40, 48, 56
            for s in (S_QKV, S_QKV + 1):
                empty(s)
                for b in range(2):
                    j = 2 * (s - S_QKV) + b
                    for cb in range(4):
                        last = TS(wq[:, j, cb * P:(cb + 1) * P].rearrange("p (r q) -> p r q", q=16),
                                  bank(s, b).rearrange("p (r c q) -> p r c q", c=4, q=16)[:, :, cb, :],
                                  bcol(B_Q + j), 0.125, ALU.add, ALU.mult)
                last.then_inc(emptied, 1)
            norm_mod(7, ctxT, csq[:, 2, :], 8, 1, ch, cl, NMEM)
            for s in range(S_QKV + 2, S_QKV + 6):
                j0 = s - S_QKV - 2
                empty(s)
                lat, cxt, bb = (wk, wkc, B_K) if j0 < 2 else (wvr, wvc, B_V)
                for b in range(2):
                    j = 2 * (j0 % 2) + b
                    TS(lat[:, j, :], bank(s, b), bcol(bb + j), None, ALU.add)
                    last = TS(cxt[:, j, :], ps[:, 4 + s % 2, b * NMEM:(b + 1) * NMEM], bcol(bb + j), None, ALU.add)
                last.then_inc(emptied, 1)
            for j in range(4):
                for q in range(3):
                    dve.wait_ge(vt_tr, 3 * j + q + 1)
                    if q < 2:
                        last = V.tensor_copy(vtok[:, 4 * q:4 * q + 4, j * P:(j + 1) * P], ps[:, 4 + q, :].rearrange("p (a b) -> p a b", b=P))
                    else:
                        last = V.tensor_copy(vct[:, :, j * P:(j + 1) * P], ps[:, 6, 0:256].rearrange("p (a b) -> p a b", b=P))
                    last.then_inc(vt_ev, 1)
            for s in (S_QKV + 6, S_QKV + 7):
                empty(s)
                for b in range(2):
                    j = 2 * (s - S_QKV - 6) + b
                    last = TS(wcz[:, j, :], bank(s, b), bcol(B_CZ + j), None, ALU.add)
                last.then_inc(emptied, 1)
            dve.wait_ge(q_act, 1)

            def win_take(g, b):
                cb, hp = g // 4, g % 4
                y = wcz[:, hp, :].rearrange("p (r c q) -> p r c q", c=4, q=16)[:, :, cb, :]
                TT(y, ps[:, b, 0:P].rearrange("p (r q) -> p r q", q=16), y, ALU.mult).then_inc(o_read, 1)
            attention("win", A_W, G_W, pr2, win_take)
            dve.wait_ge(o_read, 16)
            for j in range(4):
                split(lambda t: copy(t, wcz[:, j, :]), bh[:, j, :], bl[:, j, :])
            flush()

            def gates(S, bb):
                for j in range(4):
                    empty(S + j)
                    for b in range(2):
                        last = TS(sig[:, 2 * j + b, :], bank(S + j, b), bcol(bb + 2 * j + b), None, ALU.add)
                    last.then_inc(emptied, 1)

            def branch(S, n, first, add=True):
                dve.wait_ge(q_act, n)
                for s in (S, S + 1):
                    empty(s)
                    for b in range(4):
                        k = 4 * (s - S) + b
                        o = ps[:, 4 * (s % 2) + b, :]
                        if first:
                            last = TT(mm_[:, k, :], o, sig[:, k, :], ALU.mult)
                        else:
                            last = TT(sig[:, k, :], o, sig[:, k, :], ALU.mult)
                    last.then_inc(emptied, 1)
                if not first and add:
                    dve.wait_ge(emptied, S + 2)
                    link(TT(mm_[:], mm_[:], sig[:], ALU.add))

            gates(S_GC, B_GC)
            branch(S_BC, 5, True)
            for j in range(4):
                s = S_A + 2 * j
                p_ = atmp[:, 0, :]
                empty(s)
                link(TS(atmp[:, 1, :], bank(s, 0), bcol(B_AC + j), None, ALU.add))
                STT(out=p_, in0=bank(s, 1), scalar=bcol(B_AX + j), in1=atmp[:, 1, :], op0=ALU.add, op1=ALU.mult).then_inc(emptied, 1)
                dve.wait_ge(emptied, s + 1)
                a = acc2[:, j % 2, :]
                link(TS(a, p_, vv("wc2", 4 + j), vv("bc2", j), ALU.mult, ALU.add))
                link(STT(out=a[:, 1:T], in0=p_[:, 0:T - 1], scalar=vv("wc2", j), in1=a[:, 1:T], op0=ALU.mult, op1=ALU.add))
                link(STT(out=a[:, 0:T - 1], in0=p_[:, 1:T], scalar=vv("wc2", 8 + j), in1=a[:, 0:T - 1], op0=ALU.mult, op1=ALU.add))
                empty(s + 1)
                link(STT(out=a, in0=bank(s + 1, 0), scalar=bcol(B_AB + j), in1=a, op0=ALU.add, op1=ALU.mult))
                TS(az[:, j % 2, :], bank(s + 1, 1), bcol(B_AZ + j), None, ALU.add).then_inc(emptied, 1)
                dve.wait_ge(q_act, 5 + j + 1)
                split(lambda t: TT(t, a, az[:, j % 2, :], ALU.mult), bh[:, j, :], bl[:, j, :])
            flush()
            gates(S_GA, B_GA)
            branch(S_BA, 13, False)
            for s in range(S_F, S_F + 4):
                j0 = s - S_F
                empty(s)
                for b in range(2):
                    j = 2 * (j0 % 2) + b
                    last = TS((fu, fz)[j0 // 2][:, j, :], bank(s, b), bcol((B_FU, B_FZ)[j0 // 2] + j), None, ALU.add)
                last.then_inc(emptied, 1)
            for n in range(8):
                g, q = n // 2, n % 2
                dve.wait_ge(df_mm, n + 1)
                TS(xc[:, 2 * q:2 * q + 2, g, :], ps[:, 4 + n % 2, :].rearrange("p (a b) -> p a b", b=256), 1.0 / 256, None,
                   ALU.mult).then_inc(df_ev, 1)
            dve.wait_ge(q_act, 14)
            for g in range(4):
                dve.wait_ge(df_mm, 8 + g + 1)
                split(lambda t: TT(t, ps[:, 6 + g % 2, :], fz[:, g, :], ALU.mult), bh[:, g, :], bl[:, g, :])
            flush()
            gates(S_GF, B_GF)
            branch(S_BF, 18, False, add=False)
            dve.wait_ge(emptied, S_BF + 2)
            for k in range(8):
                split(lambda t: TT(t, mm_[:, k, :], sig[:, k, :], ALU.add), hh[:, k, :], hl[:, k, :])
            flush()
            out_proj(S_O2, 5, gate=lambda k: mod[:, 32 + 2 * k:33 + 2 * k])
            dve.wait_ge(rstd_ready, 8)
            for k in range(8):
                last = STT(out=yT[:, k, :], in0=xT[:, k, :], scalar=vv("fin", k), in1=rstd, op0=ALU.mult, op1=ALU.mult)
            last.then_inc(yn_ready, 1)
            for n in range(8):
                tt, q = n // 2, n % 2
                dve.wait_ge(y_tr, n + 1)
                V.tensor_copy(ytok[:, tt, q * T:(q + 1) * T], ps[:, n % 2, :]).then_inc(y_ev, 1)


def slots(wm, K, cols):
    n = wm.shape[1] // cols
    return np.ascontiguousarray(wm.reshape(K, P, n, cols).transpose(2, 1, 0, 3).reshape(n, P, K * cols))


def padded(a):
    return np.concatenate([a, np.zeros((a.shape[0], P, SLOT - a.shape[2]), a.dtype)], axis=2) if a.shape[2] < SLOT else a


def paired(wm, a, b, n):
    x = wm[:, a:a + n * P].reshape(-1, n, 1, P)
    y = wm[:, b:b + n * P].reshape(-1, n, 1, P)
    return slots(np.concatenate([x, y], axis=2).reshape(-1, 2 * n * P), 8, 256)


def down(wm):
    return np.ascontiguousarray(wm.reshape(2, 11, P, 8, P).transpose(3, 0, 2, 1, 4).reshape(16, P, DSLOT))


def columns(v):
    return v.reshape(-1, P).T


def constants():
    c = {n: np.zeros((P, k), np.float32) for n, k in CON}
    c["ones"][:] = 1
    c["ident"][:] = np.eye(P)
    c["b64"][:64, :64] = c["b64"][64:, 64:] = 1
    for b in (0, 64):
        for j in range(32):
            c["rot"][b + j + 32, b + j] = -1
            c["rot"][b + j, b + j + 32] = 1
    i = np.arange(P)
    c["causal"][:] = np.where(i[None, :] <= i[:, None], 0, NEG)
    for cb in range(4):
        q = cb * 16 + i % 16
        lo = np.clip(q - 8, 0, 48)
        kc = KCS[cb] + np.arange(32)
        c["winmask"][:, cb * 32:(cb + 1) * 32] = np.where((kc >= lo[:, None]) & (kc < lo[:, None] + 16), 0, NEG)
    c["scan"][:] = (np.arange(T) % P != 0)
    for l in range(7):
        h = 64 >> l
        t = np.arange(64)
        c["lvl"][:, 64 * l:64 * l + 64] = i[:, None] // h == 2 * (t // h)[None, :]
    c["inv"][:, 0] = np.float32(10000.0) ** (-(i % 32).astype(np.float32) / np.float32(32))
    c["e1"][:], c["e64"][:], c["e192"][:] = EPS, 64 * EPS, 192 * EPS
    return np.concatenate([c[n] for n, _ in CON], axis=1)


def layout(i):
    d = {"x": i["x"], "mem": i["mem"], "pos": i["positions"], "ctx": i["ctx_2"]}
    mk = i["w_mem_kv"]
    d["w0"] = np.concatenate([slots(mk[0], 8, 256), slots(mk[1], 8, 256), slots(i["hg_w_in"][0], 8, 256)])

    def out_up(l):
        return [slots(i["w_out"][l], 8, 256), paired(i["w_up"][l], 0, FF, FC)]
    d["w0b"] = np.concatenate(out_up(0))
    d["wd0"], d["wd1"] = down(i["w_down"][0]), down(i["w_down"][1])
    win = i["mla_w_in"][0]
    z = np.concatenate([win[:, 0:704], win[:, 640:704], win[:, 704:960]], axis=1)
    uq = i["mla_w_uq"][0].reshape(384, 3, 2, 192)
    uq = np.concatenate([uq[:, :, :, 0:128].reshape(384, 3, 256), uq[:, :, :, 128:192].reshape(384, 3, 128)], axis=2)
    ukv = i["mla_w_ukv"][0].reshape(256, 3, 2, 2, 128).transpose(0, 1, 3, 2, 4)
    d["w1"] = np.concatenate([slots(z, 8, 256), padded(slots(uq.reshape(384, 1152), 3, 384)),
                              padded(slots(ukv.reshape(256, 1536), 2, 512))] + out_up(1))
    w2 = i["w_in_2"][0]
    br = lambda n: slots(i[n][0], 4, 512)
    conv = np.stack([paired(w2, 1024, 0, 4), paired(w2, 512, 1536, 4)], axis=1).reshape(8, P, SLOT)
    d["w2"] = np.concatenate([slots(w2[:, 3072:5120], 8, 256), slots(w2[:, 7168:8192], 8, 256), br("w_br_c_2"),
                              conv, slots(w2[:, 5120:6144], 8, 256), br("w_br_a_2"),
                              slots(w2[:, 2048:3072], 8, 256), slots(w2[:, 6144:7168], 8, 256), br("w_br_f_2"),
                              slots(i["w_out_2"][0], 8, 256)])
    d["wada"] = slots(i["w_ada_2"][0], 8, 256)
    r = i["rpb_2"][0].transpose(1, 0, 2)
    r = np.pad(r, ((0, 0), (0, 0), (16, 17))).reshape(120, 64)
    d["rpb"] = np.stack([r[:, 15 - q:63 - q] for q in range(16)])
    twice = lambda v: np.concatenate([v, v]).reshape(P, 1)
    v = {}
    for l in range(2):
        v[f"mix{l}"], v[f"ffn{l}"], v[f"mem{l}"] = (columns(i[n][l]) for n in ("mix_norm_g", "ffn_norm_g", "mem_norm_g"))
        v[f"cw{l}"], v[f"cb{l}"] = columns(i["conv_w"][l]), columns(i["conv_b"][l])
        v[f"mq{l}"], v[f"mk{l}"] = twice(i["mem_q_norm_g"][l]), twice(i["mem_k_norm_g"][l])
    v["bin"], v["bada"], v["ng2"], v["fin"] = columns(i["b_in_2"][0]), columns(i["b_ada_2"][0]), columns(i["norm_g_2"][0]), columns(i["final_g_2"])
    v["wc2"], v["bc2"] = columns(i["w_conv_2"][0]), columns(i["b_conv_2"][0])
    v["cc"] = np.stack([columns(i["c_2"][0]), columns(i["c_ctx_2"])], axis=2).reshape(P, 16)
    v["lb"], v["hgo"] = columns(i["hg_lb_logits"]), columns(i["hg_out_norm_g"][0])
    v["qa"], v["kva"] = columns(i["mla_qa_norm_g"][0]), columns(i["mla_kva_norm_g"][0])
    for n, k in (("qn", "mla_q_norm_g"), ("kn", "mla_k_norm_g")):
        v[n + "n"], v[n + "r"] = i[k][0][0:128].reshape(P, 1), twice(i[k][0][128:192])
    d["vec"] = np.ascontiguousarray(np.concatenate([v[n] for n, _ in VEC], axis=1))
    d["con"] = constants()
    t = np.arange(T)
    a = (t[:, None] * t[None, :] % T) * (TWO_PI / T)
    c = np.arange(P)
    b = (c[:, None] * c[None, :] % P) * (TWO_PI / P)
    d["dft"] = np.stack([np.cos(a), np.sin(a)]).astype(np.float32)
    d["dcc"] = np.concatenate([np.cos(b), -np.sin(b)], axis=1).astype(np.float32)
    return d


def kernel(**inputs):
    import concourse.bacc as bacc
    from concourse.bass_utils import run_bass_kernel_spmd as run

    nc = bacc.Bacc("TRN2", target_bir_lowering=False, num_devices=1)
    arrays, dr = {}, {}
    for name, a in layout({k: np.asarray(v) for k, v in inputs.items()}).items():
        a = np.ascontiguousarray(a)
        arrays["in_" + name] = a
        dr[name] = nc.dram_tensor("in_" + name, a.shape, mybir.dt.from_np(a.dtype), kind="ExternalInput").ap()
    out = nc.dram_tensor("out_0", (1, T, D), F32, kind="ExternalOutput").ap()
    build(nc, dr, out)
    return run(nc, [arrays], core_ids=[0]).results[0]["out_0"]
```

```python
from contextlib import ExitStack

import numpy as np
import concourse.bass as bass
from concourse import mybir
from concourse.alu_op_type import AluOpType as ALU

F32, F32R, U32, I32 = mybir.dt.float32, mybir.dt.float32r, mybir.dt.uint32, mybir.dt.int32
ACT = mybir.ActivationFunctionType
AX = mybir.AxisListType.X

P, T, D, KC = 128, 512, 1024, 8
NMEM = 256
FF = 2816
FC = FF // P
HH = 6
SLOT = 2048
DSLOT = 11 * P
EPS = 1e-6
NEG = -1e30
KCS = [0, 8, 24, 32]

S_Z0 = 0
S_M = S_Z0 + 6
S_Z0B = S_M + 4
S_O0 = S_Z0B + 7
S_U0 = S_O0 + 4
S_D0 = S_U0 + 22
S_Z1 = S_D0 + 16
S_UQ = S_Z1 + 4
S_UKV = S_UQ + 3
S_O1 = S_UKV + 3
S_U1 = S_O1 + 4
S_D1 = S_U1 + 22
S_QKV = S_D1 + 16
S_GC = S_QKV + 8
S_BC = S_GC + 4
S_A = S_BC + 2
S_GA = S_A + 8
S_BA = S_GA + 4
S_F = S_BA + 2
S_GF = S_F + 4
S_BF = S_GF + 4
S_O2 = S_BF + 2
NS = S_O2 + 4
NADA = 12

VEC = [("mix0", 8), ("mix1", 8), ("ffn0", 8), ("ffn1", 8), ("mem0", 8), ("mem1", 8),
       ("cw0", 132), ("cw1", 132), ("cb0", 44), ("cb1", 44), ("bin", 64), ("bada", 24), ("ng2", 8),
       ("fin", 8), ("wc2", 12), ("bc2", 4), ("cc", 16), ("lb", 18), ("hgo", 1), ("qa", 3), ("kva", 2),
       ("qnn", 1), ("qnr", 1), ("knn", 1), ("knr", 1), ("mq0", 1), ("mq1", 1), ("mk0", 1), ("mk1", 1)]
VOFF, _n = {}, 0
for _name, _c in VEC:
    VOFF[_name] = _n
    _n += _c
NV = _n

CON = [("ones", 128), ("ident", 128), ("b64", 128), ("rot", 128), ("causal", 128), ("winmask", 128),
       ("scan", 512), ("lvl", 448), ("inv", 1), ("e1", 1), ("e64", 1), ("e192", 1)]
COFF, _n = {}, 0
for _name, _c in CON:
    COFF[_name] = _n
    _n += _c
NC = _n

TWO_PI = 2 * np.pi
C1 = 6.28125
C2 = float(np.float32(TWO_PI - C1))
C3 = float(np.float32(TWO_PI - C1 - C2))
MAGIC = 12582912.0


class Chain:

    def __init__(self, eng, sem):
        self.eng, self.sem, self.n = eng, sem, 0

    def __call__(self, ins):
        self.n += 1
        ins.then_inc(self.sem, 1)
        self.eng.wait_ge(self.sem, self.n)


def build(nc, dr, out):
    KB = 1024
    base = 16512
    RAW, WHI, WLO, HR, XT, CONST, SCR, WORK = (base + KB * k for k in (0, 16, 32, 48, 80, 96, 106, 118))

    def at(name, off, shape, dt=F32):
        return nc.alloc_sbuf_tensor_at(name, shape, dt, offset=off)

    wraw = at("wraw", RAW, [P, 2, SLOT])
    whi = at("whi", WHI, [P, 2, SLOT], F32R)
    wlo = at("wlo", WLO, [P, 2, SLOT], F32R)
    hh = at("hh", HR, [P, KC, T], F32R)
    hl = at("hl", HR + 16 * KB, [P, KC, T], F32R)
    xT = at("xT", XT, [P, KC, T])
    con = at("con", CONST, [P, NC])
    vec = at("vec", CONST + 4 * ((NC + 7) // 8 * 8), [P, NV])
    so = CONST + 4 * ((NC + 7) // 8 * 8) + 4 * ((NV + 7) // 8 * 8)
    small = at("small", so, [P, 176])
    assert so + 176 * 4 <= SCR, so + 176 * 4 - SCR
    scr = at("scr", SCR, [P, 4, T])
    km1 = at("km1", SCR + 8 * KB, [P, 2, NMEM])
    vm1 = at("vm1", SCR + 10 * KB, [P, 2, NMEM])
    sqacc, rstd = scr[:, 0, :], scr[:, 1, :]
    tb = [scr[:, 2, :], scr[:, 3, :]]

    def w(name, kb, shape, dt=F32):
        return at(name, WORK + int(kb * KB), shape, dt)

    xtok = w("xtok", 0, [P, 4, D])
    ada = w("ada", 24, [P, 3, SLOT])
    arow = w("arow", 48, [P, 12, 256])
    mh = [w(f"mh{l}", 24 + 16 * l, [P, KC, NMEM], F32R) for l in range(2)]
    ml = [w(f"ml{l}", 32 + 16 * l, [P, KC, NMEM], F32R) for l in range(2)]
    memT = w("memT", 60, [P, KC, NMEM])
    msq = w("msq", 68, [P, 3, NMEM])
    mtok = w("mtok", 76, [P, 2, D])
    sqx = w("sqx", 76, [P, T])
    hq, hk, hb, hgate = (w(n, k, [P, HH, T]) for n, k in (("hq", 0), ("hk", 12), ("hb", 24), ("hgate", 36)))
    hv = w("hv", 48, [P, 4, HH * P])
    hA = w("hA", 60, [P, HH, T])
    qm0 = w("qm0", 72, [P, 2, T])
    km0 = w("km0", 84, [P, 2, NMEM])
    vm0 = w("vm0", 86, [P, 2, NMEM])
    hE = at("hE", HR, [P, HH, T])
    hKL = at("hKL", HR + 12 * KB, [P, HH, T])
    hQL = at("hQL", HR + 24 * KB, [P, HH, T // 2])
    hkT = w("hkT", 12, [P, HH, 3, P])
    hS = w("hS", 24, [P, 3, HH, P])
    gh = w("gh", 0, [P, FC, T], F32R)
    gl = w("gl", 44, [P, FC, T], F32R)
    pr0, pt0 = w("pr0", 0, [P, 3, T]), [w("pt00", 12, [P, 4, T]), w("pt01", 24, [P, 4, T])]
    z1 = w("z1", 0, [P, 8, T])
    mqn, mqr, mkn, mkr = (w("mqn", 16, [P, HH, T]), w("mqr", 28, [P, 3, T]), w("mkn", 34, [P, HH, T]),
                          w("mkr", 46, [P, 3, T]))
    mv = w("mv", 52, [P, 4, HH * P])
    cosT, sinT = w("cosT", 64, [P, T]), w("sinT", 66, [P, T])
    pr1, pt1 = w("pr1", 68, [P, 3, T]), [w("pt10", 0, [P, 4, T]), w("pt11", 74, [P, 4, T])]
    kr0 = w("kr0", 82, [P, T])
    rtmp = w("rtmp", 84, [P, 2, T])
    posi = w("posi", 68, [P, T], I32)
    posf = w("posf", 70, [P, 2, T])
    sqr = w("sqr", 0, [P, 2, T])
    wq, wk, wcz, wvr = (w(n, k, [P, 4, T]) for n, k in (("wq", 0), ("wk", 8), ("wcz", 16), ("wvr", 24)))
    vtok = w("vtok", 32, [P, 8, T])
    wkc, wvc, vct = w("wkc", 48, [P, 4, NMEM]), w("wvc", 52, [P, 4, NMEM]), w("vct", 56, [P, 2, T])
    wbias = w("wbias", 60, [P, 8, 8, 48])
    wbm = w("wbm", 72, [P, 4, NMEM])
    pr2 = w("pr2", 76, [P, 3, T])
    ptw = w("ptw", 24, [P, 4, 4, P])
    vtmp = w("vtmp", 76, [P, 2, D])
    ctok = w("ctok", 76, [P, 2, D])
    ctxT = w("ctxT", 48, [P, KC, NMEM])
    ch, cl = w("ch", 60, [P, KC, NMEM], F32R), w("cl", 68, [P, KC, NMEM], F32R)
    csq = w("csq", 84, [P, 3, NMEM])
    bh, bl = w("bh", 0, [P, 4, T], F32R), w("bl", 8, [P, 4, T], F32R)
    mm_ = w("mm_", 32, [P, KC, T])
    sig = w("sig", 48, [P, KC, T])
    atmp = w("atmp", 16, [P, 2, T])
    az = w("az", 20, [P, 2, T])
    acc2 = w("acc2", 24, [P, 2, T])
    btmp = w("btmp", 28, [P, 2, T])
    fu, fz = w("fu", 16, [P, 4, T]), w("fz", 24, [P, 4, T])
    xc = w("xc", 64, [P, 4, 4, 256])
    dft = w("dft", 48, [P, 8, T])
    dcc = w("dcc", 80, [P, 256])
    yT = w("yT", 0, [P, KC, T])
    ytok = w("ytok", 16, [P, 4, D])

    ps = nc.alloc_psum_tensor("ps", [P, 8, T], F32)

    def cc(name, a=0, n=None):
        return con[:, COFF[name] + a:COFF[name] + a + (n or dict(CON)[name])]

    def vv(name, j=0, n=1):
        return vec[:, VOFF[name] + j:VOFF[name] + j + n]

    nmx, sm, rc = small[:, 0:4], small[:, 4:8], small[:, 8:12]
    lbt, oml = small[:, 12:18], small[:, 18:24]
    lbx = small[:, 24:48]
    cs = small[:, 48:64]
    mod = small[:, 64:112]
    gsc = small[:, 112:128]

    with ExitStack() as ctx:
        def sem(name):
            return ctx.enter_context(nc.semaphore(name))

        raw_ready = [sem("raw_ready0"), sem("raw_ready1")]
        hi_ready, lo_ready = sem("hi_ready"), sem("lo_ready")
        used = sem("used")
        emptied = sem("emptied")
        x_in, v_in, c_in, m_in = sem("x_in"), sem("v_in"), sem("c_in"), sem("m_in")
        tr, ev = sem("tr"), sem("ev")
        sq_ready, sq_added, sum_ready, rstd_ready = sem("sq_ready"), sem("sq_added"), sem("sum_ready"), sem("rstd_ready")
        msq_ready, msq_added = sem("msq_ready"), sem("msq_added")
        t_ready, thi_ready, split_done = sem("t_ready"), sem("thi_ready"), sem("split_done")
        yn_ready, hn_sq, hn_mm, hn_rstd, hn_done = (sem(n) for n in ("yn_ready", "hn_sq", "hn_mm", "hn_rstd", "hn_done"))
        ch_act, ch_dve = sem("ch_act"), sem("ch_dve")
        f_acc, f_tap, f_conv, f_silu, f_g, f_hi, f_lo = (sem(n) for n in ("f_acc", "f_tap", "f_conv", "f_silu", "f_g", "f_hi", "f_lo"))
        g_act, g_dve = sem("g_act"), sem("g_dve")
        lv_d, lv_e, lv_k, lv_q, lv_mm, lv_cp = (sem(n) for n in ("lv_d", "lv_e", "lv_k", "lv_q", "lv_mm", "lv_cp"))
        st_k, st_tr, st_tc, st_kv, st_s = (sem(n) for n in ("st_k", "st_tr", "st_tc", "st_kv", "st_s"))
        ho_mm, ho_cp = sem("ho_mm"), sem("ho_cp")
        ada_in = [sem(f"ada_in{i}") for i in range(3)]
        ada_used, ada_cs, ada_row, ada_t, mod_ready = (sem(n) for n in ("ada_used", "ada_cs", "ada_row", "ada_t", "mod_ready"))
        sc_ready, mx_ready, ex_ready, pn_ready, tp_ready, pt_ready, pv_done, o_read = (
            sem(n) for n in ("sc_ready", "mx_ready", "ex_ready", "pn_ready", "tp_ready", "pt_ready", "pv_done", "o_read"))
        bm_ready = sem("bm_ready")
        pos_in, rp_d, rp_a, rot_mm, rot_rd, kq_ready = (sem(n) for n in ("pos_in", "rp_d", "rp_a", "rot_mm", "rot_rd", "kq_ready"))
        q_act, q_dve = sem("q_act"), sem("q_dve")
        ctx_in, b_in, dft_in = sem("ctx_in"), sem("b_in"), sem("dft_in")
        vt_c, vt_tr, vt_ev = sem("vt_c"), sem("vt_tr"), sem("vt_ev")
        df_mm, df_ev = sem("df_mm"), sem("df_ev")
        d1_done = sem("d1_done")
        y_tr, y_ev, out_done = sem("y_tr"), sem("y_ev"), sem("out_done")
        block = ctx.enter_context(nc.Block())


        Q_H0 = 0
        Q_MEM = Q_H0 + 8
        Q_Y0 = Q_MEM + 16
        Q_F0 = Q_Y0 + 8
        Q_H1 = Q_F0 + 8
        Q_C1 = Q_H1 + 8
        Q_Y1 = Q_C1 + 5
        Q_F1 = Q_Y1 + 8
        Q_H2 = Q_F1 + 8
        Q_CTX = Q_H2 + 8
        Q_BC = Q_CTX + 8
        Q_BA = Q_BC + 4
        Q_BF = Q_BA + 4
        Q_M2 = Q_BF + 4
        A_M0, A_MLA, A_M1, A_W = 0, 16, 40, 56
        G_M0, G_MLA, G_M1, G_W = 0, 2, 8, 10
        H_KM, H_HG, H_QM0, H_C1, H_Q1, H_K1, H_QM1 = 0, 2, 8, 10, 12, 18, 24
        HN_IN = [1, 1] + [1] * 6 + [1, 1] + [3, 2] + [2] * 6 + [2] * 6 + [1, 1]
        HN_AT = [sum(HN_IN[:i]) for i in range(len(HN_IN) + 1)]

        def sqbuf(i):
            return sqacc if i % 2 == 0 else sqx[:]

        def units(kind, layer=0):
            if kind == "mem":
                return [(2, h // 2, h % 2 == 1 and tt == 3) for h in range(4) for tt in range(4)]
            if kind == "mla":
                return [(i + 1, h, i == 3) for h in range(HH) for i in range(4)]
            return [(4, cb * 4 + h // 2, h % 2 == 1) for cb in range(4) for h in range(8)]

        @block.sync
        def _(sp):
            sp.dma_start(xtok[:], dr["x"].rearrange("a (t p) d -> p (a t) d", p=P)).then_inc(x_in, 16)

            def load(s, src):
                if s >= 2:
                    sp.wait_ge(lo_ready, s - 1)
                wd = src.shape[1]
                sp.dma_start(wraw[:, s % 2, 0:wd], src).then_inc(raw_ready[s % 2], 16)

            def load_many(s0, n, dram):
                wd = dram.shape[2]
                i0 = 0
                while s0 + i0 < 2 or (n - i0) % 2:
                    load(s0 + i0, dram[i0])
                    i0 += 1
                with sp.Fori(0, (n - i0) // 2) as i:
                    for u in range(2):
                        s = s0 + i0 + u
                        src = dram[bass.ds(2 * i + (i0 + u), 1), :, :].rearrange("a p n -> (a p) n")
                        sp.wait_ge(lo_ready, 2 * i + (s - 1))
                        sp.dma_start(wraw[:, s % 2, 0:wd], src).then_inc(raw_ready[s % 2], 16)

            load_many(0, S_O0, dr["w0"])
            for s0, dram in ((S_O0, "w0b"), (S_D0, "wd0"), (S_Z1, "w1"), (S_D1, "wd1"), (S_QKV, "w2")):
                load_many(s0, dr[dram].shape[0], dr[dram])
            for tt in range(4):
                sp.wait_ge(y_ev, 2 * tt + 2)
                sp.dma_start(out[0, tt * P:(tt + 1) * P, :], ytok[:, tt, :]).then_inc(out_done, 16)
            sp.wait_ge(out_done, 64)

        @block.tensor
        def _(pe):
            mm = nc.tensor.matmul

            def three(o, wsl, asl, K, moving_w=False):
                for k in range(K):
                    for n, (a, b) in enumerate(((0, 0), (0, 1), (1, 0))):
                        l, r = (wsl(a, k), asl(b, k)) if not moving_w else (asl(b, k), wsl(a, k))
                        last = mm(o, l, r, start=(k == 0 and n == 0), stop=(k == K - 1 and n == 2))
                return last

            def wv(par, cols, width=256, off=0, n=P):
                return lambda a, k: (whi, wlo)[a][:, par, k * cols + off:k * cols + off + n]

            def hv_(k0=0):
                return lambda a, k: (hh, hl)[a][:, k0 + k, :]

            def first_slot(S, q):
                pe.wait_ge(lo_ready, S + 1)
                for k in range(8):
                    pe.wait_ge(split_done, q + k + 1)
                    for b in range(2):
                        o, w_ = ps[:, 2 * (S % 2) + b, :], wv(S % 2, 256, off=b * P)
                        mm(o, w_(0, k), hh[:, k, :], start=(k == 0), stop=False)
                        mm(o, w_(0, k), hl[:, k, :], start=False, stop=False)
                        last = mm(o, w_(1, k), hh[:, k, :], start=False, stop=(k == 7))
                last.then_inc(used, 1)

            def slot_loop(S, n, body, lead=1, q=None):
                pe.wait_ge(emptied, S)
                i0 = n % 2
                if q is not None:
                    first_slot(S, q)
                    if not i0:
                        pe.wait_ge(lo_ready, S + 2)
                        body((S + 1) % 2).then_inc(used, 1)
                        i0 = 2
                elif i0:
                    pe.wait_ge(lo_ready, S + 1)
                    body(S % 2).then_inc(used, 1)
                m = (n - i0) // 2
                if m == 0:
                    return
                if m == 1:
                    for u in range(2):
                        s = S + i0 + u
                        pe.wait_ge(emptied, max(s - lead, S))
                        pe.wait_ge(lo_ready, s + 1)
                        body(s % 2).then_inc(used, 1)
                    return
                with pe.Fori(0, m) as i:
                    for u in range(2):
                        s = S + i0 + u
                        pe.wait_ge(emptied, 2 * i + (s - lead))
                        pe.wait_ge(lo_ready, 2 * i + (s + 1))
                        body(s % 2).then_inc(used, 1)

            def plain(par, act=None, K=8):
                a = act or hv_()
                for b in range(2):
                    last = three(ps[:, 2 * par + b, :], wv(par, 256, off=b * P), a, K)
                return last

            def ada_slot(a):
                b = 2 + a // 2 if a < 4 else 6 + a // 2 % 2
                if a >= 8:
                    pe.wait_ge(ada_row, a // 2 - 2)
                pe.wait_ge(ada_in[a % 3], 16 * (a // 3 + 1))
                for k in range(8):
                    last = mm(ps[0:2, b, a % 2 * 256:a % 2 * 256 + 256], cs[:, 2 * k:2 * k + 2],
                              ada[:, a % 3, k * 256:(k + 1) * 256], start=(k == 0), stop=(k == 7))
                last.then_inc(ada_used, 1)

            pe.wait_ge(ada_cs, 1)
            for a in range(3):
                ada_slot(a)
            pe.wait_ge(c_in, 16)
            pe.wait_ge(x_in, 16)
            for n in range(8):
                if n >= 2:
                    pe.wait_ge(ev, n - 1)
                for tt in range(4):
                    last = nc.tensor.transpose(ps[:, 4 + n % 2, tt * P:(tt + 1) * P], xtok[:, tt, n * P:(n + 1) * P], cc("ident"))
                last.then_inc(tr, 1)

            def norm_sum(n):
                pe.wait_ge(sq_added, 8 * n + 8)
                mm(ps[:, 7, :], cc("ones"), sqacc, start=True, stop=True).then_inc(sum_ready, 1)

            norm_sum(0)

            ada_slot(3)
            ada_slot(4)

            def mid_slot(s):
                if s:
                    pe.wait_ge(emptied, s - 1)
                pe.wait_ge(lo_ready, s + 1)
                plain(s % 2).then_inc(used, 1)

            first_slot(S_Z0, Q_H0)
            pe.wait_ge(m_in, 16)
            for n in range(4):
                pe.wait_ge(ev, 8 + n - 1)
                for j in range(4):
                    k, mt = 2 * n + j // 2, j % 2
                    last = nc.tensor.transpose(ps[:, 4 + n % 2, j * P:(j + 1) * P], mtok[:, mt, k * P:(k + 1) * P], cc("ident"))
                last.then_inc(tr, 1)
            for a in range(5, 8):
                ada_slot(a)
            pe.wait_ge(ada_row, 1)
            pe.wait_ge(lo_ready, 2)
            plain(1).then_inc(used, 1)
            pe.wait_ge(msq_added, 8)
            mm(ps[:, 4, 0:NMEM], cc("ones"), msq[:, 2, :], start=True, stop=True).then_inc(sum_ready, 1)
            ada_slot(8)
            ada_slot(9)
            mid_slot(2)
            ada_slot(10)
            ada_slot(11)
            mid_slot(3)
            pe.wait_ge(ada_row, 5)
            for n in range(24):
                last = nc.tensor.transpose(ps[:, 5, 2 * n:2 * n + 2], arow[0:2, n // 2, n % 2 * P:n % 2 * P + P], cc("ident")[0:2, 0:2])
            last.then_inc(ada_t, 1)
            mid_slot(4)
            mid_slot(5)

            def mem_proj(l):
                def act(a, k):
                    return (mh, ml)[a][l][:, k, :]
                s = S_M + 2 * l
                pe.wait_ge(split_done, Q_MEM + 8 * l + 8)
                pe.wait_ge(emptied, s - 1)
                pe.wait_ge(lo_ready, s + 1)
                for b in range(2):
                    last = three(ps[:, 2 * (s % 2), b * NMEM:(b + 1) * NMEM], wv(s % 2, 256, off=b * P), act, 8)
                last.then_inc(used, 1)
                s += 1
                pe.wait_ge(emptied, s - 1)
                pe.wait_ge(lo_ready, s + 1)
                for mt in range(2):
                    last = three(ps[:, 2 * (s % 2), mt * NMEM:(mt + 1) * NMEM], wv(s % 2, 256, n=256),
                                 lambda a, k: act(a, k)[:, mt * P:(mt + 1) * P], 8, moving_w=True)
                last.then_inc(used, 1)

            mem_proj(0)
            mem_proj(1)
            pe.wait_ge(mod_ready, 1)

            def hn_sums(r, mats):
                if r >= 2:
                    pe.wait_ge(hn_rstd, r - 1)
                for j, m in enumerate(mats):
                    i = HN_AT[r] + j
                    pe.wait_ge(hn_sq, i + 1)
                    lhs, rhs = m(i)
                    mm(ps[:, 4 + r % 2, :], lhs, rhs, start=(j == 0), stop=(j == len(mats) - 1)).then_inc(hn_mm, 1)

            def whole(name):
                return lambda i: (cc(name), sqbuf(i))

            for l in range(2):
                hn_sums(H_KM + l, [whole("b64")])

            def tok_major(par):
                for tt in range(4):
                    last = three(ps[:, 2 * par + tt // 2, (tt % 2) * 256:(tt % 2) * 256 + 256], wv(par, 256, n=256),
                                 lambda a, k: (hh, hl)[a][:, k, tt * P:(tt + 1) * P], 8, moving_w=True)
                return last
            slot_loop(S_Z0B, 3, tok_major)
            slot_loop(S_Z0B + 3, 4, plain)

            for hf in range(2):
                pe.wait_ge(g_dve, 3)
                if hf == 0:
                    pe.wait_ge(emptied, S_O0)
                for h in range(3 * hf, 3 * hf + 3):
                    for c in range(4):
                        last = mm(ps[:, h, c * P:(c + 1) * P], hk[:, h, c * P:(c + 1) * P], hq[:, h, c * P:(c + 1) * P],
                                  start=True, stop=True)
                last.then_inc(lv_mm, 1)
            for j in range(14):
                hf, l = j % 2, j // 2
                pe.wait_ge(lv_k, j + 1)
                pe.wait_ge(lv_q, j + 1)
                pe.wait_ge(lv_cp, j + 1)
                for h3 in range(3):
                    h = 3 * hf + h3
                    for c in range(4):
                        o = h3 * 256 + c * 64
                        last = mm(ps[:, 3 * hf + o // 512, o % 512:o % 512 + 64], hKL[:, h, c * P:(c + 1) * P],
                                  hQL[:, h, c * 64:(c + 1) * 64], start=True, stop=True)
                last.then_inc(lv_mm, 1)
            pe.wait_ge(st_k, 1)
            pe.wait_ge(lv_cp, 16)
            for n in range(HH):
                if n >= 2:
                    pe.wait_ge(st_tc, n - 1)
                for c in range(3):
                    last = nc.tensor.transpose(ps[:, n % 2, c * P:(c + 1) * P], hKL[:, n, c * P:(c + 1) * P], cc("ident"))
                last.then_inc(st_tr, 1)
            for n in range(HH):
                pe.wait_ge(st_tc, n + 1)
                if n >= 2:
                    pe.wait_ge(st_s, n - 1)
                for c in range(3):
                    last = mm(ps[:, 2 + n % 2, c * P:(c + 1) * P], hkT[:, n, c, :], hv[:, c, n * P:(n + 1) * P],
                              start=True, stop=True)
                last.then_inc(st_kv, 1)
            for h in range(HH):
                pe.wait_ge(st_s, HH)
                if h >= 2:
                    pe.wait_ge(ho_cp, h - 1)
                for c in range(4):
                    t = slice(c * P, (c + 1) * P)
                    last = mm(ps[:, h % 2, t], hv[:, c, h * P:(h + 1) * P], hA[:, h, t], start=True, stop=(c == 0))
                    if c:
                        last = mm(ps[:, h % 2, t], hS[:, c - 1, h, :], hq[:, h, t], start=False, stop=True)
                last.then_inc(ho_mm, 1)
                if h >= 1:
                    hn_sums(H_HG + h - 1, [whole("ones")])
            hn_sums(H_HG + 5, [whole("ones")])
            for j in range(2):
                hn_sums(H_QM0 + j, [whole("b64")])

            def attention(kind, U0, G0, scores, pv, ready=None):
                us = units(kind)
                for n in range(len(us) + 3):
                    if n < len(us):
                        u = U0 + n
                        if n < 3:
                            if n == 0 and ready:
                                ready()
                        if u >= 3:
                            pe.wait_ge(ex_ready, u - 2)
                        scores(n, 4 + u % 3).then_inc(sc_ready, 1)
                    if 2 <= n < len(us) + 2:
                        u = U0 + n - 2
                        pe.wait_ge(pn_ready, u + 1)
                        if u >= 2:
                            pe.wait_ge(pt_ready, u - 1)
                        b = (7, 3)[u % 2]
                        for j in range(us[n - 2][0]):
                            last = nc.tensor.transpose(ps[:, b, j * P:(j + 1) * P], prs[kind][:, u % 3, j * P:(j + 1) * P], cc("ident"))
                        last.then_inc(tp_ready, 1)
                    if n >= 3 and us[n - 3][2]:
                        g = G0 + us[n - 3][1]
                        pe.wait_ge(pt_ready, U0 + n - 2)
                        if g >= 2:
                            pe.wait_ge(*OREAD[g - 2])
                        pv(us[n - 3][1], g % 2).then_inc(pv_done, 1)

            OREAD = [(t_ready, q + 1) for q in (*range(Q_Y0 + 6, Q_Y0 + 8), *range(Q_Y1, Q_Y1 + 8))] + [(o_read, n + 1) for n in range(16)]
            prs = {"mem": pr0, "mla": pr1, "win": pr2}

            def mem_attention(l, q, kmm, vmm):
                def scores(n, b):
                    h, tt = n // 4, n % 4
                    r = slice(64 * (h % 2), 64 * (h % 2) + 64)
                    return mm(ps[:, b, 0:NMEM], q[r, h // 2, tt * P:(tt + 1) * P], kmm[r, h // 2, :], start=True, stop=True)

                def pv(g, b):
                    for h in (2 * g, 2 * g + 1):
                        for c in range(2):
                            last = mm(ps[64 * (h % 2):64 * (h % 2) + 64, b, :], vmm[:, c, h * 64:(h + 1) * 64],
                                      pts[l][h % 2][:, c, :], start=(c == 0), stop=(c == 1))
                    return last
                prs["mem"] = (pr0, pr1)[l]
                r = (H_QM0, H_QM1)[l]
                attention("mem", (A_M0, A_M1)[l], (G_M0, G_M1)[l], scores, pv, lambda: pe.wait_ge(hn_done, r + 2))

            pts = [pt0, pt1]
            mem_attention(0, qm0, km0, vm0)
            slot_loop(S_O0, 4, plain, q=Q_Y0)
            norm_sum(1)

            def ffn(S_U, S_D, q, layer):
                slot_loop(S_U, 22, plain, q=q)
                pe.wait_ge(f_lo, 22 * layer + 22)
                pe.wait_ge(emptied, S_D)
                with pe.Fori(0, 4) as i:
                    for n in range(2):
                        s = S_D + 2 * n
                        pe.wait_ge(emptied, 4 * i + (s - 2))
                        for hf in range(2):
                            pe.wait_ge(lo_ready, 4 * i + (s + hf + 1))
                            par = (s + hf) % 2
                            for k in range(11):
                                for m, (a, b) in enumerate(((0, 0), (0, 1), (1, 0))):
                                    last = mm(ps[:, n, :], (whi, wlo)[a][:, par, k * P:(k + 1) * P],
                                              (gh, gl)[b][:, 11 * hf + k, :],
                                              start=(hf == 0 and k == 0 and m == 0), stop=(hf == 1 and k == 10 and m == 2))
                            last.then_inc(used, 1)

            ffn(S_U0, S_D0, Q_F0, 0)
            norm_sum(2)

            slot_loop(S_Z1, 4, plain, q=Q_H1)
            hn_sums(H_C1, [whole("ones")] * 3)
            hn_sums(H_C1 + 1, [whole("ones")] * 2)
            pe.wait_ge(split_done, Q_C1 + 3)

            def uq(par):
                for b in range(3):
                    last = three(ps[:, b, :], wv(par, 384, off=b * P), hv_(), 3)
                return last
            slot_loop(S_UQ, 3, uq, lead=0)
            pe.wait_ge(split_done, Q_C1 + 5)

            def ukv(par):
                for b in range(2):
                    three(ps[:, b, :], wv(par, 512, off=b * P), hv_(3), 2)
                for tt in range(4):
                    last = three(ps[:, 2 + tt // 2, (tt % 2) * 256:(tt % 2) * 256 + 256], wv(par, 512, off=256, n=256),
                                 lambda a, k: (hh, hl)[a][:, 3 + k, tt * P:(tt + 1) * P], 2, moving_w=True)
                return last
            slot_loop(S_UKV, 3, ukv, lead=0)
            def half(h, rhs):
                r = slice(64 * (h % 2), 64 * (h % 2) + 64)
                return lambda i: (con[r, COFF["ones"]:COFF["ones"] + P], rhs[r, :])
            for h in range(HH):
                hn_sums(H_Q1 + h, [whole("ones"), half(h, sqr[:, 0, :])])
                if h % 2 == 1:
                    pe.wait_ge(hn_done, H_Q1 + h + 1)
                    if h > 1:
                        pe.wait_ge(rot_rd, h // 2)
                    mm(ps[:, 6, :], cc("rot"), mqr[:, h // 2, :], start=True, stop=True).then_inc(rot_mm, 1)
            pe.wait_ge(kq_ready, 1)
            pe.wait_ge(rot_rd, 3)
            mm(ps[:, 6, :], cc("rot"), z1[:, 5, :], start=True, stop=True).then_inc(rot_mm, 1)
            for h in range(HH):
                hn_sums(H_K1 + h, [whole("ones"), half(0, sqr[:, 1, :])])
            for j in range(2):
                hn_sums(H_QM1 + j, [whole("b64")])

            def mla_scores(n, b):
                h, i = n // 4, n % 4
                r = slice(64 * (h % 2), 64 * (h % 2) + 64)
                wd = (i + 1) * P
                t = slice(i * P, (i + 1) * P)
                mm(ps[:, b, 0:wd], mqn[:, h, t], mkn[:, h, 0:wd], start=True, stop=False)
                mm(ps[:, b, wd - P:wd], cc("ident"), cc("causal"), start=False, stop=False)
                return mm(ps[:, b, 0:wd], mqr[r, h // 2, t], mkr[r, h // 2, 0:wd], start=False, stop=True)

            def mla_pv(h, b):
                for i in range(4):
                    t = slice(i * P, (i + 1) * P)
                    for j in range(i + 1):
                        last = mm(ps[:, b, t], mv[:, j, h * P:(h + 1) * P], pt1[h % 2][:, j, t], start=(j == 0), stop=(j == i))
                return last

            attention("mla", A_MLA, G_MLA, mla_scores, mla_pv, lambda: pe.wait_ge(hn_done, H_QM1 + 2))
            mem_attention(1, z1[:, 6:8, :], km1, vm1)
            slot_loop(S_O1, 4, plain, q=Q_Y1)
            norm_sum(3)
            ffn(S_U1, S_D1, Q_F1, 1)
            norm_sum(4)

            def ctx_tr(n):
                if n >= 2:
                    pe.wait_ge(ev, 12 + n - 1)
                for j in range(4):
                    k, mt = 2 * n + j // 2, j % 2
                    last = nc.tensor.transpose(ps[:, 4 + n % 2, j * P:(j + 1) * P], ctok[:, mt, k * P:(k + 1) * P], cc("ident"))
                last.then_inc(tr, 1)

            pe.wait_ge(ctx_in, 16)
            ctx_tr(0)
            ctx_tr(1)
            slot_loop(S_QKV, 2, plain, q=Q_H2)
            ctx_tr(2)
            ctx_tr(3)
            pe.wait_ge(lo_ready, S_QKV + 3)
            pe.wait_ge(emptied, S_QKV + 1)
            plain(S_QKV % 2).then_inc(used, 1)
            pe.wait_ge(msq_added, 16)
            mm(ps[:, 6, 0:NMEM], cc("ones"), csq[:, 2, :], start=True, stop=True).then_inc(sum_ready, 1)
            pe.wait_ge(lo_ready, S_QKV + 4)
            pe.wait_ge(emptied, S_QKV + 2)
            plain((S_QKV + 1) % 2).then_inc(used, 1)
            pe.wait_ge(split_done, Q_CTX + 8)

            def kv(par):
                for b in range(2):
                    three(ps[:, 4 + par, b * NMEM:(b + 1) * NMEM], wv(par, 256, off=b * P),
                          lambda a, k: (ch, cl)[a][:, k, :], 8)
                return plain(par)
            slot_loop(S_QKV + 4, 2, kv)
            for u in range(2):
                s = S_QKV + 6 + u
                pe.wait_ge(emptied, s - 1)
                pe.wait_ge(lo_ready, s + 1)
                kv(s % 2).then_inc(used, 1)
                for j in (2 * u, 2 * u + 1):
                    pe.wait_ge(vt_c, j + 1)
                    for q in range(3):
                        n = 3 * j + q
                        if n >= 2:
                            pe.wait_ge(vt_ev, n - 1)
                        for i in range(4 if q < 2 else 2):
                            src = vtmp[:, j % 2, (4 * q + i) * P:(4 * q + i + 1) * P] if q < 2 else wvc[:, j, i * P:(i + 1) * P]
                            last = nc.tensor.transpose(ps[:, 6 + n % 2, i * P:(i + 1) * P], src, cc("ident"))
                        last.then_inc(vt_tr, 1)

            def win_scores(n, b):
                cb, h = n // 8, n % 8
                r = slice(64 * (h % 2), 64 * (h % 2) + 64)
                q = wq[r, h // 2, cb * P:(cb + 1) * P]
                ks = wk[r, h // 2, :].rearrange("p (r c) -> p r c", c=64)[:, :, KCS[cb]:KCS[cb] + 32]
                mm(ps[:, b, 0:256].rearrange("p (r c) -> p r c", c=32), q, ks, start=True, stop=True)
                return mm(ps[:, b, 256:512], q, wkc[r, h // 2, :], start=True, stop=True)

            def win_pv(g, b):
                cb, hp = g // 4, g % 4
                for h in (2 * hp, 2 * hp + 1):
                    u = A_W + cb * 8 + h
                    for c in range(4):
                        v = vtok[:, 2 * cb + c, h * 64:(h + 1) * 64] if c < 2 else vct[:, c - 2, h * 64:(h + 1) * 64]
                        last = mm(ps[64 * (h % 2):64 * (h % 2) + 64, b, 0:P], v, ptw[:, u % 4, c, :],
                                  start=(c == 0), stop=(c == 3))
                return last

            def win_ready():
                pe.wait_ge(vt_ev, 12)
                pe.wait_ge(emptied, S_GC)

            attention("win", A_W, G_W, win_scores, win_pv, win_ready)
            pe.wait_ge(o_read, 16)
            slot_loop(S_GC, 4, plain)

            def branch(S, q):
                pe.wait_ge(split_done, q + 4)
                for s in (S, S + 1):
                    pe.wait_ge(emptied, max(S, s - 1))
                    pe.wait_ge(lo_ready, s + 1)
                    for b in range(4):
                        last = three(ps[:, 4 * (s % 2) + b, :], wv(s % 2, 512, off=b * P),
                                     lambda a, k: (bh, bl)[a][:, k, :], 4)
                    last.then_inc(used, 1)
            branch(S_BC, Q_BC)
            slot_loop(S_A, 8, plain)
            slot_loop(S_GA, 4, plain)
            branch(S_BA, Q_BA)
            slot_loop(S_F, 4, plain)
            pe.wait_ge(emptied, S_GF)
            pe.wait_ge(dft_in, 32)
            for n in range(8):
                g, q = n // 2, n % 2
                if n >= 2:
                    pe.wait_ge(df_ev, n - 1)
                for i in range(2):
                    tt = 2 * q + i
                    last = mm(ps[:, 4 + n % 2, i * 256:(i + 1) * 256], fu[:, g, tt * P:(tt + 1) * P], dcc[:], start=True, stop=True)
                last.then_inc(df_mm, 1)
            for g in range(4):
                pe.wait_ge(df_ev, 8)
                if g >= 2:
                    pe.wait_ge(t_ready, Q_BF + g - 1)
                for tt in range(4):
                    for i in range(2):
                        last = mm(ps[:, 6 + g % 2, :], xc[:, tt, g, i * P:(i + 1) * P], dft[:, 4 * i + tt, :],
                                  start=(tt == 0 and i == 0), stop=(tt == 3 and i == 1))
                last.then_inc(df_mm, 1)
            slot_loop(S_GF, 4, plain)
            branch(S_BF, Q_BF)
            slot_loop(S_O2, 4, plain, q=Q_M2)
            norm_sum(5)
            pe.wait_ge(yn_ready, 1)
            for n in range(8):
                tt, q = n // 2, n % 2
                if n >= 2:
                    pe.wait_ge(y_ev, n - 1)
                for i in range(4):
                    k = 4 * q + i
                    last = nc.tensor.transpose(ps[:, n % 2, i * P:(i + 1) * P], yT[:, k, tt * P:(tt + 1) * P], cc("ident"))
                last.then_inc(y_tr, 1)

        @block.gpsimd
        def _(pool):
            def lo(s, i=None):
                n = s + 1 if i is None else 2 * i + (s + 1)
                pool.wait_ge(hi_ready, n)
                nc.gpsimd.tensor_tensor(wlo[:, s % 2, :], wraw[:, s % 2, :], whi[:, s % 2, :].bitcast(F32),
                                        ALU.subtract).then_inc(lo_ready, 1)

            def lo_many(s0, n):
                if n % 2:
                    lo(s0)
                s0 += n % 2
                if n < 2:
                    return
                with pool.Fori(0, n // 2) as i:
                    for u in range(2):
                        lo(s0 + u, i)

            lo_many(0, S_O0)
            lo(S_O0)
            lo(S_O0 + 1)
            for j in range(14):
                hf = j % 2
                pool.wait_ge(lv_e, j + 1)
                if j >= 2:
                    pool.wait_ge(lv_mm, j + 1)
                nc.gpsimd.tensor_tensor(hKL[:, 3 * hf:3 * hf + 3, :], hk[:, 3 * hf:3 * hf + 3, :],
                                        hE[:, 3 * hf:3 * hf + 3, :], ALU.mult).then_inc(lv_k, 1)
            lo_many(S_O0 + 2, S_GC - S_O0 - 2)
            for n in range(32):
                cb, h = n // 8, n % 8
                if n == 0:
                    pool.wait_ge(b_in, 128)
                if n >= 4:
                    pool.wait_ge(mx_ready, A_W + n - 3)
                off = (0, -8, -8, -16)[cb] + 16
                nc.gpsimd.tensor_tensor(wbm[:, n % 4, :].rearrange("p (r c) -> p r c", c=32), wbias[:, :, h, off:off + 32],
                                        cc("winmask", 32 * cb, 32).unsqueeze(1).to_broadcast([P, 8, 32]),
                                        ALU.add).then_inc(bm_ready, 1)
            lo_many(S_GC, NS - S_GC)

        @block.scalar
        def _(act):
            A = nc.scalar.activation
            link = Chain(act, ch_act)
            state = {"conv": 0, "q": 0, "ada": False}

            act.dma_start(vec[:], dr["vec"]).then_inc(v_in, 16)
            act.dma_start(con[:], dr["con"]).then_inc(c_in, 16)

            def load_ada(a):
                if a >= 3:
                    act.wait_ge(ada_used, a - 2)
                act.dma_start(ada[:, a % 3, :], dr["wada"][a]).then_inc(ada_in[a % 3], 16)

            for a in range(3):
                load_ada(a)
            act.dma_start(mtok[:], dr["mem"].rearrange("a (t p) d -> p (a t) d", p=P)).then_inc(m_in, 16)

            def conv(s, i=None, step=2):
                k = 0 if i is None else i
                h = step // 2
                if s >= 2 or i is not None:
                    act.wait_ge(used, k * step + (s - 1))
                act.wait_ge(raw_ready[s % 2], k * (16 * h) + 16 * (s // 2 + 1))
                A(whi[:, s % 2, :], wraw[:, s % 2, :], ACT.Copy).then_inc(hi_ready, 1)

            def conv_upto(n):
                while state["conv"] <= min(n, NS - 1):
                    conv(state["conv"])
                    state["conv"] += 1

            def hi(dst, src=None, wd=T):
                q = state["q"]
                act.wait_ge(t_ready, q + 1)
                A(dst, (src if src is not None else tb[q % 2])[:, 0:wd], ACT.Copy).then_inc(thi_ready, 1)
                state["q"] += 1

            def squares(n, wait, ks=range(8)):
                for k in ks:
                    wait(k)
                    i = 8 * n + k
                    if i >= 2:
                        act.wait_ge(sq_added, i - 1)
                    A(tb[k % 2], xT[:, k, :], ACT.Square).then_inc(sq_ready, 1)

            def rnorm(i, src, dst, scale, eps):
                act.wait_ge(sum_ready, i + 1)
                link(A(dst, src, ACT.Ln, bias=eps, scale=scale))
                A(dst, dst, ACT.Exp, scale=-0.5).then_inc(rstd_ready, 1)

            act.wait_ge(v_in, 16)
            A(cs, vv("cc", 0, 16), ACT.Silu).then_inc(ada_cs, 1)
            nc.scalar.preload_act_table_set("natural_log_exp_and_others")
            load_ada(3)
            load_ada(4)
            act.wait_ge(c_in, 16)
            squares(0, lambda k: act.wait_ge(ev, k + 1), range(4))
            conv_upto(0)
            squares(0, lambda k: act.wait_ge(ev, k + 1), range(4, 8))
            rnorm(0, ps[:, 7, :], rstd, 1.0 / D, cc("e1"))
            load_ada(5)
            for k in range(8):
                hi(hh[:, k, :])
            conv_upto(1)
            load_ada(6)
            load_ada(7)
            conv_upto(2)
            for n in range(8):
                act.wait_ge(ev, 8 + n // 2 + 1)
                if n >= 2:
                    act.wait_ge(msq_added, n - 1)
                A(msq[:, n % 2, :], memT[:, n, :], ACT.Square).then_inc(msq_ready, 1)
            load_ada(8)
            load_ada(9)
            load_ada(10)
            conv_upto(3)
            rnorm(1, ps[:, 4, 0:NMEM], msq[:, 2, :], 1.0 / D, cc("e1"))
            load_ada(11)
            conv_upto(4)
            conv_upto(5)
            for l in range(2):
                for k in range(8):
                    hi(mh[l][:, k, :], wd=NMEM)
                conv_upto(6 + l)

            def hn_sq_(r, tiles):
                for j, (wait, x) in enumerate(tiles):
                    i = HN_AT[r] + j
                    if wait:
                        wait()
                    if i >= 2:
                        act.wait_ge(hn_mm, i - 1)
                    A(sqbuf(i), x, ACT.Square).then_inc(hn_sq, 1)

            def hn_ln(r, scale, eps):
                act.wait_ge(hn_mm, HN_AT[r + 1])
                if r >= 1:
                    act.wait_ge(hn_done, r)
                link(A(rstd, ps[:, 4 + r % 2, :], ACT.Ln, bias=eps, scale=scale))
                A(rstd, rstd, ACT.Exp, scale=-0.5).then_inc(hn_rstd, 1)

            for l in range(2):
                conv_upto(S_M + 2 * l + 2)
                hn_sq_(H_KM + l, [(lambda: act.wait_ge(emptied, S_M + 2 * l + 1), (km0, km1)[l][:].rearrange("p a b -> p (a b)"))])
                conv_upto(S_M + 2 * l + 3)
            for l in range(2):
                hn_ln(H_KM + l, 1.0 / 64, cc("e1"))
            conv_upto(S_Z0B + 2)
            A(hq[:], hq[:], ACT.Silu).then_inc(g_act, 1)
            conv_upto(S_Z0B + 3)
            A(hk[:], hk[:], ACT.Sigmoid).then_inc(g_act, 1)
            nc.scalar.preload_act_table_set("natural_log_exp_and_others")
            conv_upto(S_Z0B + 4)
            act.wait_ge(g_dve, 1)
            A(lbx[:, 0:18], lbx[:, 0:18], ACT.Exp).then_inc(g_act, 1)
            conv_upto(S_Z0B + 5)
            act.wait_ge(g_dve, 2)
            A(hA[:], hb[:], ACT.Ln).then_inc(g_act, 1)
            conv_upto(S_Z0B + 6)
            conv_upto(S_O0)
            act.wait_ge(emptied, S_Z0B + 6)
            A(hgate[:], hgate[:], ACT.Silu).then_inc(g_act, 1)
            nc.scalar.preload_act_table_set("natural_log_exp_and_others")
            conv_upto(S_O0 + 1)
            for j in range(14):
                hf = j % 2
                act.wait_ge(lv_d, j + 1)
                A(hE[:, 3 * hf:3 * hf + 3, :], hE[:, 3 * hf:3 * hf + 3, :], ACT.Exp).then_inc(lv_e, 1)
            act.wait_ge(lv_d, 15)
            A(hE[:], hE[:], ACT.Exp).then_inc(lv_e, 1)
            act.wait_ge(st_k, 1)
            A(hE[:], hb[:], ACT.Exp).then_inc(lv_e, 1)
            for n in range(HH):
                act.wait_ge(st_tr, n + 1)
                A(hkT[:, n, :, :], ps[:, n % 2, 0:3 * P].rearrange("p (c k) -> p c k", k=P), ACT.Copy).then_inc(st_tc, 1)
            for h in range(HH):
                hn_sq_(H_HG + h, [(lambda: act.wait_ge(ho_cp, h + 1), hA[:, h, :])])
                hn_ln(H_HG + h, 1.0 / P, cc("e1"))
                if h >= 1:
                    hi(hh[:, h - 1, :])
            hi(hh[:, 5, :])
            for j in range(2):
                hn_sq_(H_QM0 + j, [(None, qm0[:, j, :])])
                hn_ln(H_QM0 + j, 1.0, cc("e64"))

            def attention(kind, U0, G0, prb, evac, pvbuf, chunk=None):
                us = units(kind)
                for n in range(len(us) + 4):
                    if n < len(us):
                        u = U0 + n
                        wd = us[n][0] * P
                        act.wait_ge(mx_ready, u + 1)
                        if u >= 3:
                            act.wait_ge(tp_ready, u - 2)
                        A(prb[:, u % 3, 0:wd], ps[:, 4 + u % 3, 0:wd], ACT.Exp, bias=nmx[:, u % 4:u % 4 + 1],
                          accum_out=sm[:, u % 4:u % 4 + 1]).then_inc(ex_ready, 1)
                    if 2 <= n < len(us) + 2:
                        m = n - 2
                        u = U0 + m
                        act.wait_ge(tp_ready, u + 1)
                        w_ = pvbuf(m)
                        if w_:
                            act.wait_ge(pv_done, w_)
                        dst, src = evac(m, ps[:, (7, 3)[u % 2], :])
                        A(dst, src, ACT.Copy).then_inc(pt_ready, 1)
                    if chunk is not None and n >= 4 and us[n - 4][2]:
                        hi(hh[:, chunk + us[n - 4][1], :])

            def mem_att(l):
                def evac(m, b):
                    h, tt = m // 4, m % 4
                    return (pt0, pt1)[l][h % 2][:, 0:2, tt * P:(tt + 1) * P], b[:, 0:256].rearrange("p (c t) -> p c t", t=P)
                G = (G_M0, G_M1)[l]
                attention("mem", (A_M0, A_M1)[l], G, (pr0, pr1)[l], evac, lambda m: G + 1 if m >= 8 else G, 6)

            mem_att(0)

            def out_proj(S, n):
                conv_upto(S + 1)
                conv_upto(S + 2)
                for j in range(4):
                    conv_upto(S + j + 1)
                    act.wait_ge(emptied, S + j + 1)
                    for k in (2 * j, 2 * j + 1):
                        i = 8 * n + k
                        act.wait_ge(sq_added, i - 1)
                        A(tb[k % 2], xT[:, k, :], ACT.Square).then_inc(sq_ready, 1)

            out_proj(S_O0, 1)
            nc.scalar.preload_act_table_set("natural_log_exp_and_others")
            rnorm(2, ps[:, 7, :], rstd, 1.0 / D, cc("e1"))
            for k in range(8):
                hi(hh[:, k, :])

            def ffn_up(S, layer):
                cw, cb = VOFF[f"cw{layer}"], VOFF[f"cb{layer}"]
                b0 = 22 * layer
                conv_upto(S + 1)
                with act.Fori(0, 11) as i:
                    for u in range(2):
                        s = S + u
                        par = s % 2
                        conv(s + 2, i)
                        act.wait_ge(f_lo, 2 * i + b0)
                        for ab in range(2):
                            col = cb + 22 * ab + u
                            wc = cw + 88 + 22 * ab + u
                            A(scr[:, 2 * u + ab, :], ps[:, 2 * par + ab, :], ACT.Identity, bias=vec[:, bass.ds(2 * i + col, 1)],
                              scale=vec[:, bass.ds(2 * i + wc, 1)]).then_inc(f_acc, 1)
                        act.wait_ge(f_conv, 2 * i + (b0 + u + 1))
                        A(scr[:, 2 * u, :], scr[:, 2 * u, :], ACT.Silu).then_inc(f_silu, 1)
                        act.wait_ge(f_g, 2 * i + (b0 + u + 1))
                        A(gh[:].rearrange("p c t -> p (c t)")[:, bass.ds((2 * i + u) * T, T)], scr[:, 2 * u, :],
                          ACT.Copy).then_inc(f_hi, 1)
                state["conv"] = S + 24

            def ffn_down(S, n):
                for k in range(8):
                    for j in (1, 2):
                        conv_upto(S + 2 * k + j)
                    act.wait_ge(emptied, S + 2 * k + 2)
                    i = 8 * n + k
                    act.wait_ge(sq_added, i - 1)
                    A(tb[k % 2], xT[:, k, :], ACT.Square).then_inc(sq_ready, 1)

            ffn_up(S_U0, 0)
            ffn_down(S_D0, 2)
            act.wait_ge(used, S_Z1)
            act.dma_start(posi[:], bass.AP(tensor=dr["pos"].tensor, offset=0, ap=[[0, P], [1, T]])).then_inc(pos_in, 16)
            nc.scalar.preload_act_table_set("natural_log_exp_and_others")
            rnorm(3, ps[:, 7, :], rstd, 1.0 / D, cc("e1"))
            for k in range(8):
                hi(hh[:, k, :])
            conv_upto(S_Z1 + 1)
            for j, dst in enumerate((sinT, cosT)):
                act.wait_ge(rp_d, j + 1)
                A(dst[:], posf[:, j, :], ACT.Sin).then_inc(rp_a, 1)
            nc.scalar.preload_act_table_set("natural_log_exp_and_others")
            for s in range(S_Z1 + 1, S_UQ + 1):
                conv_upto(s)
            hn_sq_(H_C1, [(lambda j=j: act.wait_ge(emptied, S_Z1 + j // 2 + 1), z1[:, j, :]) for j in range(3)])
            hn_sq_(H_C1 + 1, [(lambda j=j: act.wait_ge(emptied, S_Z1 + 3), z1[:, 3 + j, :]) for j in range(2)])
            hn_ln(H_C1, 1.0 / 384, cc("e1"))
            for j in range(3):
                hi(hh[:, j, :])
            hn_ln(H_C1 + 1, 1.0 / 256, cc("e1"))
            for j in range(3, 5):
                hi(hh[:, j, :])
            for s in range(S_UQ, S_O1 + 1):
                conv_upto(s)
            conv_upto(S_O1 + 1)
            act.wait_ge(emptied, S_O1)
            act.wait_ge(split_done, Q_C1 + 5)
            for h in range(HH):
                hn_sq_(H_Q1 + h, [(None, mqn[:, h, :])])
                r = slice(64 * (h % 2), 64 * (h % 2) + 64)
                act.wait_ge(hn_mm, HN_AT[H_Q1 + h])
                A(sqr[r, 0, :], mqr[r, h // 2, :], ACT.Square).then_inc(hn_sq, 1)
                hn_ln(H_Q1 + h, 1.0, cc("e192"))
            for h in range(HH):
                hn_sq_(H_K1 + h, [(None, mkn[:, h, :])])
                act.wait_ge(hn_mm, HN_AT[H_K1 + h])
                A(sqr[0:64, 1, :], posf[0:64, 0, :], ACT.Square).then_inc(hn_sq, 1)
                hn_ln(H_K1 + h, 1.0 / 192, cc("e1"))
            for j in range(2):
                hn_sq_(H_QM1 + j, [(None, z1[:, 6 + j, :])])
                hn_ln(H_QM1 + j, 1.0, cc("e64"))

            def mla_evac(m, b):
                h, i = m // 4, m % 4
                n = i + 1
                return pt1[h % 2][:, 0:n, i * P:(i + 1) * P], b[:, 0:n * P].rearrange("p (c t) -> p c t", t=P)
            act.wait_ge(hn_done, H_QM1 + 2)
            attention("mla", A_MLA, G_MLA, pr1, mla_evac, lambda m: G_MLA + m // 4 - 1 if m >= 8 else G_MLA, 0)
            act.wait_ge(pv_done, G_MLA + 6)
            mem_att(1)
            out_proj(S_O1, 3)
            rnorm(4, ps[:, 7, :], rstd, 1.0 / D, cc("e1"))
            for k in range(8):
                hi(hh[:, k, :])
            ffn_up(S_U1, 1)
            ffn_down(S_D1, 4)

            nc.scalar.preload_act_table_set("natural_log_exp_and_others")
            act.wait_ge(used, S_QKV)
            act.dma_start(ctok[:], dr["ctx"].rearrange("a (t p) d -> p (a t) d", p=P)).then_inc(ctx_in, 16)
            rnorm(5, ps[:, 7, :], rstd, 1.0 / D, cc("e1"))
            for k in range(8):
                hi(hh[:, k, :])
            def ctx_squares(half):
                for n in range(4 * half, 4 * half + 4):
                    act.wait_ge(ev, 12 + n // 2 + 1)
                    act.wait_ge(msq_added, 8 + n - 1)
                    A(csq[:, n % 2, :], ctxT[:, n, :], ACT.Square).then_inc(msq_ready, 1)
            conv_upto(S_QKV + 1)
            ctx_squares(0)
            conv_upto(S_QKV + 2)
            conv_upto(S_QKV + 3)
            ctx_squares(1)
            conv_upto(S_QKV + 4)
            rnorm(6, ps[:, 6, 0:NMEM], csq[:, 2, :], 1.0 / D, cc("e1"))
            for k in range(8):
                hi(ch[:, k, :], wd=NMEM)
            for s in range(S_QKV + 5, S_QKV + 8):
                conv_upto(s)
            act.wait_ge(emptied, S_QKV + 6)
            for j in range(4):
                if j >= 2:
                    conv_upto(S_QKV + 8)
                    act.wait_ge(vt_tr, 3 * (j - 2) + 2)
                for cb in range(4):
                    src = wvr[:, j, :].rearrange("p (r c) -> p r c", c=64)[:, :, KCS[cb]:KCS[cb] + 32]
                    last = A(vtmp[:, j % 2, cb * 256:(cb + 1) * 256].rearrange("p (r c) -> p r c", c=32), src, ACT.Copy)
                last.then_inc(vt_c, 1)
            act.wait_ge(used, S_QKV + 8)
            for r in range(8):
                act.dma_start(wbias[r * 16:r * 16 + 16, :, :, :].rearrange("p a b c -> p (a b) c"),
                              dr["rpb"][:, (7 - r) * 8:(7 - r) * 8 + 64, :]).then_inc(b_in, 16)
            A(wcz[:], wcz[:], ACT.Silu).then_inc(q_act, 1)
            nc.scalar.preload_act_table_set("natural_log_exp_and_others")
            conv_upto(S_GC + 1)
            act.wait_ge(vt_ev, 12)

            def win_evac(m, b):
                return ptw[:, (A_W + m) % 4, :, :], b.rearrange("p (c t) -> p c t", t=P)
            attention("win", A_W, G_W, pr2, win_evac, lambda m: G_W + m // 2 - 1 if m >= 4 else G_W)
            for j in range(4):
                hi(bh[:, j, :])

            def gates(S, n0):
                for j in range(4):
                    conv_upto(S + j + 1)
                    act.wait_ge(emptied, S + j + 1)
                    A(sig[:, 2 * j:2 * j + 2, :], sig[:, 2 * j:2 * j + 2, :], ACT.Sigmoid).then_inc(q_act, 1)
                conv_upto(S + 5)
            gates(S_GC, 1)
            conv_upto(S_A)
            for j in range(4):
                conv_upto(S_A + 2 * j + 1)
                conv_upto(S_A + 2 * j + 2)
                act.wait_ge(emptied, S_A + 2 * j + 2)
                A(az[:, j % 2, :], az[:, j % 2, :], ACT.Silu).then_inc(q_act, 1)
                hi(bh[:, j, :])
            gates(S_GA, 9)
            conv_upto(S_F)
            for s in range(S_F, S_F + 5):
                conv_upto(s)
            act.wait_ge(emptied, S_F + 1)
            act.dma_start(dft[:], dr["dft"].rearrange("a (t p) d -> p (a t) d", p=P)).then_inc(dft_in, 16)
            act.dma_start(dcc[:], dr["dcc"]).then_inc(dft_in, 16)
            act.wait_ge(emptied, S_F + 4)
            A(fz[:], fz[:], ACT.Silu).then_inc(q_act, 1)
            for g in range(4):
                hi(bh[:, g, :])
            gates(S_GF, 14)
            conv_upto(S_BF + 1)
            conv_upto(S_BF + 2)
            for k in range(8):
                hi(hh[:, k, :])
            out_proj(S_O2, 5)
            nc.scalar.preload_act_table_set("natural_log_exp_and_others")
            rnorm(7, ps[:, 7, :], rstd, 1.0 / D, cc("e1"))

        @block.vector
        def _(dve):
            V = nc.vector
            TT, TS, STT = V.tensor_tensor, V.tensor_scalar, V.scalar_tensor_tensor
            link = Chain(dve, ch_dve)
            state = {"q": 0, "pend": None}

            def flush():
                if state["pend"] is None:
                    return
                q, src, dh, dl = state["pend"]
                dve.wait_ge(thi_ready, q + 1)
                TT(dl, src, dh.bitcast(F32), ALU.subtract).then_inc(split_done, 1)
                state["pend"] = None

            def split(emit, dh, dl, src=None, wd=T):
                q = state["q"]
                t = (src if src is not None else tb[q % 2])[:, 0:wd]
                if q >= 2:
                    dve.wait_ge(split_done, q - 1)
                emit(t).then_inc(t_ready, 1)
                state["q"] += 1
                flush()
                state["pend"] = (q, t, dh, dl)

            def add_sq(n, k):
                i = 8 * n + k
                dve.wait_ge(sq_ready, i + 1)
                if k:
                    dve.wait_ge(sq_added, i)
                    TT(sqacc, sqacc, tb[k % 2], ALU.add).then_inc(sq_added, 1)
                else:
                    V.tensor_copy(sqacc, tb[k % 2]).then_inc(sq_added, 1)
                if k == 7:
                    dve.wait_ge(sq_added, i + 1)

            def add_msq(buf, n, k):
                i = 8 * n + k
                dve.wait_ge(msq_ready, i + 1)
                if k:
                    dve.wait_ge(msq_added, i)
                    TT(buf[:, 2, :], buf[:, 2, :], buf[:, k % 2, :], ALU.add).then_inc(msq_added, 1)
                else:
                    V.tensor_copy(buf[:, 2, :], buf[:, k % 2, :]).then_inc(msq_added, 1)

            for n in range(8):
                dve.wait_ge(tr, n + 1)
                V.tensor_copy(xT[:, n, :], ps[:, 4 + n % 2, :]).then_inc(ev, 1)
                if n >= 1:
                    add_sq(0, n - 1)
            add_sq(0, 7)

            def norm_h(i, g):
                dve.wait_ge(rstd_ready, i)
                for k in range(8):
                    split(lambda t: STT(out=t, in0=xT[:, k, :], scalar=vv(g, k), in1=rstd, op0=ALU.mult, op1=ALU.mult),
                          hh[:, k, :], hl[:, k, :])
                flush()

            norm_h(1, "mix0")

            def empty(s):
                dve.wait_ge(used, s + 1)

            def bank(s, b):
                return ps[:, 2 * (s % 2) + b, :]

            def copy(dst, src):
                return TS(dst, src, 1.0, None, ALU.mult)

            def hn_apply(r, ops):
                dve.wait_ge(hn_rstd, r + 1)
                for n, (dst, src, g) in enumerate(ops):
                    ins = STT(out=dst, in0=src, scalar=g, in1=rstd, op0=ALU.mult, op1=ALU.mult)
                ins.then_inc(hn_done, 1)

            def take_z0(s):
                j = s - S_Z0 if s < S_M else s - S_Z0B + 6
                empty(s)
                if 6 <= j < 9:
                    for q in range(2):
                        last = V.tensor_copy(hv[:, 2 * q:2 * q + 2, (j - 6) * 256:(j - 5) * 256],
                                             bank(s, q).rearrange("p (a b) -> p a b", b=256))
                else:
                    dst, n = (hq, 0) if j < 3 else (hk, 6) if j < 6 else (hgate, 18) if j < 12 else (qm0, 24)
                    for b in range(2):
                        last = V.tensor_copy(dst[:, 2 * j + b - n, :], bank(s, b))
                last.then_inc(emptied, 1)

            def ada_rows(r):
                dve.wait_ge(ada_used, 2 * r + 4)
                if r == 0:
                    V.tensor_copy(arow[0:2, 0:4, :].rearrange("p a b -> p (a b)"),
                                  ps[0:2, 2:4, :].rearrange("p a b -> p (a b)")).then_inc(ada_row, 1)
                else:
                    V.tensor_copy(arow[0:2, 2 * r + 2:2 * r + 4, :].rearrange("p a b -> p (a b)"),
                                  ps[0:2, 6 + (r + 1) % 2, :]).then_inc(ada_row, 1)

            ada_rows(0)
            for n in range(4):
                dve.wait_ge(tr, 8 + n + 1)
                V.tensor_copy(memT[:, 2 * n:2 * n + 2, :].rearrange("p a b -> p (a b)"), ps[:, 4 + n % 2, :]).then_inc(ev, 1)
            take_z0(0)
            ada_rows(1)
            for k in range(8):
                add_msq(msq, 0, k)
            ada_rows(2)
            take_z0(1)
            ada_rows(3)
            take_z0(2)
            ada_rows(4)
            take_z0(3)
            dve.wait_ge(ada_t, 1)
            link(TT(mod.rearrange("p (n c) -> p n c", c=2), ps[:, 5, 0:48].rearrange("p (n c) -> p n c", c=2),
                    vv("bada", 0, 24).unsqueeze(2).to_broadcast([P, 24, 2]), ALU.add))
            TS(gsc, mod[:, 16:32], 1.0, None, ALU.add).then_inc(mod_ready, 1)
            dve.wait_ge(mod_ready, 1)
            link(TT(gsc.rearrange("p (n c) -> p n c", c=2), gsc.rearrange("p (n c) -> p n c", c=2),
                    vv("ng2", 0, 8).unsqueeze(2).to_broadcast([P, 8, 2]), ALU.mult))

            dve.wait_ge(rstd_ready, 2)
            for l in range(2):
                for k in range(8):
                    split(lambda t: STT(out=t, in0=memT[:, k, :], scalar=vv(f"mem{l}", k), in1=msq[:, 2, :],
                                        op0=ALU.mult, op1=ALU.mult), mh[l][:, k, :], ml[l][:, k, :], wd=NMEM)
                flush()
                take_z0(4 + l)
            for l in range(2):
                s = S_M + 2 * l
                empty(s)
                V.tensor_copy((km0, km1)[l][:].rearrange("p a b -> p (a b)"), bank(s, 0)).then_inc(emptied, 1)
                empty(s + 1)
                V.tensor_copy((vm0, vm1)[l][:].rearrange("p a b -> p (a b)"), bank(s + 1, 0)).then_inc(emptied, 1)
            for l in range(2):
                kk = (km0, km1)[l][:].rearrange("p a b -> p (a b)")
                hn_apply(H_KM + l, [(kk, kk, vv(f"mk{l}"))])
            take_z0(S_Z0B)

            l3 = vv("lb", 0, 18).rearrange("p (r h) -> p r h", h=HH)
            mxl, e3, sl = lbx[:, 18:24], lbx[:, 0:18].rearrange("p (r h) -> p r h", h=HH), lbt
            link(TT(mxl, l3[:, 0, :], l3[:, 1, :], ALU.max))
            link(TT(mxl, mxl, l3[:, 2, :], ALU.max))
            TT(e3, l3, mxl.unsqueeze(1).to_broadcast([P, 3, HH]), ALU.subtract).then_inc(g_dve, 1)
            take_z0(S_Z0B + 1)
            take_z0(S_Z0B + 2)
            dve.wait_ge(g_act, 3)
            link(TT(sl, e3[:, 0, :], e3[:, 1, :], ALU.add))
            link(TT(sl, sl, e3[:, 2, :], ALU.add))
            link(V.reciprocal(sl, sl))
            link(TT(lbt, e3[:, 0, :], sl, ALU.mult))
            link(TS(oml, lbt, -1.0, 1.0, ALU.mult, ALU.add))
            for h in range(HH):
                last = TS(hb[:, h, :], hk[:, h, :], oml[:, h:h + 1], lbt[:, h:h + 1], ALU.mult, ALU.add)
            last.then_inc(g_dve, 1)
            dve.wait_ge(g_dve, 2)
            TS(hk[:], hb[:], -1.0, 1.0, ALU.mult, ALU.add).then_inc(g_dve, 1)
            take_z0(S_Z0B + 3)
            dve.wait_ge(g_act, 4)
            dve.wait_ge(g_dve, 3)
            for h in range(HH):
                last = V.tensor_tensor_scan(hb[:, h, :], cc("scan"), hA[:, h, :], 0.0, ALU.mult, ALU.add)
            last.then_inc(g_dve, 1)

            for j in range(4, 7):
                take_z0(S_Z0B + j)
            SC = float(P) ** -0.5
            dve.wait_ge(g_dve, 4)

            def lv_diff(j):
                hf, l = j % 2, j // 2
                h = 64 >> l
                if j >= 2:
                    dve.wait_ge(lv_k, j - 1)
                    dve.wait_ge(lv_q, j - 1)
                G = 3 * T // (2 * h)
                b = hb[:, 3 * hf:3 * hf + 3, :].rearrange("p a t -> p (a t)").rearrange("p (g t) -> p g t", t=2 * h)
                e = hE[:, 3 * hf:3 * hf + 3, :].rearrange("p a t -> p (a t)").rearrange("p (g t) -> p g t", t=2 * h)
                mid = b[:, :, h - 1:h].to_broadcast([P, G, h])
                TT(e[:, :, h:2 * h], b[:, :, h:2 * h], mid, ALU.subtract)
                TT(e[:, :, 0:h], mid, b[:, :, 0:h], ALU.subtract).then_inc(lv_d, 1)

            for hf in range(2):
                dve.wait_ge(lv_mm, hf + 1)
                for h in range(3 * hf, 3 * hf + 3):
                    last = STT(out=hA[:, h, :].rearrange("p (c t) -> p c t", t=P), in0=ps[:, h, :].rearrange("p (c t) -> p c t", t=P),
                               scalar=SC, in1=cc("ident").unsqueeze(1).to_broadcast([P, 4, P]), op0=ALU.mult, op1=ALU.mult)
                last.then_inc(lv_cp, 1)
            lv_diff(0)
            for j in range(14):
                hf, l = j % 2, j // 2
                h = 64 >> l
                if j < 13:
                    lv_diff(j + 1)
                dve.wait_ge(lv_e, j + 1)
                if j >= 2:
                    dve.wait_ge(lv_mm, j + 1)
                rt = lambda x: x[:, 3 * hf:3 * hf + 3, :].rearrange("p a t -> p (a t)").rearrange("p (g t) -> p g t", t=2 * h)[:, :, h:2 * h]
                STT(out=hQL[:, 3 * hf:3 * hf + 3, :].rearrange("p a t -> p (a t)").rearrange("p (g t) -> p g t", t=h),
                    in0=rt(hq), scalar=SC, in1=rt(hE), op0=ALU.mult, op1=ALU.mult).then_inc(lv_q, 1)

                def copies(j):
                    hf, l = j % 2, j // 2
                    h = 64 >> l
                    dve.wait_ge(lv_mm, j + 3)
                    dve.wait_ge(lv_cp, 2)
                    n = 64 // h
                    msk = cc("lvl", 64 * l, 64).bitcast(U32)
                    for h3 in range(3):
                        hd = 3 * hf + h3
                        o = h3 * 256
                        for c in range(4):
                            src = ps[:, 3 * hf + o // 512, o % 512 + 64 * c:o % 512 + 64 * c + 64].rearrange("p (g t) -> p g t", t=h)
                            dst = hA[:, hd, c * P:(c + 1) * P].rearrange("p (g t) -> p g t", t=2 * h)[:, :, h:2 * h]
                            last = V.copy_predicated(dst, msk.rearrange("p (g t) -> p g t", t=h), src)
                    last.then_inc(lv_cp, 1)
                if j >= 1:
                    copies(j - 1)
            copies(13)
            b4 = hb[:].rearrange("p a t -> p (a t)").rearrange("p (g t) -> p g t", t=P)
            e4 = hE[:].rearrange("p a t -> p (a t)").rearrange("p (g t) -> p g t", t=P)
            dve.wait_ge(lv_k, 14)
            dve.wait_ge(lv_q, 14)
            TT(e4, b4[:, :, P - 1:P].to_broadcast([P, 24, P]), b4, ALU.subtract).then_inc(lv_d, 1)
            dve.wait_ge(lv_e, 15)
            TT(hKL[:], hk[:], hE[:], ALU.mult).then_inc(st_k, 1)
            dve.wait_ge(lv_e, 16)
            link(STT(out=hq[:], in0=hq[:], scalar=SC, in1=hE[:], op0=ALU.mult, op1=ALU.mult))
            for n in range(HH):
                dve.wait_ge(st_kv, n + 1)
                for c in range(3):
                    kvp = ps[:, 2 + n % 2, c * P:(c + 1) * P]
                    if c == 0:
                        ins = copy(hS[:, 0, n, :], kvp)
                    else:
                        ins = STT(out=hS[:, c, n, :], in0=hS[:, c - 1, n, :], scalar=hE[:, n, c * P + P - 1:c * P + P], in1=kvp,
                                  op0=ALU.mult, op1=ALU.add)
                    if c < 2:
                        link(ins)
                ins.then_inc(st_s, 1)
            dve.wait_ge(g_act, 5)

            def gated(h):
                split(lambda t: TT(t, hA[:, h, :], hgate[:, h, :], ALU.mult), hh[:, h, :], hl[:, h, :])
            for h in range(HH):
                dve.wait_ge(ho_mm, h + 1)
                V.tensor_copy(hA[:, h, :], ps[:, h % 2, :]).then_inc(ho_cp, 1)
                if h >= 1:
                    hn_apply(H_HG + h - 1, [(hA[:, h - 1, :], hA[:, h - 1, :], vv("hgo"))])
                    dve.wait_ge(hn_done, H_HG + h)
                    gated(h - 1)
            hn_apply(H_HG + 5, [(hA[:, 5, :], hA[:, 5, :], vv("hgo"))])
            dve.wait_ge(hn_done, H_HG + 6)
            gated(5)
            flush()
            for j in range(2):
                hn_apply(H_QM0 + j, [(qm0[:, j, :], qm0[:, j, :], vv("mq0"))])

            def attention(kind, U0, G0, prb, consume):
                us = units(kind)
                for n in range(len(us) + 4):
                    if n < len(us):
                        u = U0 + n
                        wd = us[n][0] * P
                        dve.wait_ge(sc_ready, u + 1)
                        if kind == "win":
                            dve.wait_ge(bm_ready, n + 1)
                            b = ps[:, 4 + u % 3, 0:256]
                            link(TT(b, b, wbm[:, n % 4, :], ALU.add))
                        V.tensor_reduce(nmx[:, u % 4:u % 4 + 1], ps[:, 4 + u % 3, 0:wd], AX, ALU.max,
                                        negate=True).then_inc(mx_ready, 1)
                    if 1 <= n < len(us) + 1:
                        u = U0 + n - 1
                        wd = us[n - 1][0] * P
                        dve.wait_ge(ex_ready, u + 1)
                        link(V.reciprocal(rc[:, u % 4:u % 4 + 1], sm[:, u % 4:u % 4 + 1]))
                        x = prb[:, u % 3, 0:wd]
                        TS(x, x, rc[:, u % 4:u % 4 + 1], None, ALU.mult).then_inc(pn_ready, 1)
                    if n >= 4 and us[n - 4][2]:
                        g = us[n - 4][1]
                        dve.wait_ge(pv_done, G0 + g + 1)
                        consume(g, (G0 + g) % 2)

            def take(c):
                def f(g, b):
                    split(lambda t: copy(t, ps[:, b, :]), hh[:, c + g, :], hl[:, c + g, :])
                return f

            attention("mem", A_M0, G_M0, pr0, take(6))
            flush()

            def out_proj(S, n, gate=None):
                for j in range(4):
                    s = S + j
                    empty(s)
                    for b in range(2):
                        x = xT[:, 2 * j + b, :]
                        if gate is None:
                            last = TT(x, x, bank(s, b), ALU.add)
                        else:
                            last = STT(out=x, in0=bank(s, b), scalar=gate(2 * j + b), in1=x, op0=ALU.mult, op1=ALU.add)
                    last.then_inc(emptied, 1)
                    for k in (2 * j - 2, 2 * j - 1):
                        if k >= 0:
                            add_sq(n, k)
                add_sq(n, 6)
                add_sq(n, 7)

            out_proj(S_O0, 1)
            norm_h(3, "ffn0")

            def ffn_up(S, layer):
                cw = VOFF[f"cw{layer}"]
                b0 = 22 * layer
                with dve.Fori(0, 11) as i:
                    for u in range(2):
                        s = S + u
                        par = s % 2
                        n = 2 * b0 + 2 * u
                        a, b = scr[:, 2 * u, :], scr[:, 2 * u + 1, :]
                        pa, pb = ps[:, 2 * par, :], ps[:, 2 * par + 1, :]

                        def tap(dst, src, d, col, sm_):
                            STT(out=dst[:, d:T], in0=src[:, 0:T - d], scalar=vec[:, bass.ds(2 * i + col, 1)], in1=dst[:, d:T],
                                op0=ALU.mult, op1=ALU.add).then_inc(sm_, 1)
                        dve.wait_ge(f_acc, 4 * i + (n + 1))
                        tap(a, pa, 1, cw + 44 + u, f_tap)
                        dve.wait_ge(f_acc, 4 * i + (n + 2))
                        tap(b, pb, 1, cw + 44 + 22 + u, f_tap)
                        dve.wait_ge(f_tap, 4 * i + (n + 1))
                        tap(a, pa, 2, cw + u, f_conv)
                        dve.wait_ge(f_tap, 4 * i + (n + 2))
                        tap(b, pb, 2, cw + 22 + u, emptied)
                        dve.wait_ge(f_silu, 2 * i + (b0 + u + 1))
                        dve.wait_ge(emptied, 2 * i + (s + 1))
                        TT(a, a, b, ALU.mult).then_inc(f_g, 1)
                        dve.wait_ge(f_hi, 2 * i + (b0 + u + 1))
                        sl_ = bass.ds((2 * i + u) * T, T)
                        TT(gl[:].rearrange("p c t -> p (c t)")[:, sl_], a,
                           gh[:].rearrange("p c t -> p (c t)")[:, sl_].bitcast(F32), ALU.subtract).then_inc(f_lo, 1)

            def ffn_down(S, n):
                dve.wait_ge(f_lo, 22 * (n // 2))
                for k in range(8):
                    empty(S + 2 * k + 1)
                    x = xT[:, k, :]
                    TT(x, x, ps[:, k % 2, :], ALU.add).then_inc(emptied, 2)
                    if k:
                        add_sq(n, k - 1)
                add_sq(n, 7)

            ffn_up(S_U0, 0)
            ffn_down(S_D0, 2)

            norm_h(4, "mix1")
            dve.wait_ge(pos_in, 16)
            link(V.tensor_copy(rtmp[:, 0, :], posi[:]))
            ang = rtmp[:, 0, :]
            link(TS(ang, ang, cc("inv"), None, ALU.mult))
            for j in range(2):
                n_, r_ = rtmp[:, 1, :], posf[:, j, :]
                link(TS(n_, ang, 1.0 / TWO_PI, 0.25 * j, ALU.mult, ALU.add))
                link(TS(n_, n_, MAGIC, -MAGIC, ALU.add, ALU.add))
                link(STT(out=r_, in0=n_, scalar=-C1, in1=ang, op0=ALU.mult, op1=ALU.add))
                link(STT(out=r_, in0=n_, scalar=-C2, in1=r_, op0=ALU.mult, op1=ALU.add))
                link(STT(out=r_, in0=n_, scalar=-C3, in1=r_, op0=ALU.mult, op1=ALU.add))
                if j:
                    link(TS(r_, r_, float(np.pi / 2), None, ALU.add))
                TS(r_, r_, 3.1415925, -3.1415925, ALU.min, ALU.max).then_inc(rp_d, 1)
            for s in range(S_Z1, S_UQ):
                empty(s)
                for b in range(2):
                    last = V.tensor_copy(z1[:, 2 * (s - S_Z1) + b, :], bank(s, b))
                last.then_inc(emptied, 1)
            for r, (c0, nn, g) in enumerate(((0, 3, "qa"), (3, 2, "kva"))):
                dve.wait_ge(hn_rstd, H_C1 + r + 1)
                for j in range(nn):
                    split(lambda t: STT(out=t, in0=z1[:, c0 + j, :], scalar=vv(g, j), in1=rstd, op0=ALU.mult, op1=ALU.mult),
                          hh[:, c0 + j, :], hl[:, c0 + j, :])
                flush()
                dve.wait_ge(split_done, state["q"])
                dve.sem_inc(hn_done, 1)
            dve.wait_ge(rp_a, 2)
            link(V.tensor_copy(posf[:, 0, :], z1[:, 5, :]))
            TS(z1[:, 5, :], z1[:, 5, :], vv("knr"), None, ALU.mult).then_inc(kq_ready, 1)
            for s in range(S_UQ, S_UKV):
                p = s - S_UQ
                empty(s)
                V.tensor_copy(mqn[:, 2 * p, :], ps[:, 0, :])
                V.tensor_copy(mqn[:, 2 * p + 1, :], ps[:, 1, :])
                V.tensor_copy(mqr[:, p, :], ps[:, 2, :]).then_inc(emptied, 1)
            for s in range(S_UKV, S_O1):
                p = s - S_UKV
                empty(s)
                V.tensor_copy(mkn[:, 2 * p, :], ps[:, 0, :])
                V.tensor_copy(mkn[:, 2 * p + 1, :], ps[:, 1, :])
                for q in range(2):
                    last = V.tensor_copy(mv[:, 2 * q:2 * q + 2, p * 256:(p + 1) * 256],
                                         ps[:, 2 + q, :].rearrange("p (a b) -> p a b", b=256))
                last.then_inc(emptied, 1)

            def rope(x, r):
                dve.wait_ge(rot_mm, r + 1)
                TT(rtmp[:, 0, :], ps[:, 6, :], sinT[:], ALU.mult).then_inc(rot_rd, 1)
                link(TT(rtmp[:, 1, :], x, cosT[:], ALU.mult))
                dve.wait_ge(rot_rd, r + 1)

            for h in range(HH):
                r = slice(64 * (h % 2), 64 * (h % 2) + 64)
                dve.wait_ge(hn_rstd, H_Q1 + h + 1)
                STT(out=mqr[r, h // 2, :], in0=mqr[r, h // 2, :], scalar=vv("qnr")[r, :], in1=scr[r, 1, :], op0=ALU.mult, op1=ALU.mult)
                STT(out=mqn[:, h, :], in0=mqn[:, h, :], scalar=vv("qnn"), in1=rstd, op0=ALU.mult, op1=ALU.mult).then_inc(hn_done, 1)
                if h % 2 == 1:
                    rope(mqr[:, h // 2, :], h // 2)
                    link(TT(mqr[:, h // 2, :], rtmp[:, 0, :], rtmp[:, 1, :], ALU.add))
            rope(z1[:, 5, :], 3)
            link(TT(kr0[:], rtmp[:, 0, :], rtmp[:, 1, :], ALU.add))
            for h in range(HH):
                r = slice(64 * (h % 2), 64 * (h % 2) + 64)
                dve.wait_ge(hn_rstd, H_K1 + h + 1)
                TT(mkr[r, h // 2, :], kr0[r, :], scr[r, 1, :], ALU.mult)
                STT(out=mkn[:, h, :], in0=mkn[:, h, :], scalar=vv("knn"), in1=rstd, op0=ALU.mult, op1=ALU.mult).then_inc(hn_done, 1)
            for j in range(2):
                hn_apply(H_QM1 + j, [(z1[:, 6 + j, :], z1[:, 6 + j, :], vv("mq1"))])
            attention("mla", A_MLA, G_MLA, pr1, take(0))
            flush()
            attention("mem", A_M1, G_M1, pr1, take(6))
            flush()
            out_proj(S_O1, 3)
            norm_h(5, "ffn1")
            ffn_up(S_U1, 1)
            ffn_down(S_D1, 4)

            def norm_mod(i, src, rs, K, c, dh, dl, wd):
                dve.wait_ge(rstd_ready, i)
                for k in range(8):
                    def emit(t):
                        link(STT(out=t, in0=src[:, k, :], scalar=gsc[:, 2 * k + c:2 * k + c + 1], in1=rs, op0=ALU.mult, op1=ALU.mult))
                        return TS(t, t, mod[:, 2 * k + c:2 * k + c + 1], None, ALU.add)
                    split(emit, dh[:, k, :], dl[:, k, :], wd=wd)
                flush()

            norm_mod(6, xT, rstd, 8, 0, hh, hl, T)
            def ctx_in_half(half):
                for n in (2 * half, 2 * half + 1):
                    dve.wait_ge(tr, 12 + n + 1)
                    V.tensor_copy(ctxT[:, 2 * n:2 * n + 2, :].rearrange("p a b -> p (a b)"), ps[:, 4 + n % 2, :]).then_inc(ev, 1)
                for k in range(4 * half, 4 * half + 4):
                    add_msq(csq, 1, k)

            ctx_in_half(0)

            def bcol(n):
                return vv("bin", n)
            B_AX, B_AB, B_AC, B_AZ, B_FU, B_FZ, B_Q, B_K, B_V, B_CZ, B_GA, B_GF, B_GC = 0, 4, 8, 12, 16, 20, 24, 28, 32, 36, 40, 48, 56
            for s in (S_QKV, S_QKV + 1):
                empty(s)
                for b in range(2):
                    j = 2 * (s - S_QKV) + b
                    for cb in range(4):
                        last = TS(wq[:, j, cb * P:(cb + 1) * P].rearrange("p (r q) -> p r q", q=16),
                                  bank(s, b).rearrange("p (r c q) -> p r c q", c=4, q=16)[:, :, cb, :],
                                  bcol(B_Q + j), 0.125, ALU.add, ALU.mult)
                last.then_inc(emptied, 1)
            ctx_in_half(1)

            def take_cz(u):
                s = S_QKV + 2 + u
                empty(s)
                for b in range(2):
                    last = TS(wcz[:, 2 * u + b, :], bank(s, b), bcol(B_CZ + 2 * u + b), None, ALU.add)
                last.then_inc(emptied, 1)
            take_cz(0)
            norm_mod(7, ctxT, csq[:, 2, :], 8, 1, ch, cl, NMEM)
            take_cz(1)

            def take_kv(s, lat, cxt, bb):
                empty(s)
                for b in range(2):
                    j = 2 * ((s - S_QKV) % 2) + b
                    TS(lat[:, j, :], bank(s, b), bcol(bb + j), None, ALU.add)
                    last = TS(cxt[:, j, :], ps[:, 4 + s % 2, b * NMEM:(b + 1) * NMEM], bcol(bb + j), None, ALU.add)
                last.then_inc(emptied, 1)
            take_kv(S_QKV + 4, wvr, wvc, B_V)
            take_kv(S_QKV + 5, wvr, wvc, B_V)
            for u in range(2):
                take_kv(S_QKV + 6 + u, wk, wkc, B_K)
                for j in (2 * u, 2 * u + 1):
                    for q in range(3):
                        n = 3 * j + q
                        dve.wait_ge(vt_tr, n + 1)
                        if q < 2:
                            last = V.tensor_copy(vtok[:, 4 * q:4 * q + 4, j * P:(j + 1) * P], ps[:, 6 + n % 2, :].rearrange("p (a b) -> p a b", b=P))
                        else:
                            last = V.tensor_copy(vct[:, :, j * P:(j + 1) * P], ps[:, 6 + n % 2, 0:256].rearrange("p (a b) -> p a b", b=P))
                        last.then_inc(vt_ev, 1)
            dve.wait_ge(q_act, 1)

            def win_take(g, b):
                cb, hp = g // 4, g % 4
                y = wcz[:, hp, :].rearrange("p (r c q) -> p r c q", c=4, q=16)[:, :, cb, :]
                TT(y, ps[:, b, 0:P].rearrange("p (r q) -> p r q", q=16), y, ALU.mult).then_inc(o_read, 1)
            attention("win", A_W, G_W, pr2, win_take)
            dve.wait_ge(o_read, 16)
            for j in range(4):
                split(lambda t: copy(t, wcz[:, j, :]), bh[:, j, :], bl[:, j, :])
            flush()

            def gates(S, bb):
                for j in range(4):
                    empty(S + j)
                    for b in range(2):
                        last = TS(sig[:, 2 * j + b, :], bank(S + j, b), bcol(bb + 2 * j + b), None, ALU.add)
                    last.then_inc(emptied, 1)

            def branch(S, n, first):
                dve.wait_ge(q_act, n)
                for s in (S, S + 1):
                    empty(s)
                    for b in range(4):
                        k = 4 * (s - S) + b
                        o = ps[:, 4 * (s % 2) + b, :]
                        if first:
                            last = TT(mm_[:, k, :], o, sig[:, k, :], ALU.mult)
                        else:
                            last = TT(sig[:, k, :], o, sig[:, k, :], ALU.mult)
                    last.then_inc(emptied, 1)
                if not first:
                    dve.wait_ge(emptied, S + 2)
                    link(TT(mm_[:], mm_[:], sig[:], ALU.add))

            gates(S_GC, B_GC)
            branch(S_BC, 5, True)
            for j in range(4):
                s = S_A + 2 * j
                p_ = atmp[:, 0, :]
                empty(s)
                link(TS(atmp[:, 1, :], bank(s, 0), bcol(B_AC + j), None, ALU.add))
                STT(out=p_, in0=bank(s, 1), scalar=bcol(B_AX + j), in1=atmp[:, 1, :], op0=ALU.add, op1=ALU.mult).then_inc(emptied, 1)
                dve.wait_ge(emptied, s + 1)
                a = acc2[:, j % 2, :]
                link(TS(a, p_, vv("wc2", 4 + j), vv("bc2", j), ALU.mult, ALU.add))
                link(STT(out=a[:, 1:T], in0=p_[:, 0:T - 1], scalar=vv("wc2", j), in1=a[:, 1:T], op0=ALU.mult, op1=ALU.add))
                link(STT(out=a[:, 0:T - 1], in0=p_[:, 1:T], scalar=vv("wc2", 8 + j), in1=a[:, 0:T - 1], op0=ALU.mult, op1=ALU.add))
                empty(s + 1)
                link(STT(out=a, in0=bank(s + 1, 0), scalar=bcol(B_AB + j), in1=a, op0=ALU.add, op1=ALU.mult))
                TS(az[:, j % 2, :], bank(s + 1, 1), bcol(B_AZ + j), None, ALU.add).then_inc(emptied, 1)
                dve.wait_ge(q_act, 5 + j + 1)
                split(lambda t: TT(t, a, az[:, j % 2, :], ALU.mult), bh[:, j, :], bl[:, j, :])
            flush()
            gates(S_GA, B_GA)
            branch(S_BA, 13, False)
            for s in range(S_F, S_F + 4):
                j0 = s - S_F
                empty(s)
                for b in range(2):
                    j = 2 * (j0 % 2) + b
                    last = TS((fu, fz)[j0 // 2][:, j, :], bank(s, b), bcol((B_FU, B_FZ)[j0 // 2] + j), None, ALU.add)
                last.then_inc(emptied, 1)
            for n in range(8):
                g, q = n // 2, n % 2
                dve.wait_ge(df_mm, n + 1)
                TS(xc[:, 2 * q:2 * q + 2, g, :], ps[:, 4 + n % 2, :].rearrange("p (a b) -> p a b", b=256), 1.0 / 256, None,
                   ALU.mult).then_inc(df_ev, 1)
            dve.wait_ge(q_act, 14)
            for g in range(4):
                dve.wait_ge(df_mm, 8 + g + 1)
                split(lambda t: TT(t, ps[:, 6 + g % 2, :], fz[:, g, :], ALU.mult), bh[:, g, :], bl[:, g, :])
            flush()
            gates(S_GF, B_GF)
            dve.wait_ge(q_act, 18)
            for s in (S_BF, S_BF + 1):
                empty(s)
                for b in range(4):
                    k = 4 * (s - S_BF) + b
                    ins = TT(sig[:, k, :], ps[:, 4 * (s % 2) + b, :], sig[:, k, :], ALU.mult)
                    if b == 3:
                        ins.then_inc(emptied, 1)
                        dve.wait_ge(emptied, s + 1)
                    else:
                        link(ins)
                    split(lambda t: TT(t, mm_[:, k, :], sig[:, k, :], ALU.add), hh[:, k, :], hl[:, k, :])
            flush()
            out_proj(S_O2, 5, gate=lambda k: mod[:, 32 + 2 * k:33 + 2 * k])
            dve.wait_ge(rstd_ready, 8)
            for k in range(8):
                last = STT(out=yT[:, k, :], in0=xT[:, k, :], scalar=vv("fin", k), in1=rstd, op0=ALU.mult, op1=ALU.mult)
            last.then_inc(yn_ready, 1)
            for n in range(8):
                tt, q = n // 2, n % 2
                dve.wait_ge(y_tr, n + 1)
                V.tensor_copy(ytok[:, tt, q * T:(q + 1) * T], ps[:, n % 2, :]).then_inc(y_ev, 1)


def slots(wm, K, cols):
    n = wm.shape[1] // cols
    return np.ascontiguousarray(wm.reshape(K, P, n, cols).transpose(2, 1, 0, 3).reshape(n, P, K * cols))


def padded(a):
    return np.concatenate([a, np.zeros((a.shape[0], P, SLOT - a.shape[2]), a.dtype)], axis=2) if a.shape[2] < SLOT else a


def paired(wm, a, b, n):
    x = wm[:, a:a + n * P].reshape(-1, n, 1, P)
    y = wm[:, b:b + n * P].reshape(-1, n, 1, P)
    return slots(np.concatenate([x, y], axis=2).reshape(-1, 2 * n * P), 8, 256)


def down(wm):
    return np.ascontiguousarray(wm.reshape(2, 11, P, 8, P).transpose(3, 0, 2, 1, 4).reshape(16, P, DSLOT))


def columns(v):
    return v.reshape(-1, P).T


def constants():
    c = {n: np.zeros((P, k), np.float32) for n, k in CON}
    c["ones"][:] = 1
    c["ident"][:] = np.eye(P)
    c["b64"][:64, :64] = c["b64"][64:, 64:] = 1
    for b in (0, 64):
        for j in range(32):
            c["rot"][b + j + 32, b + j] = -1
            c["rot"][b + j, b + j + 32] = 1
    i = np.arange(P)
    c["causal"][:] = np.where(i[None, :] <= i[:, None], 0, NEG)
    for cb in range(4):
        q = cb * 16 + i % 16
        lo = np.clip(q - 8, 0, 48)
        kc = KCS[cb] + np.arange(32)
        c["winmask"][:, cb * 32:(cb + 1) * 32] = np.where((kc >= lo[:, None]) & (kc < lo[:, None] + 16), 0, NEG)
    c["scan"][:] = (np.arange(T) % P != 0)
    for l in range(7):
        h = 64 >> l
        t = np.arange(64)
        c["lvl"][:, 64 * l:64 * l + 64] = i[:, None] // h == 2 * (t // h)[None, :]
    c["inv"][:, 0] = np.float32(10000.0) ** (-(i % 32).astype(np.float32) / np.float32(32))
    c["e1"][:], c["e64"][:], c["e192"][:] = EPS, 64 * EPS, 192 * EPS
    return np.concatenate([c[n] for n, _ in CON], axis=1)


def layout(i):
    d = {"x": i["x"], "mem": i["mem"], "pos": i["positions"], "ctx": i["ctx_2"]}
    mk, z = i["w_mem_kv"], slots(i["hg_w_in"][0], 8, 256)
    d["w0"] = np.concatenate([z[:6], slots(mk[0], 8, 256), slots(mk[1], 8, 256), z[6:]])

    def out_up(l):
        return [slots(i["w_out"][l], 8, 256), paired(i["w_up"][l], 0, FF, FC)]
    d["w0b"] = np.concatenate(out_up(0))
    d["wd0"], d["wd1"] = down(i["w_down"][0]), down(i["w_down"][1])
    win = i["mla_w_in"][0]
    z = np.concatenate([win[:, 0:704], win[:, 640:704], win[:, 704:960]], axis=1)
    uq = i["mla_w_uq"][0].reshape(384, 3, 2, 192)
    uq = np.concatenate([uq[:, :, :, 0:128].reshape(384, 3, 256), uq[:, :, :, 128:192].reshape(384, 3, 128)], axis=2)
    ukv = i["mla_w_ukv"][0].reshape(256, 3, 2, 2, 128).transpose(0, 1, 3, 2, 4)
    d["w1"] = np.concatenate([slots(z, 8, 256), padded(slots(uq.reshape(384, 1152), 3, 384)),
                              padded(slots(ukv.reshape(256, 1536), 2, 512))] + out_up(1))
    w2 = i["w_in_2"][0]
    br = lambda n: slots(i[n][0], 4, 512)
    conv = np.stack([paired(w2, 1024, 0, 4), paired(w2, 512, 1536, 4)], axis=1).reshape(8, P, SLOT)
    d["w2"] = np.concatenate([*(slots(w2[:, a:a + 512], 8, 256) for a in (3072, 4608, 4096, 3584)), slots(w2[:, 7168:8192], 8, 256), br("w_br_c_2"),
                              conv, slots(w2[:, 5120:6144], 8, 256), br("w_br_a_2"),
                              slots(w2[:, 2048:3072], 8, 256), slots(w2[:, 6144:7168], 8, 256), br("w_br_f_2"),
                              slots(i["w_out_2"][0], 8, 256)])
    d["wada"] = slots(i["w_ada_2"][0], 8, 256)
    r = i["rpb_2"][0].transpose(1, 0, 2)
    r = np.pad(r, ((0, 0), (0, 0), (16, 17))).reshape(120, 64)
    d["rpb"] = np.stack([r[:, 15 - q:63 - q] for q in range(16)])
    twice = lambda v: np.concatenate([v, v]).reshape(P, 1)
    v = {}
    for l in range(2):
        v[f"mix{l}"], v[f"ffn{l}"], v[f"mem{l}"] = (columns(i[n][l]) for n in ("mix_norm_g", "ffn_norm_g", "mem_norm_g"))
        v[f"cw{l}"], v[f"cb{l}"] = columns(i["conv_w"][l]), columns(i["conv_b"][l])
        v[f"mq{l}"], v[f"mk{l}"] = twice(i["mem_q_norm_g"][l]), twice(i["mem_k_norm_g"][l])
    v["bin"], v["bada"], v["ng2"], v["fin"] = columns(i["b_in_2"][0]), columns(i["b_ada_2"][0]), columns(i["norm_g_2"][0]), columns(i["final_g_2"])
    v["wc2"], v["bc2"] = columns(i["w_conv_2"][0]), columns(i["b_conv_2"][0])
    v["cc"] = np.stack([columns(i["c_2"][0]), columns(i["c_ctx_2"])], axis=2).reshape(P, 16)
    v["lb"], v["hgo"] = columns(i["hg_lb_logits"]), columns(i["hg_out_norm_g"][0])
    v["qa"], v["kva"] = columns(i["mla_qa_norm_g"][0]), columns(i["mla_kva_norm_g"][0])
    for n, k in (("qn", "mla_q_norm_g"), ("kn", "mla_k_norm_g")):
        v[n + "n"], v[n + "r"] = i[k][0][0:128].reshape(P, 1), twice(i[k][0][128:192])
    d["vec"] = np.ascontiguousarray(np.concatenate([v[n] for n, _ in VEC], axis=1))
    d["con"] = constants()
    t = np.arange(T)
    a = (t[:, None] * t[None, :] % T) * (TWO_PI / T)
    c = np.arange(P)
    b = (c[:, None] * c[None, :] % P) * (TWO_PI / P)
    d["dft"] = np.stack([np.cos(a), np.sin(a)]).astype(np.float32)
    d["dcc"] = np.concatenate([np.cos(b), -np.sin(b)], axis=1).astype(np.float32)
    return d


def kernel(**inputs):
    import concourse.bacc as bacc
    from concourse.bass_utils import run_bass_kernel_spmd as run

    nc = bacc.Bacc("TRN2", target_bir_lowering=False, num_devices=1)
    arrays, dr = {}, {}
    for name, a in layout({k: np.asarray(v) for k, v in inputs.items()}).items():
        a = np.ascontiguousarray(a)
        arrays["in_" + name] = a
        dr[name] = nc.dram_tensor("in_" + name, a.shape, mybir.dt.from_np(a.dtype), kind="ExternalInput").ap()
    out = nc.dram_tensor("out_0", (1, T, D), F32, kind="ExternalOutput").ap()
    build(nc, dr, out)
    return run(nc, [arrays], core_ids=[0]).results[0]["out_0"]
```

```python
from contextlib import ExitStack

import numpy as np
import concourse.bass as bass
from concourse import mybir
from concourse.alu_op_type import AluOpType as ALU

F32, F32R, U32, I32 = mybir.dt.float32, mybir.dt.float32r, mybir.dt.uint32, mybir.dt.int32
ACT = mybir.ActivationFunctionType
AX = mybir.AxisListType.X

P, T, D, KC = 128, 512, 1024, 8
NMEM = 256
FF = 2816
FC = FF // P
HH = 6
SLOT = 2048
DSLOT = 11 * P
EPS = 1e-6
NEG = -1e30
KCS = [0, 8, 24, 32]

S_Z0 = 0
S_M = S_Z0 + 6
S_Z0B = S_M + 4
S_O0 = S_Z0B + 7
S_U0 = S_O0 + 4
S_D0 = S_U0 + 22
S_Z1 = S_D0 + 16
S_UQ = S_Z1 + 4
S_UKV = S_UQ + 3
S_O1 = S_UKV + 3
S_U1 = S_O1 + 4
S_D1 = S_U1 + 22
S_QKV = S_D1 + 16
S_GC = S_QKV + 8
S_BC = S_GC + 4
S_A = S_BC + 2
S_GA = S_A + 8
S_BA = S_GA + 4
S_F = S_BA + 2
S_GF = S_F + 4
S_BF = S_GF + 4
S_O2 = S_BF + 2
NS = S_O2 + 4
NADA = 12

VEC = [("mix0", 8), ("mix1", 8), ("ffn0", 8), ("ffn1", 8), ("mem0", 8), ("mem1", 8),
       ("cw0", 132), ("cw1", 132), ("cb0", 44), ("cb1", 44), ("bin", 64), ("bada", 24), ("ng2", 8),
       ("fin", 8), ("wc2", 12), ("bc2", 4), ("cc", 16), ("lb", 18), ("hgo", 1), ("qa", 3), ("kva", 2),
       ("qnn", 1), ("qnr", 1), ("knn", 1), ("knr", 1), ("mq0", 1), ("mq1", 1), ("mk0", 1), ("mk1", 1)]
VOFF, _n = {}, 0
for _name, _c in VEC:
    VOFF[_name] = _n
    _n += _c
NV = _n

CON = [("ones", 128), ("ident", 128), ("b64", 128), ("rot", 128), ("causal", 128), ("winmask", 128),
       ("scan", 512), ("lvl", 448), ("inv", 1), ("e1", 1), ("e64", 1), ("e192", 1)]
COFF, _n = {}, 0
for _name, _c in CON:
    COFF[_name] = _n
    _n += _c
NC = _n

TWO_PI = 2 * np.pi
C1 = 6.28125
C2 = float(np.float32(TWO_PI - C1))
C3 = float(np.float32(TWO_PI - C1 - C2))
MAGIC = 12582912.0


class Chain:

    def __init__(self, eng, sem):
        self.eng, self.sem, self.n = eng, sem, 0

    def __call__(self, ins):
        self.n += 1
        ins.then_inc(self.sem, 1)
        self.eng.wait_ge(self.sem, self.n)


def build(nc, dr, out):
    KB = 1024
    base = 16512
    RAW, WHI, WLO, HR, XT, CONST, SCR, WORK = (base + KB * k for k in (0, 16, 32, 48, 80, 96, 106, 118))

    def at(name, off, shape, dt=F32):
        return nc.alloc_sbuf_tensor_at(name, shape, dt, offset=off)

    wraw = at("wraw", RAW, [P, 2, SLOT])
    whi = at("whi", WHI, [P, 2, SLOT], F32R)
    wlo = at("wlo", WLO, [P, 2, SLOT], F32R)
    hh = at("hh", HR, [P, KC, T], F32R)
    hl = at("hl", HR + 16 * KB, [P, KC, T], F32R)
    xT = at("xT", XT, [P, KC, T])
    con = at("con", CONST, [P, NC])
    vec = at("vec", CONST + 4 * ((NC + 7) // 8 * 8), [P, NV])
    so = CONST + 4 * ((NC + 7) // 8 * 8) + 4 * ((NV + 7) // 8 * 8)
    small = at("small", so, [P, 176])
    assert so + 176 * 4 <= SCR, so + 176 * 4 - SCR
    scr = at("scr", SCR, [P, 4, T])
    km1 = at("km1", SCR + 8 * KB, [P, 2, NMEM])
    vm1 = at("vm1", SCR + 10 * KB, [P, 2, NMEM])
    sqacc, rstd = scr[:, 0, :], scr[:, 1, :]
    tb = [scr[:, 2, :], scr[:, 3, :]]

    def w(name, kb, shape, dt=F32):
        return at(name, WORK + int(kb * KB), shape, dt)

    xtok = w("xtok", 0, [P, 4, D])
    ada = w("ada", 24, [P, 3, SLOT])
    arow = w("arow", 48, [P, 12, 256])
    mh = [w(f"mh{l}", 24 + 16 * l, [P, KC, NMEM], F32R) for l in range(2)]
    ml = [w(f"ml{l}", 32 + 16 * l, [P, KC, NMEM], F32R) for l in range(2)]
    memT = w("memT", 60, [P, KC, NMEM])
    msq = w("msq", 68, [P, 3, NMEM])
    mtok = w("mtok", 76, [P, 2, D])
    sqx, rstd2 = w("sqx", 76, [P, T]), w("rstd2", 78, [P, T])
    hq, hk, hb, hgate = (w(n, k, [P, HH, T]) for n, k in (("hq", 0), ("hk", 12), ("hb", 24), ("hgate", 36)))
    hv = w("hv", 48, [P, 4, HH * P])
    hA = w("hA", 60, [P, HH, T])
    qm0 = w("qm0", 72, [P, 2, T])
    km0 = w("km0", 84, [P, 2, NMEM])
    vm0 = w("vm0", 86, [P, 2, NMEM])
    hE = at("hE", HR, [P, HH, T])
    hKL = at("hKL", HR + 12 * KB, [P, HH, T])
    hQL = at("hQL", HR + 24 * KB, [P, HH, T // 2])
    hkT = w("hkT", 12, [P, HH, 3, P])
    hS = w("hS", 24, [P, 3, HH, P])
    gh = w("gh", 0, [P, FC, T], F32R)
    gl = w("gl", 44, [P, FC, T], F32R)
    pr0, pt0 = w("pr0", 0, [P, 3, T]), [w("pt00", 12, [P, 4, T]), w("pt01", 24, [P, 4, T])]
    z1 = w("z1", 0, [P, 8, T])
    mqn, mqr, mkn, mkr = (w("mqn", 16, [P, HH, T]), w("mqr", 28, [P, 3, T]), w("mkn", 34, [P, HH, T]),
                          w("mkr", 46, [P, 3, T]))
    mv = w("mv", 52, [P, 4, HH * P])
    cosT, sinT = w("cosT", 64, [P, T]), w("sinT", 66, [P, T])
    pr1, pt1 = w("pr1", 68, [P, 3, T]), [w("pt10", 0, [P, 4, T]), w("pt11", 74, [P, 4, T])]
    kr0 = w("kr0", 82, [P, T])
    rtmp = w("rtmp", 84, [P, 2, T])
    posi = w("posi", 68, [P, T], I32)
    posf = w("posf", 70, [P, 2, T])
    sqr, sqk = w("sqr", 0, [P, 2, T]), w("sqk", 4, [P, T])
    wq, wk, wcz, wvr = (w(n, k, [P, 4, T]) for n, k in (("wq", 0), ("wk", 8), ("wcz", 16), ("wvr", 24)))
    vtok = w("vtok", 32, [P, 8, T])
    wkc, wvc, vct = w("wkc", 48, [P, 4, NMEM]), w("wvc", 52, [P, 4, NMEM]), w("vct", 56, [P, 2, T])
    wbias = w("wbias", 60, [P, 8, 8, 48])
    wbm = w("wbm", 72, [P, 4, NMEM])
    pr2 = w("pr2", 76, [P, 3, T])
    ptw = w("ptw", 24, [P, 4, 4, P])
    vtmp = w("vtmp", 76, [P, 2, D])
    ctok = w("ctok", 76, [P, 2, D])
    ctxT = w("ctxT", 48, [P, KC, NMEM])
    ch, cl = w("ch", 60, [P, KC, NMEM], F32R), w("cl", 68, [P, KC, NMEM], F32R)
    csq = w("csq", 84, [P, 3, NMEM])
    bh, bl = w("bh", 0, [P, 4, T], F32R), w("bl", 8, [P, 4, T], F32R)
    mm_ = w("mm_", 32, [P, KC, T])
    sig = w("sig", 48, [P, KC, T])
    atmp = w("atmp", 16, [P, 2, T])
    az = w("az", 20, [P, 2, T])
    acc2 = w("acc2", 24, [P, 2, T])
    btmp = w("btmp", 28, [P, 2, T])
    fu, fz = w("fu", 16, [P, 4, T]), w("fz", 24, [P, 4, T])
    xc = w("xc", 64, [P, 4, 4, 256])
    dft = w("dft", 48, [P, 8, T])
    dcc = w("dcc", 80, [P, 256])
    yT = w("yT", 0, [P, KC, T])
    ytok = w("ytok", 16, [P, 4, D])

    ps = nc.alloc_psum_tensor("ps", [P, 8, T], F32)

    def cc(name, a=0, n=None):
        return con[:, COFF[name] + a:COFF[name] + a + (n or dict(CON)[name])]

    def vv(name, j=0, n=1):
        return vec[:, VOFF[name] + j:VOFF[name] + j + n]

    nmx, sm, rc = small[:, 0:4], small[:, 4:8], small[:, 8:12]
    lbt, oml = small[:, 12:18], small[:, 18:24]
    lbx = small[:, 24:48]
    cs = small[:, 48:64]
    mod = small[:, 64:112]
    gsc = small[:, 112:128]

    with ExitStack() as ctx:
        def sem(name):
            return ctx.enter_context(nc.semaphore(name))

        raw_ready = [sem("raw_ready0"), sem("raw_ready1")]
        hi_ready, lo_ready = sem("hi_ready"), sem("lo_ready")
        used = sem("used")
        emptied = sem("emptied")
        x_in, v_in, c_in, k_in, m_in = (sem(n) for n in ("x_in", "v_in", "c_in", "k_in", "m_in"))
        tr, ev = sem("tr"), sem("ev")
        sq_ready, sq_added, sum_ready, rstd_ready = sem("sq_ready"), sem("sq_added"), sem("sum_ready"), sem("rstd_ready")
        msq_ready, msq_added = sem("msq_ready"), sem("msq_added")
        t_ready, thi_ready, split_done = sem("t_ready"), sem("thi_ready"), sem("split_done")
        yn_ready, hn_sq, hn_mm, hn_rstd, hn_done = (sem(n) for n in ("yn_ready", "hn_sq", "hn_mm", "hn_rstd", "hn_done"))
        ch_act, ch_dve = sem("ch_act"), sem("ch_dve")
        f_acc, f_tap, f_conv, f_silu, f_g, f_hi, f_lo = (sem(n) for n in ("f_acc", "f_tap", "f_conv", "f_silu", "f_g", "f_hi", "f_lo"))
        g_act, g_dve = sem("g_act"), sem("g_dve")
        lv_d, lv_p, lv_e, lv_k, lv_q, lv_mm, lv_cp = (sem(n) for n in ("lv_d", "lv_p", "lv_e", "lv_k", "lv_q", "lv_mm", "lv_cp"))
        st_k, st_tr, st_tc, st_kv, st_s = (sem(n) for n in ("st_k", "st_tr", "st_tc", "st_kv", "st_s"))
        ho_mm, ho_cp = sem("ho_mm"), sem("ho_cp")
        ada_in = [sem(f"ada_in{i}") for i in range(3)]
        ada_used, ada_cs, ada_row, ada_t, mod_ready = (sem(n) for n in ("ada_used", "ada_cs", "ada_row", "ada_t", "mod_ready"))
        sc_ready, mx_ready, ex_ready, pn_ready, tp_ready, pt_ready, pv_done, o_read = (
            sem(n) for n in ("sc_ready", "mx_ready", "ex_ready", "pn_ready", "tp_ready", "pt_ready", "pv_done", "o_read"))
        bm_ready = sem("bm_ready")
        pos_in, rp_d, rp_a, rot_mm, rot_rd, kq_ready = (sem(n) for n in ("pos_in", "rp_d", "rp_a", "rot_mm", "rot_rd", "kq_ready"))
        q_act, q_dve = sem("q_act"), sem("q_dve")
        ctx_in, b_in, dft_in = sem("ctx_in"), sem("b_in"), sem("dft_in")
        vt_c, vt_tr, vt_ev = sem("vt_c"), sem("vt_tr"), sem("vt_ev")
        df_mm, df_ev = sem("df_mm"), sem("df_ev")
        d1_done = sem("d1_done")
        y_tr, y_ev, out_done = sem("y_tr"), sem("y_ev"), sem("out_done")
        block = ctx.enter_context(nc.Block())


        Q_H0 = 0
        Q_MEM = Q_H0 + 8
        Q_Y0 = Q_MEM + 16
        Q_F0 = Q_Y0 + 8
        Q_H1 = Q_F0 + 8
        Q_C1 = Q_H1 + 8
        Q_Y1 = Q_C1 + 5
        Q_F1 = Q_Y1 + 8
        Q_H2 = Q_F1 + 8
        Q_CTX = Q_H2 + 8
        Q_BC = Q_CTX + 8
        Q_BA = Q_BC + 4
        Q_BF = Q_BA + 4
        Q_M2 = Q_BF + 4
        A_M0, A_MLA, A_M1, A_W = 0, 16, 40, 56
        G_M0, G_MLA, G_M1, G_W = 0, 2, 8, 10
        H_KM, H_HG, H_QM0, H_C1, H_Q1, H_K1, H_QM1 = 0, 2, 8, 10, 12, 18, 24
        HN_IN = [1, 1] + [1] * 6 + [1, 1] + [3, 2] + [2] * 6 + [2] * 6 + [1, 1]
        HN_IN[H_K1 + 1:H_K1 + 6] = [1] * 5
        HN_AT = [sum(HN_IN[:i]) for i in range(len(HN_IN) + 1)]

        def level(x, j):
            hf, h = j % 2, 64 >> j // 2
            return x[:, 3 * hf:3 * hf + 3, :].rearrange("p a t -> p (a t)").rearrange("p (g t) -> p g t", t=2 * h)

        def rst(r):
            return rstd if r % 2 == 0 else rstd2[:]

        def sqbuf(i):
            return sqacc if i % 2 == 0 else sqx[:]

        def uq_bank(par, b):
            return (b, (3, 6, 7)[b])[par != S_UQ % 2]

        def ukv_bank(par):
            return (4, 0)[par != S_UKV % 2]

        def units(kind, layer=0):
            if kind == "mem":
                return [(2, h // 2, h % 2 == 1 and tt == 3) for h in range(4) for tt in range(4)]
            if kind == "mla":
                return [(i + 1, h, i == 3) for h in range(HH) for i in range(4)]
            return [(4, cb * 4 + h // 2, h % 2 == 1) for cb in range(4) for h in range(8)]

        @block.sync
        def _(sp):
            sp.dma_start(xtok[:], dr["x"].rearrange("a (t p) d -> p (a t) d", p=P)).then_inc(x_in, 16)

            def load(s, src):
                if s >= 2:
                    sp.wait_ge(lo_ready, s - 1)
                wd = src.shape[1]
                sp.dma_start(wraw[:, s % 2, 0:wd], src).then_inc(raw_ready[s % 2], 16)

            def load_many(s0, n, dram):
                wd = dram.shape[2]
                i0 = 0
                while s0 + i0 < 2 or (n - i0) % 2:
                    load(s0 + i0, dram[i0])
                    i0 += 1
                with sp.Fori(0, (n - i0) // 2) as i:
                    for u in range(2):
                        s = s0 + i0 + u
                        src = dram[bass.ds(2 * i + (i0 + u), 1), :, :].rearrange("a p n -> (a p) n")
                        sp.wait_ge(lo_ready, 2 * i + (s - 1))
                        sp.dma_start(wraw[:, s % 2, 0:wd], src).then_inc(raw_ready[s % 2], 16)

            load_many(0, S_O0, dr["w0"])
            for s0, dram in ((S_O0, "w0b"), (S_D0, "wd0"), (S_Z1, "w1"), (S_D1, "wd1"), (S_QKV, "w2")):
                load_many(s0, dr[dram].shape[0], dr[dram])
            for q in range(2):
                sp.wait_ge(y_ev, 4 * q + 4)
                sp.dma_start(out.rearrange("a (t p) d -> p (a t) d", p=P)[:, :, q * T:(q + 1) * T],
                             ytok[:, :, q * T:(q + 1) * T]).then_inc(out_done, 16)
            sp.wait_ge(out_done, 32)

        @block.tensor
        def _(pe):
            mm = nc.tensor.matmul

            def three(o, wsl, asl, K, moving_w=False):
                for k in range(K):
                    for n, (a, b) in enumerate(((0, 0), (0, 1), (1, 0))):
                        l, r = (wsl(a, k), asl(b, k)) if not moving_w else (asl(b, k), wsl(a, k))
                        last = mm(o, l, r, start=(k == 0 and n == 0), stop=(k == K - 1 and n == 2))
                return last

            def wv(par, cols, width=256, off=0, n=P):
                return lambda a, k: (whi, wlo)[a][:, par, k * cols + off:k * cols + off + n]

            def hv_(k0=0):
                return lambda a, k: (hh, hl)[a][:, k0 + k, :]

            def first_slot(S, q):
                pe.wait_ge(lo_ready, S + 1)
                for k in range(8):
                    pe.wait_ge(split_done, q + k + 1)
                    for b in range(2):
                        o, w_ = ps[:, 2 * (S % 2) + b, :], wv(S % 2, 256, off=b * P)
                        mm(o, w_(0, k), hh[:, k, :], start=(k == 0), stop=False)
                        mm(o, w_(0, k), hl[:, k, :], start=False, stop=False)
                        last = mm(o, w_(1, k), hh[:, k, :], start=False, stop=(k == 7))
                last.then_inc(used, 1)

            def slot_loop(S, n, body, lead=1, q=None, early=False):
                pe.wait_ge(emptied, S - 1 if early else S)
                i0 = n % 2
                if q is not None:
                    first_slot(S, q)
                    if not i0:
                        pe.wait_ge(lo_ready, S + 2)
                        body((S + 1) % 2).then_inc(used, 1)
                        i0 = 2
                elif i0:
                    pe.wait_ge(lo_ready, S + 1)
                    body(S % 2).then_inc(used, 1)
                m = (n - i0) // 2
                if m == 0:
                    return
                if m == 1:
                    for u in range(2):
                        s = S + i0 + u
                        pe.wait_ge(emptied, max(s - lead, S))
                        pe.wait_ge(lo_ready, s + 1)
                        body(s % 2).then_inc(used, 1)
                    return
                with pe.Fori(0, m) as i:
                    for u in range(2):
                        s = S + i0 + u
                        pe.wait_ge(emptied, 2 * i + (s - lead))
                        pe.wait_ge(lo_ready, 2 * i + (s + 1))
                        body(s % 2).then_inc(used, 1)

            def plain(par, act=None, K=8):
                a = act or hv_()
                for b in range(2):
                    last = three(ps[:, 2 * par + b, :], wv(par, 256, off=b * P), a, K)
                return last

            def ada_slot(a):
                if a >= 4:
                    pe.wait_ge(ada_row, a // 2 - 1)
                pe.wait_ge(ada_in[a % 3], 16 * (a // 3 + 1))
                for k in range(8):
                    last = mm(ps[0:2, 6 + a // 2 % 2, a % 2 * 256:a % 2 * 256 + 256], cs[:, 2 * k:2 * k + 2],
                              ada[:, a % 3, k * 256:(k + 1) * 256], start=(k == 0), stop=(k == 7))
                last.then_inc(ada_used, 1)

            pe.wait_ge(c_in, 16)
            pe.wait_ge(x_in, 16)
            for n in range(8):
                if n >= 2:
                    pe.wait_ge(ev, n - 1)
                for tt in range(4):
                    last = nc.tensor.transpose(ps[:, 4 + n % 2, tt * P:(tt + 1) * P], xtok[:, tt, n * P:(n + 1) * P], cc("ident"))
                last.then_inc(tr, 1)

            def norm_sum(n):
                pe.wait_ge(sq_added, 8 * n + 8)
                mm(ps[:, 7, :], cc("ones"), sqacc, start=True, stop=True).then_inc(sum_ready, 1)

            norm_sum(0)

            pe.wait_ge(ada_cs, 1)
            ada_slot(0)

            def mid_slot(s):
                if s > 1:
                    pe.wait_ge(emptied, s - 1)
                pe.wait_ge(lo_ready, s + 1)
                plain(s % 2).then_inc(used, 1)

            first_slot(S_Z0, Q_H0)
            pe.wait_ge(m_in, 16)
            for n in range(4):
                pe.wait_ge(ev, 8 + n - 1)
                for j in range(4):
                    k, mt = 2 * n + j // 2, j % 2
                    last = nc.tensor.transpose(ps[:, 4 + n % 2, j * P:(j + 1) * P], mtok[:, mt, k * P:(k + 1) * P], cc("ident"))
                last.then_inc(tr, 1)
            for a in range(1, 4):
                ada_slot(a)
            mid_slot(1)
            pe.wait_ge(msq_added, 8)
            mm(ps[:, 4, 0:NMEM], cc("ones"), msq[:, 2, :], start=True, stop=True).then_inc(sum_ready, 1)
            for a in range(4, 7):
                ada_slot(a)
            mid_slot(2)
            for a in range(7, 12):
                ada_slot(a)
            mid_slot(3)
            pe.wait_ge(ada_row, 6)
            for n in range(24):
                last = nc.tensor.transpose(ps[:, 5, 2 * n:2 * n + 2], arow[0:2, n // 2, n % 2 * P:n % 2 * P + P], cc("ident")[0:2, 0:2])
            last.then_inc(ada_t, 1)
            mid_slot(4)
            mid_slot(5)

            def mem_proj(l):
                def act(a, k):
                    return (mh, ml)[a][l][:, k, :]
                s = S_M + 2 * l
                pe.wait_ge(split_done, Q_MEM + 8 * l + 8)
                pe.wait_ge(emptied, s - 1)
                pe.wait_ge(lo_ready, s + 1)
                for b in range(2):
                    last = three(ps[:, 2 * (s % 2), b * NMEM:(b + 1) * NMEM], wv(s % 2, 256, off=b * P), act, 8)
                last.then_inc(used, 1)
                s += 1
                pe.wait_ge(emptied, s - 1)
                pe.wait_ge(lo_ready, s + 1)
                for mt in range(2):
                    last = three(ps[:, 2 * (s % 2), mt * NMEM:(mt + 1) * NMEM], wv(s % 2, 256, n=256),
                                 lambda a, k: act(a, k)[:, mt * P:(mt + 1) * P], 8, moving_w=True)
                last.then_inc(used, 1)

            mem_proj(0)
            mem_proj(1)
            pe.wait_ge(mod_ready, 1)

            def hn_sums(r, mats):
                if r >= 2:
                    pe.wait_ge(hn_rstd, r - 1)
                for j, m in enumerate(mats):
                    i = HN_AT[r] + j
                    pe.wait_ge(hn_sq, i + 1)
                    lhs, rhs = m(i)
                    mm(ps[:, 4 + r % 2, :], lhs, rhs, start=(j == 0), stop=(j == len(mats) - 1)).then_inc(hn_mm, 1)

            def whole(name):
                return lambda i: (cc(name), sqbuf(i))

            for l in range(2):
                hn_sums(H_KM + l, [whole("b64")])

            def tok_major(par):
                for tt in range(4):
                    last = three(ps[:, 2 * par + tt // 2, (tt % 2) * 256:(tt % 2) * 256 + 256], wv(par, 256, n=256),
                                 lambda a, k: (hh, hl)[a][:, k, tt * P:(tt + 1) * P], 8, moving_w=True)
                return last
            slot_loop(S_Z0B, 3, tok_major)
            slot_loop(S_Z0B + 3, 4, plain, early=True)

            for hf in range(2):
                pe.wait_ge(g_dve, 3)
                if hf == 0:
                    pe.wait_ge(emptied, S_O0)
                for h in range(3 * hf, 3 * hf + 3):
                    for c in range(4):
                        last = mm(ps[:, h, c * P:(c + 1) * P], hk[:, h, c * P:(c + 1) * P], hq[:, h, c * P:(c + 1) * P],
                                  start=True, stop=True)
                last.then_inc(lv_mm, 1)
            for j in range(14):
                hf, l = j % 2, j // 2
                pe.wait_ge(lv_k, j + 1)
                pe.wait_ge(lv_q, j + 1)
                pe.wait_ge(lv_cp, j + 1)
                for h3 in range(3):
                    h = 3 * hf + h3
                    for c in range(4):
                        o = h3 * 256 + c * 64
                        last = mm(ps[:, 3 * hf + o // 512, o % 512:o % 512 + 64], hKL[:, h, c * P:(c + 1) * P],
                                  hQL[:, h, c * 64:(c + 1) * 64], start=True, stop=True)
                last.then_inc(lv_mm, 1)
            pe.wait_ge(lv_cp, 16)
            for n in range(HH):
                pe.wait_ge(st_k, n // 3 + 1)
                if n >= 2:
                    pe.wait_ge(st_tc, n - 1)
                for c in range(3):
                    last = nc.tensor.transpose(ps[:, n % 2, c * P:(c + 1) * P], hKL[:, n, c * P:(c + 1) * P], cc("ident"))
                last.then_inc(st_tr, 1)
            for n in range(HH):
                pe.wait_ge(st_tc, n + 1)
                if n >= 2:
                    pe.wait_ge(st_s, n - 1)
                for c in range(3):
                    last = mm(ps[:, 2 + n % 2, c * P:(c + 1) * P], hkT[:, n, c, :], hv[:, c, n * P:(n + 1) * P],
                              start=True, stop=True)
                last.then_inc(st_kv, 1)
            for h in range(HH):
                if h == 0:
                    pe.wait_ge(st_tc, HH)
                pe.wait_ge(st_s, h + 1)
                if h >= 2:
                    pe.wait_ge(ho_cp, h - 1)
                for c in range(4):
                    t = slice(c * P, (c + 1) * P)
                    last = mm(ps[:, h % 2, t], hv[:, c, h * P:(h + 1) * P], hA[:, h, t], start=True, stop=(c == 0))
                    if c:
                        last = mm(ps[:, h % 2, t], hS[:, c - 1, h, :], hq[:, h, t], start=False, stop=True)
                last.then_inc(ho_mm, 1)
                if h >= 1:
                    hn_sums(H_HG + h - 1, [whole("ones")])
            hn_sums(H_HG + 5, [whole("ones")])
            for j in range(2):
                hn_sums(H_QM0 + j, [whole("b64")])

            def attention(kind, U0, G0, scores, pv, ready=None):
                us = units(kind)
                for n in range(len(us) + 3):
                    if n < len(us):
                        u = U0 + n
                        if n < 3:
                            if n == 0 and ready:
                                ready()
                        if u >= 3:
                            pe.wait_ge(ex_ready, u - 2)
                        scores(n, 4 + u % 3).then_inc(sc_ready, 1)
                    if 2 <= n < len(us) + 2:
                        u = U0 + n - 2
                        pe.wait_ge(pn_ready, u + 1)
                        if u >= 2:
                            pe.wait_ge(pt_ready, u - 1)
                        b = (7, 3)[u % 2]
                        for j in range(us[n - 2][0]):
                            last = nc.tensor.transpose(ps[:, b, j * P:(j + 1) * P], prs[kind][:, u % 3, j * P:(j + 1) * P], cc("ident"))
                        last.then_inc(tp_ready, 1)
                    if n >= 3 and us[n - 3][2]:
                        g = G0 + us[n - 3][1]
                        pe.wait_ge(pt_ready, U0 + n - 2)
                        if g >= 2:
                            pe.wait_ge(*OREAD[g - 2])
                        pv(us[n - 3][1], g % 2).then_inc(pv_done, 1)

            OREAD = [(t_ready, q + 1) for q in (*range(Q_Y0 + 6, Q_Y0 + 8), *range(Q_Y1, Q_Y1 + 8))] + [(o_read, n + 1) for n in range(16)]
            prs = {"mem": pr0, "mla": pr1, "win": pr2}

            def mem_attention(l, q, kmm, vmm):
                def scores(n, b):
                    h, tt = n // 4, n % 4
                    r = slice(64 * (h % 2), 64 * (h % 2) + 64)
                    return mm(ps[:, b, 0:NMEM], q[r, h // 2, tt * P:(tt + 1) * P], kmm[r, h // 2, :], start=True, stop=True)

                def pv(g, b):
                    for h in (2 * g, 2 * g + 1):
                        for c in range(2):
                            last = mm(ps[64 * (h % 2):64 * (h % 2) + 64, b, :], vmm[:, c, h * 64:(h + 1) * 64],
                                      pts[l][h % 2][:, c, :], start=(c == 0), stop=(c == 1))
                    return last
                prs["mem"] = (pr0, pr1)[l]
                r = (H_QM0, H_QM1)[l]
                attention("mem", (A_M0, A_M1)[l], (G_M0, G_M1)[l], scores, pv, lambda: pe.wait_ge(hn_done, r + 2))

            pts = [pt0, pt1]
            mem_attention(0, qm0, km0, vm0)
            slot_loop(S_O0, 4, plain, q=Q_Y0)
            norm_sum(1)

            def ffn(S_U, S_D, q, layer):
                slot_loop(S_U, 22, plain, q=q)
                pe.wait_ge(f_lo, 22 * layer + 11)
                with pe.Fori(0, 4) as i:
                    for n in range(2):
                        s = S_D + 2 * n
                        pe.wait_ge(emptied, 4 * i + (s - 2))
                        for hf in range(2):
                            pe.wait_ge(lo_ready, 4 * i + (s + hf + 1))
                            if n == 0 and hf == 1:
                                pe.wait_ge(f_lo, 22 * layer + 22)
                            par = (s + hf) % 2
                            for k in range(11):
                                for m, (a, b) in enumerate(((0, 0), (0, 1), (1, 0))):
                                    last = mm(ps[:, 4 + n, :], (whi, wlo)[a][:, par, k * P:(k + 1) * P],
                                              (gh, gl)[b][:, 11 * hf + k, :],
                                              start=(hf == 0 and k == 0 and m == 0), stop=(hf == 1 and k == 10 and m == 2))
                            last.then_inc(used, 1)

            ffn(S_U0, S_D0, Q_F0, 0)
            norm_sum(2)

            slot_loop(S_Z1, 4, plain, q=Q_H1)
            hn_sums(H_C1, [whole("ones")] * 3)
            hn_sums(H_C1 + 1, [whole("ones")] * 2)
            pe.wait_ge(split_done, Q_C1 + 3)

            def uq(par):
                for b in range(3):
                    last = three(ps[:, uq_bank(par, b), :], wv(par, 384, off=b * P), hv_(), 3)
                return last
            slot_loop(S_UQ, 3, uq)
            pe.wait_ge(split_done, Q_C1 + 5)

            def ukv(par):
                b0 = ukv_bank(par)
                for b in range(2):
                    three(ps[:, b0 + b, :], wv(par, 512, off=b * P), hv_(3), 2)
                for tt in range(4):
                    last = three(ps[:, b0 + 2 + tt // 2, (tt % 2) * 256:(tt % 2) * 256 + 256], wv(par, 512, off=256, n=256),
                                 lambda a, k: (hh, hl)[a][:, 3 + k, tt * P:(tt + 1) * P], 2, moving_w=True)
                return last
            slot_loop(S_UKV, 3, ukv, early=True)
            def half(h, rhs):
                r = slice(64 * (h % 2), 64 * (h % 2) + 64)
                return lambda i: (con[r, COFF["ones"]:COFF["ones"] + P], rhs[r, :])

            def rotate(n, x):
                if n:
                    pe.wait_ge(rot_rd, n)
                mm(ps[:, 6, :], cc("rot"), x, start=True, stop=True).then_inc(rot_mm, 1)

            pe.wait_ge(kq_ready, 1)
            pe.wait_ge(emptied, S_O1)
            rotate(0, z1[:, 5, :])

            def k_sums(h):
                r = H_K1 + h
                pe.wait_ge(hn_rstd, r - 1)
                pe.wait_ge(hn_sq, HN_AT[r + 1])
                mm(ps[:, 4 + r % 2, :], cc("ones"), sqbuf(r), start=True, stop=False)
                mm(ps[:, 4 + r % 2, :], *half(0, sqk[:])(0), start=False, stop=True).then_inc(hn_mm, HN_IN[r])

            for n in range(2 * HH):
                h = n % HH
                if n < HH:
                    hn_sums(H_Q1 + h, [lambda i, r=H_Q1 + h: (cc("ones"), sqbuf(r)), half(h, sqr[:, h % 2, :])])
                else:
                    k_sums(h)
                if n in (2, 4, 6):
                    pe.wait_ge(hn_done, H_Q1 + n)
                    rotate(n // 2, mqr[:, n // 2 - 1, :])
            for j in range(2):
                hn_sums(H_QM1 + j, [lambda i, r=H_QM1 + j: (cc("b64"), sqbuf(r))])

            def mla_scores(n, b):
                h, i = n // 4, n % 4
                r = slice(64 * (h % 2), 64 * (h % 2) + 64)
                wd = (i + 1) * P
                t = slice(i * P, (i + 1) * P)
                mm(ps[:, b, 0:wd], mqn[:, h, t], mkn[:, h, 0:wd], start=True, stop=False)
                mm(ps[:, b, wd - P:wd], cc("ident"), cc("causal"), start=False, stop=False)
                return mm(ps[:, b, 0:wd], mqr[r, h // 2, t], mkr[r, h // 2, 0:wd], start=False, stop=True)

            def mla_pv(h, b):
                for i in range(4):
                    t = slice(i * P, (i + 1) * P)
                    for j in range(i + 1):
                        last = mm(ps[:, b, t], mv[:, j, h * P:(h + 1) * P], pt1[h % 2][:, j, t], start=(j == 0), stop=(j == i))
                return last

            attention("mla", A_MLA, G_MLA, mla_scores, mla_pv, lambda: pe.wait_ge(hn_done, H_QM1 + 2))
            mem_attention(1, z1[:, 6:8, :], km1, vm1)
            slot_loop(S_O1, 4, plain, q=Q_Y1)
            norm_sum(3)
            ffn(S_U1, S_D1, Q_F1, 1)
            norm_sum(4)

            def ctx_tr(n):
                if n >= 2:
                    pe.wait_ge(ev, 12 + n - 1)
                for j in range(4):
                    k, mt = 2 * n + j // 2, j % 2
                    last = nc.tensor.transpose(ps[:, 4 + n % 2, j * P:(j + 1) * P], ctok[:, mt, k * P:(k + 1) * P], cc("ident"))
                last.then_inc(tr, 1)

            pe.wait_ge(ctx_in, 16)
            ctx_tr(0)
            ctx_tr(1)
            slot_loop(S_QKV, 2, plain, q=Q_H2)
            ctx_tr(2)
            ctx_tr(3)
            pe.wait_ge(lo_ready, S_QKV + 3)
            pe.wait_ge(emptied, S_QKV + 1)
            plain(S_QKV % 2).then_inc(used, 1)
            pe.wait_ge(msq_added, 16)
            mm(ps[:, 6, 0:NMEM], cc("ones"), csq[:, 2, :], start=True, stop=True).then_inc(sum_ready, 1)
            pe.wait_ge(lo_ready, S_QKV + 4)
            pe.wait_ge(emptied, S_QKV + 2)
            plain((S_QKV + 1) % 2).then_inc(used, 1)
            pe.wait_ge(split_done, Q_CTX + 8)

            def kv(par):
                for b in range(2):
                    three(ps[:, 4 + par, b * NMEM:(b + 1) * NMEM], wv(par, 256, off=b * P),
                          lambda a, k: (ch, cl)[a][:, k, :], 8)
                return plain(par)
            slot_loop(S_QKV + 4, 2, kv)
            for u in range(2):
                s = S_QKV + 6 + u
                pe.wait_ge(emptied, s - 1)
                pe.wait_ge(lo_ready, s + 1)
                kv(s % 2).then_inc(used, 1)
                for j in (2 * u, 2 * u + 1):
                    pe.wait_ge(vt_c, j + 1)
                    for q in range(3):
                        n = 3 * j + q
                        if n >= 2:
                            pe.wait_ge(vt_ev, n - 1)
                        for i in range(4 if q < 2 else 2):
                            src = vtmp[:, j % 2, (4 * q + i) * P:(4 * q + i + 1) * P] if q < 2 else wvc[:, j, i * P:(i + 1) * P]
                            last = nc.tensor.transpose(ps[:, 6 + n % 2, i * P:(i + 1) * P], src, cc("ident"))
                        last.then_inc(vt_tr, 1)

            def win_scores(n, b):
                cb, h = n // 8, n % 8
                r = slice(64 * (h % 2), 64 * (h % 2) + 64)
                q = wq[r, h // 2, cb * P:(cb + 1) * P]
                ks = wk[r, h // 2, :].rearrange("p (r c) -> p r c", c=64)[:, :, KCS[cb]:KCS[cb] + 32]
                mm(ps[:, b, 0:256].rearrange("p (r c) -> p r c", c=32), q, ks, start=True, stop=True)
                return mm(ps[:, b, 256:512], q, wkc[r, h // 2, :], start=True, stop=True)

            def win_pv(g, b):
                cb, hp = g // 4, g % 4
                for h in (2 * hp, 2 * hp + 1):
                    u = A_W + cb * 8 + h
                    for c in range(4):
                        v = vtok[:, 2 * cb + c, h * 64:(h + 1) * 64] if c < 2 else vct[:, c - 2, h * 64:(h + 1) * 64]
                        last = mm(ps[64 * (h % 2):64 * (h % 2) + 64, b, 0:P], v, ptw[:, u % 4, c, :],
                                  start=(c == 0), stop=(c == 3))
                return last

            def win_ready():
                pe.wait_ge(vt_ev, 12)
                pe.wait_ge(emptied, S_GC)

            attention("win", A_W, G_W, win_scores, win_pv, win_ready)
            pe.wait_ge(o_read, 16)
            slot_loop(S_GC, 4, plain)

            def branch(S, q, hi_first=False):
                pe.wait_ge(split_done, q + 4)
                for s in (S, S + 1):
                    pe.wait_ge(emptied, s - 1 if hi_first else S)
                    pe.wait_ge(lo_ready, s + 1)
                    for b in range(4):
                        last = three(ps[:, 4 * ((s - S + hi_first) % 2) + b, :], wv(s % 2, 512, off=b * P),
                                     lambda a, k: (bh, bl)[a][:, k, :], 4)
                    last.then_inc(used, 1)
            branch(S_BC, Q_BC)
            slot_loop(S_A, 8, plain, early=True)
            slot_loop(S_GA, 4, plain, early=True)
            branch(S_BA, Q_BA)
            slot_loop(S_F, 4, plain, early=True)
            pe.wait_ge(emptied, S_GF)
            pe.wait_ge(dft_in, 32)
            for n in range(8):
                g, q = n // 2, n % 2
                if n >= 2:
                    pe.wait_ge(df_ev, n - 1)
                for i in range(2):
                    tt = 2 * q + i
                    last = mm(ps[:, 4 + n % 2, i * 256:(i + 1) * 256], fu[:, g, tt * P:(tt + 1) * P], dcc[:], start=True, stop=True)
                last.then_inc(df_mm, 1)
            for g in range(4):
                pe.wait_ge(df_ev, 8)
                if g >= 2:
                    pe.wait_ge(t_ready, Q_BF + g - 1)
                for tt in range(4):
                    for i in range(2):
                        last = mm(ps[:, 6 + g % 2, :], xc[:, tt, g, i * P:(i + 1) * P], dft[:, 4 * i + tt, :],
                                  start=(tt == 0 and i == 0), stop=(tt == 3 and i == 1))
                last.then_inc(df_mm, 1)
            slot_loop(S_GF, 4, plain)
            branch(S_BF, Q_BF, hi_first=True)
            slot_loop(S_O2, 4, plain, q=Q_M2)
            norm_sum(5)
            for k in range(8):
                pe.wait_ge(yn_ready, k + 1)
                if k >= 2:
                    pe.wait_ge(y_ev, k - 1)
                for tt in range(4):
                    last = nc.tensor.transpose(ps[:, k % 2, tt * P:(tt + 1) * P], yT[:, k, tt * P:(tt + 1) * P], cc("ident"))
                last.then_inc(y_tr, 1)

        @block.gpsimd
        def _(pool):
            def lo(s, i=None, wd=SLOT):
                n = s + 1 if i is None else 2 * i + (s + 1)
                pool.wait_ge(hi_ready, n)
                nc.gpsimd.tensor_tensor(wlo[:, s % 2, 0:wd], wraw[:, s % 2, 0:wd], whi[:, s % 2, 0:wd].bitcast(F32),
                                        ALU.subtract).then_inc(lo_ready, 1)

            def lo_many(s0, n, wd=SLOT):
                if n % 2:
                    lo(s0, wd=wd)
                s0 += n % 2
                if n < 2:
                    return
                with pool.Fori(0, n // 2) as i:
                    for u in range(2):
                        lo(s0 + u, i, wd)

            lo_many(0, S_O0)
            lo(S_O0)
            lo(S_O0 + 1)
            def left_decays(j):
                h = 64 >> j // 2
                if j == 0:
                    pool.wait_ge(g_dve, 4)
                if j >= 2:
                    pool.wait_ge(lv_k, j - 1)
                    pool.wait_ge(lv_q, j - 1)
                b, e = level(hb, j), level(hE, j)
                nc.gpsimd.tensor_tensor(e[:, :, 0:h], b[:, :, h - 1:h].to_broadcast([P, 3 * T // (2 * h), h]), b[:, :, 0:h],
                                        ALU.subtract).then_inc(lv_p, 1)

            pool.wait_ge(emptied, S_O0)
            left_decays(0)
            for j in range(14):
                h = 64 >> j // 2
                if j < 13:
                    left_decays(j + 1)
                pool.wait_ge(lv_e, j + 1)
                if j >= 2:
                    pool.wait_ge(lv_mm, j + 1)
                kl, k, e = (level(x, j)[:, :, 0:h if j >= 2 else 2 * h] for x in (hKL, hk, hE))
                nc.gpsimd.tensor_tensor(kl, k, e, ALU.mult).then_inc(lv_k, 1)
            lo_many(S_O0 + 2, S_D0 - S_O0 - 2)
            lo_many(S_D0, 16, DSLOT)
            lo_many(S_Z1, S_D1 - S_Z1)
            lo_many(S_D1, 16, DSLOT)
            lo_many(S_QKV, S_GC - S_QKV)
            for n in range(32):
                cb, h = n // 8, n % 8
                if n == 0:
                    pool.wait_ge(b_in, 128)
                if n >= 4:
                    pool.wait_ge(mx_ready, A_W + n - 3)
                off = (0, -8, -8, -16)[cb] + 16
                nc.gpsimd.tensor_tensor(wbm[:, n % 4, :].rearrange("p (r c) -> p r c", c=32), wbias[:, :, h, off:off + 32],
                                        cc("winmask", 32 * cb, 32).unsqueeze(1).to_broadcast([P, 8, 32]),
                                        ALU.add).then_inc(bm_ready, 1)
            lo_many(S_GC, NS - S_GC)

        @block.scalar
        def _(act):
            A = nc.scalar.activation
            link = Chain(act, ch_act)
            state = {"conv": 0, "q": 0, "ada": False}

            act.dma_start(con[:, 0:2 * P], dr["con"][:, 0:2 * P]).then_inc(c_in, 16)
            act.dma_start(vec[:], dr["vec"]).then_inc(v_in, 16)

            def load_ada(a):
                if a >= 3:
                    act.wait_ge(ada_used, a - 2)
                act.dma_start(ada[:, a % 3, :], dr["wada"][a]).then_inc(ada_in[a % 3], 16)

            load_ada(0)
            act.dma_start(con[:, 2 * P:NC], dr["con"][:, 2 * P:NC]).then_inc(k_in, 16)
            act.dma_start(mtok[:], dr["mem"].rearrange("a (t p) d -> p (a t) d", p=P)).then_inc(m_in, 16)
            load_ada(1)
            load_ada(2)

            def conv(s, i=None, step=2):
                k = 0 if i is None else i
                h = step // 2
                if s >= 2 or i is not None:
                    act.wait_ge(used, k * step + (s - 1))
                act.wait_ge(raw_ready[s % 2], k * (16 * h) + 16 * (s // 2 + 1))
                wd = DSLOT if i is None and (S_D0 <= s < S_Z1 or S_D1 <= s < S_QKV) else SLOT
                A(whi[:, s % 2, 0:wd], wraw[:, s % 2, 0:wd], ACT.Copy).then_inc(hi_ready, 1)

            def conv_upto(n):
                while state["conv"] <= min(n, NS - 1):
                    conv(state["conv"])
                    state["conv"] += 1

            def hi(dst, src=None, wd=T):
                q = state["q"]
                act.wait_ge(t_ready, q + 1)
                A(dst, (src if src is not None else tb[q % 2])[:, 0:wd], ACT.Copy).then_inc(thi_ready, 1)
                state["q"] += 1

            def squares(n, wait, ks=range(8)):
                for k in ks:
                    wait(k)
                    i = 8 * n + k
                    if i >= 2:
                        act.wait_ge(sq_added, i - 1)
                    A(tb[k % 2], xT[:, k, :], ACT.Square).then_inc(sq_ready, 1)

            def rnorm(i, src, dst, scale, eps):
                act.wait_ge(sum_ready, i + 1)
                link(A(dst, src, ACT.Ln, bias=eps, scale=scale))
                A(dst, dst, ACT.Exp, scale=-0.5).then_inc(rstd_ready, 1)

            act.wait_ge(v_in, 16)
            A(cs, vv("cc", 0, 16), ACT.Silu).then_inc(ada_cs, 1)
            nc.scalar.preload_act_table_set("natural_log_exp_and_others")
            act.wait_ge(k_in, 16)
            squares(0, lambda k: act.wait_ge(ev, k + 1), range(4))
            conv_upto(0)
            squares(0, lambda k: act.wait_ge(ev, k + 1), range(4, 8))
            rnorm(0, ps[:, 7, :], rstd, 1.0 / D, cc("e1"))
            for k in range(8):
                hi(hh[:, k, :])
            load_ada(3)
            conv_upto(1)
            conv_upto(2)
            for n in range(8):
                act.wait_ge(ev, 8 + n // 2 + 1)
                if n >= 2:
                    act.wait_ge(msq_added, n - 1)
                A(msq[:, n % 2, :], memT[:, n, :], ACT.Square).then_inc(msq_ready, 1)
                if n == 3:
                    for a in range(4, 7):
                        load_ada(a)
            conv_upto(3)
            rnorm(1, ps[:, 4, 0:NMEM], msq[:, 2, :], 1.0 / D, cc("e1"))
            for a in range(7, 10):
                load_ada(a)
            conv_upto(4)
            load_ada(10)
            load_ada(11)
            for l in range(2):
                conv_upto(5 + l)
                for k in range(8):
                    hi(mh[l][:, k, :], wd=NMEM)
            conv_upto(7)

            def hn_sq_(r, tiles):
                for j, (wait, x) in enumerate(tiles):
                    i = HN_AT[r] + j
                    if wait:
                        wait()
                    if i >= 2:
                        act.wait_ge(hn_mm, i - 1)
                    A(sqbuf(i), x, ACT.Square).then_inc(hn_sq, 1)

            def hn_ln(r, scale, eps):
                act.wait_ge(hn_mm, HN_AT[r + 1])
                if r >= 2:
                    act.wait_ge(hn_done, r - 1)
                link(A(rst(r), ps[:, 4 + r % 2, :], ACT.Ln, bias=eps, scale=scale))
                A(rst(r), rst(r), ACT.Exp, scale=-0.5).then_inc(hn_rstd, 1)

            def hn_pipe(items):
                for n in range(len(items) + 1):
                    if n < len(items):
                        items[n][1]()
                    if n:
                        r, _, scale, eps, then = items[n - 1]
                        hn_ln(r, scale, eps)
                        if then:
                            then()

            for l in range(2):
                conv_upto(S_M + 2 * l + 2)
                hn_sq_(H_KM + l, [(lambda: act.wait_ge(emptied, S_M + 2 * l + 1), (km0, km1)[l][:].rearrange("p a b -> p (a b)"))])
                conv_upto(S_M + 2 * l + 3)
            for l in range(2):
                hn_ln(H_KM + l, 1.0 / 64, cc("e1"))
            conv_upto(S_Z0B + 2)
            A(hq[:], hq[:], ACT.Silu).then_inc(g_act, 1)
            conv_upto(S_Z0B + 3)
            A(hk[:], hk[:], ACT.Sigmoid).then_inc(g_act, 1)
            nc.scalar.preload_act_table_set("natural_log_exp_and_others")
            conv_upto(S_Z0B + 4)
            act.wait_ge(g_dve, 1)
            A(lbx[:, 0:18], lbx[:, 0:18], ACT.Exp).then_inc(g_act, 1)
            conv_upto(S_Z0B + 5)
            act.wait_ge(g_dve, 2)
            A(hA[:], hb[:], ACT.Ln).then_inc(g_act, 1)
            conv_upto(S_Z0B + 6)
            conv_upto(S_O0)
            act.wait_ge(emptied, S_Z0B + 6)
            A(hgate[:], hgate[:], ACT.Silu).then_inc(g_act, 1)
            nc.scalar.preload_act_table_set("natural_log_exp_and_others")
            conv_upto(S_O0 + 1)
            for j in range(14):
                hf = j % 2
                act.wait_ge(lv_d, j + 1)
                act.wait_ge(lv_p, j + 1)
                A(hE[:, 3 * hf:3 * hf + 3, :], hE[:, 3 * hf:3 * hf + 3, :], ACT.Exp).then_inc(lv_e, 1)
            for hf in range(2):
                act.wait_ge(lv_d, 15 + hf)
                A(hE[:, 3 * hf:3 * hf + 3, :], hE[:, 3 * hf:3 * hf + 3, :], ACT.Exp).then_inc(lv_e, 1)
            for hf in range(2):
                act.wait_ge(st_k, hf + 1)
                A(hE[:, 3 * hf:3 * hf + 3, :], hb[:, 3 * hf:3 * hf + 3, :], ACT.Exp).then_inc(lv_e, 1)
            for n in range(HH):
                act.wait_ge(st_tr, n + 1)
                A(hkT[:, n, :, :], ps[:, n % 2, 0:3 * P].rearrange("p (c k) -> p c k", k=P), ACT.Copy).then_inc(st_tc, 1)
            hn_pipe([(H_HG + h, lambda h=h: hn_sq_(H_HG + h, [(lambda: act.wait_ge(ho_cp, h + 1), hA[:, h, :])]), 1.0 / P, cc("e1"),
                      (lambda h=h: hi(hh[:, h - 1, :])) if h else None) for h in range(HH)] +
                    [(H_QM0 + j, lambda j=j: hn_sq_(H_QM0 + j, [(None, qm0[:, j, :])]), 1.0, cc("e64"),
                      None if j else lambda: hi(hh[:, 5, :])) for j in range(2)])

            def attention(kind, U0, G0, prb, evac, pvbuf, chunk=None):
                us = units(kind)
                for n in range(len(us) + 4):
                    if n < len(us):
                        u = U0 + n
                        wd = us[n][0] * P
                        act.wait_ge(mx_ready, u + 1)
                        if u >= 3:
                            act.wait_ge(tp_ready, u - 2)
                        A(prb[:, u % 3, 0:wd], ps[:, 4 + u % 3, 0:wd], ACT.Exp, bias=nmx[:, u % 4:u % 4 + 1],
                          accum_out=sm[:, u % 4:u % 4 + 1]).then_inc(ex_ready, 1)
                    if 2 <= n < len(us) + 2:
                        m = n - 2
                        u = U0 + m
                        act.wait_ge(tp_ready, u + 1)
                        w_ = pvbuf(m)
                        if w_:
                            act.wait_ge(pv_done, w_)
                        dst, src = evac(m, ps[:, (7, 3)[u % 2], :])
                        A(dst, src, ACT.Copy).then_inc(pt_ready, 1)
                    if chunk is not None and n >= 4 and us[n - 4][2]:
                        hi(hh[:, chunk + us[n - 4][1], :])

            def mem_att(l):
                def evac(m, b):
                    h, tt = m // 4, m % 4
                    return (pt0, pt1)[l][h % 2][:, 0:2, tt * P:(tt + 1) * P], b[:, 0:256].rearrange("p (c t) -> p c t", t=P)
                G = (G_M0, G_M1)[l]
                attention("mem", (A_M0, A_M1)[l], G, (pr0, pr1)[l], evac, lambda m: G + 1 if m >= 8 else G, 6)

            mem_att(0)

            def out_proj(S, n):
                conv_upto(S + 1)
                conv_upto(S + 2)
                for j in range(4):
                    conv_upto(S + j + (2 if j == 3 else 1))
                    act.wait_ge(emptied, S + j + 1)
                    for k in (2 * j, 2 * j + 1):
                        i = 8 * n + k
                        act.wait_ge(sq_added, i - 1)
                        A(tb[k % 2], xT[:, k, :], ACT.Square).then_inc(sq_ready, 1)

            out_proj(S_O0, 1)
            nc.scalar.preload_act_table_set("natural_log_exp_and_others")
            rnorm(2, ps[:, 7, :], rstd, 1.0 / D, cc("e1"))
            for k in range(8):
                hi(hh[:, k, :])

            def ffn_up(S, layer):
                cw, cb = VOFF[f"cw{layer}"], VOFF[f"cb{layer}"]
                b0 = 22 * layer
                conv_upto(S + 1)
                with act.Fori(0, 11) as i:
                    for u in range(2):
                        s = S + u
                        par = s % 2
                        conv(s + 2, i)
                        act.wait_ge(f_lo, 2 * i + b0)
                        for ab in range(2):
                            col = cb + 22 * ab + u
                            wc = cw + 88 + 22 * ab + u
                            A(scr[:, 2 * u + ab, :], ps[:, 2 * par + ab, :], ACT.Identity, bias=vec[:, bass.ds(2 * i + col, 1)],
                              scale=vec[:, bass.ds(2 * i + wc, 1)]).then_inc(f_acc, 1)
                        act.wait_ge(f_conv, 2 * i + (b0 + u + 1))
                        A(scr[:, 2 * u, :], scr[:, 2 * u, :], ACT.Silu).then_inc(f_silu, 1)
                        act.wait_ge(f_g, 2 * i + (b0 + u + 1))
                        A(gh[:].rearrange("p c t -> p (c t)")[:, bass.ds((2 * i + u) * T, T)], scr[:, 2 * u, :],
                          ACT.Copy).then_inc(f_hi, 1)
                state["conv"] = S + 24

            def ffn_down(S, n):
                for k in range(8):
                    for j in (1, 2, 3) if k == 7 else (1, 2):
                        conv_upto(S + 2 * k + j)
                    act.wait_ge(emptied, S + 2 * k + 2)
                    i = 8 * n + k
                    act.wait_ge(sq_added, i - 1)
                    A(tb[k % 2], xT[:, k, :], ACT.Square).then_inc(sq_ready, 1)

            ffn_up(S_U0, 0)
            ffn_down(S_D0, 2)
            act.wait_ge(used, S_Z1)
            act.dma_start(posi[:], bass.AP(tensor=dr["pos"].tensor, offset=0, ap=[[0, P], [1, T]])).then_inc(pos_in, 16)
            nc.scalar.preload_act_table_set("natural_log_exp_and_others")
            rnorm(3, ps[:, 7, :], rstd, 1.0 / D, cc("e1"))
            for k in range(8):
                hi(hh[:, k, :])
            conv_upto(S_Z1 + 1)
            for j, dst in enumerate((sinT, cosT)):
                act.wait_ge(rp_d, j + 1)
                A(dst[:], posf[:, j, :], ACT.Sin).then_inc(rp_a, 1)
            nc.scalar.preload_act_table_set("natural_log_exp_and_others")
            for s in range(S_Z1 + 1, S_UQ + 1):
                conv_upto(s)
            hn_sq_(H_C1, [(lambda j=j: act.wait_ge(emptied, S_Z1 + j // 2 + 1), z1[:, j, :]) for j in range(3)])
            hn_sq_(H_C1 + 1, [(lambda j=j: act.wait_ge(emptied, S_Z1 + 3), z1[:, 3 + j, :]) for j in range(2)])
            hn_ln(H_C1, 1.0 / 384, cc("e1"))
            for j in range(3):
                hi(hh[:, j, :])
            hn_ln(H_C1 + 1, 1.0 / 256, cc("e1"))
            for j in range(3, 5):
                hi(hh[:, j, :])
            for s in range(S_UQ, S_O1 + 1):
                conv_upto(s)
            conv_upto(S_O1 + 1)
            act.wait_ge(emptied, S_O1)
            act.wait_ge(split_done, Q_C1 + 5)
            def q_squares(h):
                rows = slice(64 * (h % 2), 64 * (h % 2) + 64)
                act.wait_ge(hn_mm, HN_AT[H_Q1 + h - 1])
                A(sqbuf(H_Q1 + h), mqn[:, h, :], ACT.Square).then_inc(hn_sq, 1)
                A(sqr[rows, h % 2, :], mqr[rows, h // 2, :], ACT.Square).then_inc(hn_sq, 1)

            def k_squares(h):
                act.wait_ge(hn_mm, HN_AT[H_K1 + h - 1])
                if h == 0:
                    A(sqk[0:64, :], posf[0:64, 0, :], ACT.Square).then_inc(hn_sq, 1)
                A(sqbuf(H_K1 + h), mkn[:, h, :], ACT.Square).then_inc(hn_sq, 1)

            def m_squares(j):
                act.wait_ge(hn_mm, HN_AT[H_QM1 + j - 1])
                A(sqbuf(H_QM1 + j), z1[:, 6 + j, :], ACT.Square).then_inc(hn_sq, 1)

            hn_pipe([(H_Q1 + h, lambda h=h: q_squares(h), 1.0, cc("e192"), None) for h in range(HH)] +
                    [(H_K1 + h, lambda h=h: k_squares(h), 1.0 / 192, cc("e1"), None) for h in range(HH)] +
                    [(H_QM1 + j, lambda j=j: m_squares(j), 1.0, cc("e64"), None) for j in range(2)])

            def mla_evac(m, b):
                h, i = m // 4, m % 4
                n = i + 1
                return pt1[h % 2][:, 0:n, i * P:(i + 1) * P], b[:, 0:n * P].rearrange("p (c t) -> p c t", t=P)
            act.wait_ge(hn_done, H_QM1 + 2)
            attention("mla", A_MLA, G_MLA, pr1, mla_evac, lambda m: G_MLA + m // 4 - 1 if m >= 8 else G_MLA, 0)
            act.wait_ge(pv_done, G_MLA + 6)
            mem_att(1)
            out_proj(S_O1, 3)
            rnorm(4, ps[:, 7, :], rstd, 1.0 / D, cc("e1"))
            for k in range(8):
                hi(hh[:, k, :])
            ffn_up(S_U1, 1)
            ffn_down(S_D1, 4)

            nc.scalar.preload_act_table_set("natural_log_exp_and_others")
            act.wait_ge(used, S_QKV)
            act.dma_start(ctok[:], dr["ctx"].rearrange("a (t p) d -> p (a t) d", p=P)).then_inc(ctx_in, 16)
            rnorm(5, ps[:, 7, :], rstd, 1.0 / D, cc("e1"))
            for k in range(8):
                hi(hh[:, k, :])
            def ctx_squares(half):
                for n in range(4 * half, 4 * half + 4):
                    act.wait_ge(ev, 12 + n // 2 + 1)
                    act.wait_ge(msq_added, 8 + n - 1)
                    A(csq[:, n % 2, :], ctxT[:, n, :], ACT.Square).then_inc(msq_ready, 1)
            conv_upto(S_QKV + 1)
            ctx_squares(0)
            conv_upto(S_QKV + 2)
            conv_upto(S_QKV + 3)
            ctx_squares(1)
            conv_upto(S_QKV + 4)
            rnorm(6, ps[:, 6, 0:NMEM], csq[:, 2, :], 1.0 / D, cc("e1"))
            for k in range(8):
                hi(ch[:, k, :], wd=NMEM)
            for s in range(S_QKV + 5, S_QKV + 8):
                conv_upto(s)
            act.wait_ge(emptied, S_QKV + 6)
            for j in range(4):
                if j >= 2:
                    conv_upto(S_QKV + 8)
                    act.wait_ge(vt_tr, 3 * (j - 2) + 2)
                for cb in range(4):
                    src = wvr[:, j, :].rearrange("p (r c) -> p r c", c=64)[:, :, KCS[cb]:KCS[cb] + 32]
                    last = A(vtmp[:, j % 2, cb * 256:(cb + 1) * 256].rearrange("p (r c) -> p r c", c=32), src, ACT.Copy)
                last.then_inc(vt_c, 1)
            act.wait_ge(used, S_QKV + 8)
            for r in range(8):
                act.dma_start(wbias[r * 16:r * 16 + 16, :, :, :].rearrange("p a b c -> p (a b) c"),
                              dr["rpb"][:, (7 - r) * 8:(7 - r) * 8 + 64, :]).then_inc(b_in, 16)
            A(wcz[:], wcz[:], ACT.Silu).then_inc(q_act, 1)
            nc.scalar.preload_act_table_set("natural_log_exp_and_others")
            conv_upto(S_GC + 1)
            act.wait_ge(vt_ev, 12)

            def win_evac(m, b):
                return ptw[:, (A_W + m) % 4, :, :], b.rearrange("p (c t) -> p c t", t=P)
            attention("win", A_W, G_W, pr2, win_evac, lambda m: G_W + m // 2 - 1 if m >= 4 else G_W)
            for j in range(4):
                hi(bh[:, j, :])

            def gates(S, n0):
                for j in range(4):
                    conv_upto(S + j + 1)
                    act.wait_ge(emptied, S + j + 1)
                    A(sig[:, 2 * j:2 * j + 2, :], sig[:, 2 * j:2 * j + 2, :], ACT.Sigmoid).then_inc(q_act, 1)
                conv_upto(S + 5)
            gates(S_GC, 1)
            conv_upto(S_A)
            for j in range(4):
                conv_upto(S_A + 2 * j + 1)
                conv_upto(S_A + 2 * j + 2)
                act.wait_ge(emptied, S_A + 2 * j + 2)
                A(az[:, j % 2, :], az[:, j % 2, :], ACT.Silu).then_inc(q_act, 1)
                hi(bh[:, j, :])
            gates(S_GA, 9)
            conv_upto(S_F)
            for s in range(S_F, S_F + 5):
                conv_upto(s)
            act.wait_ge(emptied, S_F + 1)
            act.dma_start(dft[:], dr["dft"].rearrange("a (t p) d -> p (a t) d", p=P)).then_inc(dft_in, 16)
            act.dma_start(dcc[:], dr["dcc"]).then_inc(dft_in, 16)
            act.wait_ge(emptied, S_F + 4)
            A(fz[:], fz[:], ACT.Silu).then_inc(q_act, 1)
            for g in range(4):
                hi(bh[:, g, :])
            gates(S_GF, 14)
            conv_upto(S_BF + 1)
            conv_upto(S_BF + 2)
            for k in range(8):
                hi(hh[:, k, :])
            out_proj(S_O2, 5)
            nc.scalar.preload_act_table_set("natural_log_exp_and_others")
            rnorm(7, ps[:, 7, :], rstd, 1.0 / D, cc("e1"))
            for k in range(8):
                act.wait_ge(y_tr, k + 1)
                A(ytok[:, :, k * P:(k + 1) * P], ps[:, k % 2, :].rearrange("p (a b) -> p a b", b=P), ACT.Copy).then_inc(y_ev, 1)

        @block.vector
        def _(dve):
            V = nc.vector
            TT, TS, STT = V.tensor_tensor, V.tensor_scalar, V.scalar_tensor_tensor
            link = Chain(dve, ch_dve)
            state = {"q": 0, "pend": None}

            def flush():
                if state["pend"] is None:
                    return
                q, src, dh, dl = state["pend"]
                dve.wait_ge(thi_ready, q + 1)
                TT(dl, src, dh.bitcast(F32), ALU.subtract).then_inc(split_done, 1)
                state["pend"] = None

            def split(emit, dh, dl, src=None, wd=T):
                q = state["q"]
                t = (src if src is not None else tb[q % 2])[:, 0:wd]
                if q >= 2:
                    dve.wait_ge(split_done, q - 1)
                emit(t).then_inc(t_ready, 1)
                state["q"] += 1
                flush()
                state["pend"] = (q, t, dh, dl)

            def add_sq(n, k):
                i = 8 * n + k
                dve.wait_ge(sq_ready, i + 1)
                if k:
                    dve.wait_ge(sq_added, i)
                    TT(sqacc, sqacc, tb[k % 2], ALU.add).then_inc(sq_added, 1)
                else:
                    V.tensor_copy(sqacc, tb[k % 2]).then_inc(sq_added, 1)
                if k == 7:
                    dve.wait_ge(sq_added, i + 1)

            def add_msq(buf, n, k):
                i = 8 * n + k
                dve.wait_ge(msq_ready, i + 1)
                if k:
                    dve.wait_ge(msq_added, i)
                    TT(buf[:, 2, :], buf[:, 2, :], buf[:, k % 2, :], ALU.add).then_inc(msq_added, 1)
                else:
                    V.tensor_copy(buf[:, 2, :], buf[:, k % 2, :]).then_inc(msq_added, 1)

            for n in range(8):
                dve.wait_ge(tr, n + 1)
                V.tensor_copy(xT[:, n, :], ps[:, 4 + n % 2, :]).then_inc(ev, 1)
                if n >= 1:
                    add_sq(0, n - 1)
            add_sq(0, 7)

            def norm_h(i, g):
                dve.wait_ge(rstd_ready, i)
                for k in range(8):
                    split(lambda t: STT(out=t, in0=xT[:, k, :], scalar=vv(g, k), in1=rstd, op0=ALU.mult, op1=ALU.mult),
                          hh[:, k, :], hl[:, k, :])
                flush()

            norm_h(1, "mix0")

            def empty(s):
                dve.wait_ge(used, s + 1)

            def bank(s, b):
                return ps[:, 2 * (s % 2) + b, :]

            def copy(dst, src):
                return TS(dst, src, 1.0, None, ALU.mult)

            def hn_apply(r, ops):
                dve.wait_ge(hn_rstd, r + 1)
                for n, (dst, src, g) in enumerate(ops):
                    ins = STT(out=dst, in0=src, scalar=g, in1=rst(r), op0=ALU.mult, op1=ALU.mult)
                ins.then_inc(hn_done, 1)

            def take_z0(s):
                j = s - S_Z0 if s < S_M else s - S_Z0B + 6
                empty(s)
                if 6 <= j < 9:
                    for q in range(2):
                        last = V.tensor_copy(hv[:, 2 * q:2 * q + 2, (j - 6) * 256:(j - 5) * 256],
                                             bank(s, q).rearrange("p (a b) -> p a b", b=256))
                else:
                    dst, n = (hq, 0) if j < 3 else (hk, 6) if j < 6 else (hgate, 18) if j < 12 else (qm0, 24)
                    for b in range(2):
                        last = V.tensor_copy(dst[:, 2 * j + b - n, :], bank(s, b))
                last.then_inc(emptied, 1)

            def ada_rows(r):
                dve.wait_ge(ada_used, 2 * r + 2)
                V.tensor_copy(arow[0:2, 2 * r:2 * r + 2, :].rearrange("p a b -> p (a b)"), ps[0:2, 6 + r % 2, :]).then_inc(ada_row, 1)

            for n in range(4):
                dve.wait_ge(tr, 8 + n + 1)
                V.tensor_copy(memT[:, 2 * n:2 * n + 2, :].rearrange("p a b -> p (a b)"), ps[:, 4 + n % 2, :]).then_inc(ev, 1)
            take_z0(0)
            ada_rows(0)
            for k in range(8):
                add_msq(msq, 0, k)
            ada_rows(1)
            take_z0(1)
            ada_rows(2)
            take_z0(2)
            ada_rows(3)
            ada_rows(4)
            ada_rows(5)
            take_z0(3)
            dve.wait_ge(ada_t, 1)
            link(TT(mod.rearrange("p (n c) -> p n c", c=2), ps[:, 5, 0:48].rearrange("p (n c) -> p n c", c=2),
                    vv("bada", 0, 24).unsqueeze(2).to_broadcast([P, 24, 2]), ALU.add))
            TS(gsc, mod[:, 16:32], 1.0, None, ALU.add).then_inc(mod_ready, 1)
            dve.wait_ge(mod_ready, 1)
            link(TT(gsc.rearrange("p (n c) -> p n c", c=2), gsc.rearrange("p (n c) -> p n c", c=2),
                    vv("ng2", 0, 8).unsqueeze(2).to_broadcast([P, 8, 2]), ALU.mult))

            dve.wait_ge(rstd_ready, 2)
            for l in range(2):
                for k in range(8):
                    split(lambda t: STT(out=t, in0=memT[:, k, :], scalar=vv(f"mem{l}", k), in1=msq[:, 2, :],
                                        op0=ALU.mult, op1=ALU.mult), mh[l][:, k, :], ml[l][:, k, :], wd=NMEM)
                flush()
                take_z0(4 + l)
            for l in range(2):
                s = S_M + 2 * l
                empty(s)
                V.tensor_copy((km0, km1)[l][:].rearrange("p a b -> p (a b)"), bank(s, 0)).then_inc(emptied, 1)
                empty(s + 1)
                V.tensor_copy((vm0, vm1)[l][:].rearrange("p a b -> p (a b)"), bank(s + 1, 0)).then_inc(emptied, 1)
            for l in range(2):
                kk = (km0, km1)[l][:].rearrange("p a b -> p (a b)")
                hn_apply(H_KM + l, [(kk, kk, vv(f"mk{l}"))])
            take_z0(S_Z0B)

            l3 = vv("lb", 0, 18).rearrange("p (r h) -> p r h", h=HH)
            mxl, e3, sl = lbx[:, 18:24], lbx[:, 0:18].rearrange("p (r h) -> p r h", h=HH), lbt
            link(TT(mxl, l3[:, 0, :], l3[:, 1, :], ALU.max))
            link(TT(mxl, mxl, l3[:, 2, :], ALU.max))
            TT(e3, l3, mxl.unsqueeze(1).to_broadcast([P, 3, HH]), ALU.subtract).then_inc(g_dve, 1)
            take_z0(S_Z0B + 1)
            take_z0(S_Z0B + 2)
            dve.wait_ge(g_act, 3)
            link(TT(sl, e3[:, 0, :], e3[:, 1, :], ALU.add))
            link(TT(sl, sl, e3[:, 2, :], ALU.add))
            link(V.reciprocal(sl, sl))
            link(TT(lbt, e3[:, 0, :], sl, ALU.mult))
            link(TS(oml, lbt, -1.0, 1.0, ALU.mult, ALU.add))
            for h in range(HH):
                last = TS(hb[:, h, :], hk[:, h, :], oml[:, h:h + 1], lbt[:, h:h + 1], ALU.mult, ALU.add)
            last.then_inc(g_dve, 1)
            dve.wait_ge(g_dve, 2)
            TS(hk[:], hb[:], -1.0, 1.0, ALU.mult, ALU.add).then_inc(g_dve, 1)
            take_z0(S_Z0B + 3)
            dve.wait_ge(g_act, 4)
            dve.wait_ge(g_dve, 3)
            for h in range(HH):
                last = V.tensor_tensor_scan(hb[:, h, :], cc("scan"), hA[:, h, :], 0.0, ALU.mult, ALU.add)
            last.then_inc(g_dve, 1)

            for j in range(4, 7):
                take_z0(S_Z0B + j)
            SC = float(P) ** -0.5
            dve.wait_ge(g_dve, 4)

            def lv_diff(j):
                h = 64 >> j // 2
                if j >= 2:
                    dve.wait_ge(lv_k, j - 1)
                    dve.wait_ge(lv_q, j - 1)
                b, e = level(hb, j), level(hE, j)
                TT(e[:, :, h:2 * h], b[:, :, h:2 * h], b[:, :, h - 1:h].to_broadcast([P, 3 * T // (2 * h), h]),
                   ALU.subtract).then_inc(lv_d, 1)

            for hf in range(2):
                dve.wait_ge(lv_mm, hf + 1)
                for h in range(3 * hf, 3 * hf + 3):
                    last = STT(out=hA[:, h, :].rearrange("p (c t) -> p c t", t=P), in0=ps[:, h, :].rearrange("p (c t) -> p c t", t=P),
                               scalar=SC, in1=cc("ident").unsqueeze(1).to_broadcast([P, 4, P]), op0=ALU.mult, op1=ALU.mult)
                last.then_inc(lv_cp, 1)
            lv_diff(0)
            for j in range(14):
                hf, l = j % 2, j // 2
                h = 64 >> l
                if j < 13:
                    lv_diff(j + 1)
                dve.wait_ge(lv_e, j + 1)
                if j >= 2:
                    dve.wait_ge(lv_mm, j + 1)
                STT(out=hQL[:, 3 * hf:3 * hf + 3, :].rearrange("p a t -> p (a t)").rearrange("p (g t) -> p g t", t=h),
                    in0=level(hq, j)[:, :, h:2 * h], scalar=SC, in1=level(hE, j)[:, :, h:2 * h],
                    op0=ALU.mult, op1=ALU.mult).then_inc(lv_q, 1)

                def copies(j):
                    hf, l = j % 2, j // 2
                    h = 64 >> l
                    dve.wait_ge(lv_mm, j + 3)
                    dve.wait_ge(lv_cp, 2)
                    n = 64 // h
                    msk = cc("lvl", 64 * l, 64).bitcast(U32).rearrange("p (g t) -> p g t", t=h)
                    for h3 in range(3):
                        o = h3 * 256
                        src = ps[:, 3 * hf + o // 512, o % 512:o % 512 + 256].rearrange("p (c g t) -> p c g t", c=4, t=h)
                        dst = hA[:, 3 * hf + h3, :].rearrange("p (c g t) -> p c g t", c=4, t=2 * h)[:, :, :, h:2 * h]
                        last = V.copy_predicated(dst, msk.unsqueeze(1).to_broadcast([P, 4, n, h]), src)
                    last.then_inc(lv_cp, 1)
                if j >= 1:
                    copies(j - 1)
            def heads(x, hf):
                return x[:, 3 * hf:3 * hf + 3, :].rearrange("p a t -> p (a t)").rearrange("p (g t) -> p g t", t=P)

            for hf in range(2):
                dve.wait_ge(lv_k, 13 + hf)
                dve.wait_ge(lv_q, 13 + hf)
                b4 = heads(hb, hf)
                TT(heads(hE, hf), b4[:, :, P - 1:P].to_broadcast([P, 12, P]), b4, ALU.subtract).then_inc(lv_d, 1)
                if hf == 0:
                    copies(13)
            for hf in range(2):
                dve.wait_ge(lv_e, 15 + hf)
                dve.wait_ge(lv_mm, 15 + hf)
                TT(heads(hKL, hf), heads(hk, hf), heads(hE, hf), ALU.mult).then_inc(st_k, 1)
            for n in range(HH):
                if n % 3 == 0:
                    hf = n // 3
                    dve.wait_ge(lv_e, 17 + hf)
                    link(STT(out=heads(hq, hf), in0=heads(hq, hf), scalar=SC, in1=heads(hE, hf), op0=ALU.mult, op1=ALU.mult))
                dve.wait_ge(st_kv, n + 1)
                for c in range(3):
                    kvp = ps[:, 2 + n % 2, c * P:(c + 1) * P]
                    if c == 0:
                        ins = copy(hS[:, 0, n, :], kvp)
                    else:
                        ins = STT(out=hS[:, c, n, :], in0=hS[:, c - 1, n, :], scalar=hE[:, n, c * P + P - 1:c * P + P], in1=kvp,
                                  op0=ALU.mult, op1=ALU.add)
                    if c < 2:
                        link(ins)
                ins.then_inc(st_s, 1)
            dve.wait_ge(g_act, 5)

            def gated(h):
                split(lambda t: TT(t, hA[:, h, :], hgate[:, h, :], ALU.mult), hh[:, h, :], hl[:, h, :])
            for h in range(HH):
                dve.wait_ge(ho_mm, h + 1)
                V.tensor_copy(hA[:, h, :], ps[:, h % 2, :]).then_inc(ho_cp, 1)
                if h >= 1:
                    hn_apply(H_HG + h - 1, [(hA[:, h - 1, :], hA[:, h - 1, :], vv("hgo"))])
                    dve.wait_ge(hn_done, H_HG + h)
                    gated(h - 1)
            hn_apply(H_HG + 5, [(hA[:, 5, :], hA[:, 5, :], vv("hgo"))])
            dve.wait_ge(hn_done, H_HG + 6)
            gated(5)
            flush()
            for j in range(2):
                hn_apply(H_QM0 + j, [(qm0[:, j, :], qm0[:, j, :], vv("mq0"))])

            def attention(kind, U0, G0, prb, consume):
                us = units(kind)
                for n in range(len(us) + 4):
                    if n < len(us):
                        u = U0 + n
                        wd = us[n][0] * P
                        dve.wait_ge(sc_ready, u + 1)
                        if kind == "win":
                            dve.wait_ge(bm_ready, n + 1)
                            b = ps[:, 4 + u % 3, 0:256]
                            link(TT(b, b, wbm[:, n % 4, :], ALU.add))
                        V.tensor_reduce(nmx[:, u % 4:u % 4 + 1], ps[:, 4 + u % 3, 0:wd], AX, ALU.max,
                                        negate=True).then_inc(mx_ready, 1)
                    if 1 <= n < len(us) + 1:
                        u = U0 + n - 1
                        wd = us[n - 1][0] * P
                        dve.wait_ge(ex_ready, u + 1)
                        link(V.reciprocal(rc[:, u % 4:u % 4 + 1], sm[:, u % 4:u % 4 + 1]))
                        x = prb[:, u % 3, 0:wd]
                        TS(x, x, rc[:, u % 4:u % 4 + 1], None, ALU.mult).then_inc(pn_ready, 1)
                    if n >= 4 and us[n - 4][2]:
                        g = us[n - 4][1]
                        dve.wait_ge(pv_done, G0 + g + 1)
                        consume(g, (G0 + g) % 2)

            def take(c):
                def f(g, b):
                    split(lambda t: copy(t, ps[:, b, :]), hh[:, c + g, :], hl[:, c + g, :])
                return f

            attention("mem", A_M0, G_M0, pr0, take(6))
            flush()

            def out_proj(S, n, gate=None):
                for j in range(4):
                    s = S + j
                    empty(s)
                    for b in range(2):
                        x = xT[:, 2 * j + b, :]
                        if gate is None:
                            last = TT(x, x, bank(s, b), ALU.add)
                        else:
                            last = STT(out=x, in0=bank(s, b), scalar=gate(2 * j + b), in1=x, op0=ALU.mult, op1=ALU.add)
                    last.then_inc(emptied, 1)
                    for k in (2 * j - 2, 2 * j - 1):
                        if k >= 0:
                            add_sq(n, k)
                add_sq(n, 6)
                add_sq(n, 7)

            out_proj(S_O0, 1)
            norm_h(3, "ffn0")

            def ffn_up(S, layer):
                cw = VOFF[f"cw{layer}"]
                b0 = 22 * layer
                with dve.Fori(0, 11) as i:
                    for u in range(2):
                        s = S + u
                        par = s % 2
                        n = 2 * b0 + 2 * u
                        a, b = scr[:, 2 * u, :], scr[:, 2 * u + 1, :]
                        pa, pb = ps[:, 2 * par, :], ps[:, 2 * par + 1, :]

                        def tap(dst, src, d, col, sm_):
                            STT(out=dst[:, d:T], in0=src[:, 0:T - d], scalar=vec[:, bass.ds(2 * i + col, 1)], in1=dst[:, d:T],
                                op0=ALU.mult, op1=ALU.add).then_inc(sm_, 1)
                        dve.wait_ge(f_acc, 4 * i + (n + 1))
                        tap(a, pa, 1, cw + 44 + u, f_tap)
                        dve.wait_ge(f_acc, 4 * i + (n + 2))
                        tap(b, pb, 1, cw + 44 + 22 + u, f_tap)
                        dve.wait_ge(f_tap, 4 * i + (n + 1))
                        tap(a, pa, 2, cw + u, f_conv)
                        dve.wait_ge(f_tap, 4 * i + (n + 2))
                        tap(b, pb, 2, cw + 22 + u, emptied)
                        dve.wait_ge(f_silu, 2 * i + (b0 + u + 1))
                        dve.wait_ge(emptied, 2 * i + (s + 1))
                        TT(a, a, b, ALU.mult).then_inc(f_g, 1)
                        dve.wait_ge(f_hi, 2 * i + (b0 + u + 1))
                        sl_ = bass.ds((2 * i + u) * T, T)
                        TT(gl[:].rearrange("p c t -> p (c t)")[:, sl_], a,
                           gh[:].rearrange("p c t -> p (c t)")[:, sl_].bitcast(F32), ALU.subtract).then_inc(f_lo, 1)

            def ffn_down(S, n):
                dve.wait_ge(f_lo, 22 * (n // 2))
                for k in range(8):
                    empty(S + 2 * k + 1)
                    x = xT[:, k, :]
                    TT(x, x, ps[:, 4 + k % 2, :], ALU.add).then_inc(emptied, 2)
                    if k:
                        add_sq(n, k - 1)
                add_sq(n, 7)

            ffn_up(S_U0, 0)
            ffn_down(S_D0, 2)

            norm_h(4, "mix1")
            dve.wait_ge(pos_in, 16)
            link(V.tensor_copy(rtmp[:, 0, :], posi[:]))
            ang = rtmp[:, 0, :]
            link(TS(ang, ang, cc("inv"), None, ALU.mult))
            for j in range(2):
                n_, r_ = rtmp[:, 1, :], posf[:, j, :]
                link(TS(n_, ang, 1.0 / TWO_PI, 0.25 * j, ALU.mult, ALU.add))
                link(TS(n_, n_, MAGIC, -MAGIC, ALU.add, ALU.add))
                link(STT(out=r_, in0=n_, scalar=-C1, in1=ang, op0=ALU.mult, op1=ALU.add))
                link(STT(out=r_, in0=n_, scalar=-C2, in1=r_, op0=ALU.mult, op1=ALU.add))
                link(STT(out=r_, in0=n_, scalar=-C3, in1=r_, op0=ALU.mult, op1=ALU.add))
                if j:
                    link(TS(r_, r_, float(np.pi / 2), None, ALU.add))
                TS(r_, r_, 3.1415925, -3.1415925, ALU.min, ALU.max).then_inc(rp_d, 1)
            for s in range(S_Z1, S_UQ):
                empty(s)
                for b in range(2):
                    last = V.tensor_copy(z1[:, 2 * (s - S_Z1) + b, :], bank(s, b))
                last.then_inc(emptied, 1)
            for r, (c0, nn, g) in enumerate(((0, 3, "qa"), (3, 2, "kva"))):
                dve.wait_ge(hn_rstd, H_C1 + r + 1)
                for j in range(nn):
                    split(lambda t: STT(out=t, in0=z1[:, c0 + j, :], scalar=vv(g, j), in1=rst(H_C1 + r), op0=ALU.mult, op1=ALU.mult),
                          hh[:, c0 + j, :], hl[:, c0 + j, :])
                flush()
                dve.wait_ge(split_done, state["q"])
                dve.sem_inc(hn_done, 1)
            dve.wait_ge(rp_a, 2)
            link(V.tensor_copy(posf[:, 0, :], z1[:, 5, :]))
            TS(z1[:, 5, :], z1[:, 5, :], vv("knr"), None, ALU.mult).then_inc(kq_ready, 1)
            for s in range(S_UQ, S_UKV):
                p = s - S_UQ
                empty(s)
                for b, dst in enumerate((mqn[:, 2 * p, :], mqn[:, 2 * p + 1, :], mqr[:, p, :])):
                    last = V.tensor_copy(dst, ps[:, uq_bank(s % 2, b), :])
                last.then_inc(emptied, 1)
            for s in range(S_UKV, S_O1):
                p, b0 = s - S_UKV, ukv_bank(s % 2)
                empty(s)
                V.tensor_copy(mkn[:, 2 * p, :], ps[:, b0, :])
                V.tensor_copy(mkn[:, 2 * p + 1, :], ps[:, b0 + 1, :])
                for q in range(2):
                    last = V.tensor_copy(mv[:, 2 * q:2 * q + 2, p * 256:(p + 1) * 256],
                                         ps[:, b0 + 2 + q, :].rearrange("p (a b) -> p a b", b=256))
                last.then_inc(emptied, 1)

            def rope(dst, x, r):
                dve.wait_ge(rot_mm, r + 1)
                TT(rtmp[:, 0, :], ps[:, 6, :], sinT[:], ALU.mult).then_inc(rot_rd, 1)
                link(TT(rtmp[:, 1, :], x, cosT[:], ALU.mult))
                dve.wait_ge(rot_rd, r + 1)
                link(TT(dst, rtmp[:, 0, :], rtmp[:, 1, :], ALU.add))

            rope(kr0[:], z1[:, 5, :], 0)
            for n in range(2 * HH):
                h = n % HH
                rows = slice(64 * (h % 2), 64 * (h % 2) + 64)
                r = (H_Q1, H_K1)[n // HH] + h
                x, g = (mqn, "qnn") if n < HH else (mkn, "knn")
                dve.wait_ge(hn_rstd, r + 1)
                if n < HH:
                    STT(out=mqr[rows, h // 2, :], in0=mqr[rows, h // 2, :], scalar=vv("qnr")[rows, :], in1=rst(r)[rows, :],
                        op0=ALU.mult, op1=ALU.mult)
                else:
                    TT(mkr[rows, h // 2, :], kr0[rows, :], rst(r)[rows, :], ALU.mult)
                STT(out=x[:, h, :], in0=x[:, h, :], scalar=vv(g), in1=rst(r), op0=ALU.mult, op1=ALU.mult).then_inc(hn_done, 1)
                if n in (2, 4, 6):
                    rope(mqr[:, n // 2 - 1, :], mqr[:, n // 2 - 1, :], n // 2)
            for j in range(2):
                hn_apply(H_QM1 + j, [(z1[:, 6 + j, :], z1[:, 6 + j, :], vv("mq1"))])
            attention("mla", A_MLA, G_MLA, pr1, take(0))
            flush()
            attention("mem", A_M1, G_M1, pr1, take(6))
            flush()
            out_proj(S_O1, 3)
            norm_h(5, "ffn1")
            ffn_up(S_U1, 1)
            ffn_down(S_D1, 4)

            def norm_mod(i, src, rs, K, c, dh, dl, wd):
                dve.wait_ge(rstd_ready, i)
                for k in range(8):
                    def emit(t):
                        link(STT(out=t, in0=src[:, k, :], scalar=gsc[:, 2 * k + c:2 * k + c + 1], in1=rs, op0=ALU.mult, op1=ALU.mult))
                        return TS(t, t, mod[:, 2 * k + c:2 * k + c + 1], None, ALU.add)
                    split(emit, dh[:, k, :], dl[:, k, :], wd=wd)
                flush()

            norm_mod(6, xT, rstd, 8, 0, hh, hl, T)
            def ctx_in_half(half):
                for n in (2 * half, 2 * half + 1):
                    dve.wait_ge(tr, 12 + n + 1)
                    V.tensor_copy(ctxT[:, 2 * n:2 * n + 2, :].rearrange("p a b -> p (a b)"), ps[:, 4 + n % 2, :]).then_inc(ev, 1)
                for k in range(4 * half, 4 * half + 4):
                    add_msq(csq, 1, k)

            ctx_in_half(0)

            def bcol(n):
                return vv("bin", n)
            B_AX, B_AB, B_AC, B_AZ, B_FU, B_FZ, B_Q, B_K, B_V, B_CZ, B_GA, B_GF, B_GC = 0, 4, 8, 12, 16, 20, 24, 28, 32, 36, 40, 48, 56
            for s in (S_QKV, S_QKV + 1):
                empty(s)
                for b in range(2):
                    j = 2 * (s - S_QKV) + b
                    for cb in range(4):
                        last = TS(wq[:, j, cb * P:(cb + 1) * P].rearrange("p (r q) -> p r q", q=16),
                                  bank(s, b).rearrange("p (r c q) -> p r c q", c=4, q=16)[:, :, cb, :],
                                  bcol(B_Q + j), 0.125, ALU.add, ALU.mult)
                last.then_inc(emptied, 1)
            ctx_in_half(1)

            def take_cz(u):
                s = S_QKV + 2 + u
                empty(s)
                for b in range(2):
                    last = TS(wcz[:, 2 * u + b, :], bank(s, b), bcol(B_CZ + 2 * u + b), None, ALU.add)
                last.then_inc(emptied, 1)
            take_cz(0)
            norm_mod(7, ctxT, csq[:, 2, :], 8, 1, ch, cl, NMEM)
            take_cz(1)

            def take_kv(s, lat, cxt, bb):
                empty(s)
                for b in range(2):
                    j = 2 * ((s - S_QKV) % 2) + b
                    TS(lat[:, j, :], bank(s, b), bcol(bb + j), None, ALU.add)
                    last = TS(cxt[:, j, :], ps[:, 4 + s % 2, b * NMEM:(b + 1) * NMEM], bcol(bb + j), None, ALU.add)
                last.then_inc(emptied, 1)
            take_kv(S_QKV + 4, wvr, wvc, B_V)
            take_kv(S_QKV + 5, wvr, wvc, B_V)
            for u in range(2):
                take_kv(S_QKV + 6 + u, wk, wkc, B_K)
                for j in (2 * u, 2 * u + 1):
                    for q in range(3):
                        n = 3 * j + q
                        dve.wait_ge(vt_tr, n + 1)
                        if q < 2:
                            last = V.tensor_copy(vtok[:, 4 * q:4 * q + 4, j * P:(j + 1) * P], ps[:, 6 + n % 2, :].rearrange("p (a b) -> p a b", b=P))
                        else:
                            last = V.tensor_copy(vct[:, :, j * P:(j + 1) * P], ps[:, 6 + n % 2, 0:256].rearrange("p (a b) -> p a b", b=P))
                        last.then_inc(vt_ev, 1)
            dve.wait_ge(q_act, 1)

            def win_take(g, b):
                cb, hp = g // 4, g % 4
                y = wcz[:, hp, :].rearrange("p (r c q) -> p r c q", c=4, q=16)[:, :, cb, :]
                TT(y, ps[:, b, 0:P].rearrange("p (r q) -> p r q", q=16), y, ALU.mult).then_inc(o_read, 1)
            attention("win", A_W, G_W, pr2, win_take)
            dve.wait_ge(o_read, 16)
            for j in range(4):
                split(lambda t: copy(t, wcz[:, j, :]), bh[:, j, :], bl[:, j, :])
            flush()

            def gates(S, bb):
                for j in range(4):
                    empty(S + j)
                    for b in range(2):
                        last = TS(sig[:, 2 * j + b, :], bank(S + j, b), bcol(bb + 2 * j + b), None, ALU.add)
                    last.then_inc(emptied, 1)

            def branch(S, n, first):
                dve.wait_ge(q_act, n)
                for s in (S, S + 1):
                    empty(s)
                    for b in range(4):
                        k = 4 * (s - S) + b
                        o = ps[:, 4 * (s - S) + b, :]
                        if first:
                            last = TT(mm_[:, k, :], o, sig[:, k, :], ALU.mult)
                        else:
                            last = TT(sig[:, k, :], o, sig[:, k, :], ALU.mult)
                    last.then_inc(emptied, 1)
                if not first:
                    dve.wait_ge(emptied, S + 2)
                    link(TT(mm_[:], mm_[:], sig[:], ALU.add))

            gates(S_GC, B_GC)
            branch(S_BC, 5, True)
            for j in range(4):
                s = S_A + 2 * j
                p_ = atmp[:, 0, :]
                empty(s)
                link(TS(atmp[:, 1, :], bank(s, 0), bcol(B_AC + j), None, ALU.add))
                STT(out=p_, in0=bank(s, 1), scalar=bcol(B_AX + j), in1=atmp[:, 1, :], op0=ALU.add, op1=ALU.mult).then_inc(emptied, 1)
                dve.wait_ge(emptied, s + 1)
                a = acc2[:, j % 2, :]
                link(TS(a, p_, vv("wc2", 4 + j), vv("bc2", j), ALU.mult, ALU.add))
                link(STT(out=a[:, 1:T], in0=p_[:, 0:T - 1], scalar=vv("wc2", j), in1=a[:, 1:T], op0=ALU.mult, op1=ALU.add))
                link(STT(out=a[:, 0:T - 1], in0=p_[:, 1:T], scalar=vv("wc2", 8 + j), in1=a[:, 0:T - 1], op0=ALU.mult, op1=ALU.add))
                empty(s + 1)
                link(STT(out=a, in0=bank(s + 1, 0), scalar=bcol(B_AB + j), in1=a, op0=ALU.add, op1=ALU.mult))
                TS(az[:, j % 2, :], bank(s + 1, 1), bcol(B_AZ + j), None, ALU.add).then_inc(emptied, 1)
                dve.wait_ge(q_act, 5 + j + 1)
                split(lambda t: TT(t, a, az[:, j % 2, :], ALU.mult), bh[:, j, :], bl[:, j, :])
            flush()
            gates(S_GA, B_GA)
            branch(S_BA, 13, False)
            for s in range(S_F, S_F + 4):
                j0 = s - S_F
                empty(s)
                for b in range(2):
                    j = 2 * (j0 % 2) + b
                    last = TS((fu, fz)[j0 // 2][:, j, :], bank(s, b), bcol((B_FU, B_FZ)[j0 // 2] + j), None, ALU.add)
                last.then_inc(emptied, 1)
            for n in range(8):
                g, q = n // 2, n % 2
                dve.wait_ge(df_mm, n + 1)
                TS(xc[:, 2 * q:2 * q + 2, g, :], ps[:, 4 + n % 2, :].rearrange("p (a b) -> p a b", b=256), 1.0 / 256, None,
                   ALU.mult).then_inc(df_ev, 1)
            dve.wait_ge(q_act, 14)
            for g in range(4):
                dve.wait_ge(df_mm, 8 + g + 1)
                split(lambda t: TT(t, ps[:, 6 + g % 2, :], fz[:, g, :], ALU.mult), bh[:, g, :], bl[:, g, :])
            flush()
            gates(S_GF, B_GF)
            dve.wait_ge(q_act, 18)
            for s in (S_BF, S_BF + 1):
                empty(s)
                for b in range(4):
                    k = 4 * (s - S_BF) + b
                    ins = TT(sig[:, k, :], ps[:, 4 * ((s - S_BF + 1) % 2) + b, :], sig[:, k, :], ALU.mult)
                    if b == 3:
                        ins.then_inc(emptied, 1)
                        dve.wait_ge(emptied, s + 1)
                    else:
                        link(ins)
                    split(lambda t: TT(t, mm_[:, k, :], sig[:, k, :], ALU.add), hh[:, k, :], hl[:, k, :])
            flush()
            out_proj(S_O2, 5, gate=lambda k: mod[:, 32 + 2 * k:33 + 2 * k])
            dve.wait_ge(rstd_ready, 8)
            for k in range(8):
                STT(out=yT[:, k, :], in0=xT[:, k, :], scalar=vv("fin", k), in1=rstd, op0=ALU.mult, op1=ALU.mult).then_inc(yn_ready, 1)


def slots(wm, K, cols):
    n = wm.shape[1] // cols
    return np.ascontiguousarray(wm.reshape(K, P, n, cols).transpose(2, 1, 0, 3).reshape(n, P, K * cols))


def padded(a):
    return np.concatenate([a, np.zeros((a.shape[0], P, SLOT - a.shape[2]), a.dtype)], axis=2) if a.shape[2] < SLOT else a


def paired(wm, a, b, n):
    x = wm[:, a:a + n * P].reshape(-1, n, 1, P)
    y = wm[:, b:b + n * P].reshape(-1, n, 1, P)
    return slots(np.concatenate([x, y], axis=2).reshape(-1, 2 * n * P), 8, 256)


def down(wm):
    return np.ascontiguousarray(wm.reshape(2, 11, P, 8, P).transpose(3, 0, 2, 1, 4).reshape(16, P, DSLOT))


def columns(v):
    return v.reshape(-1, P).T


def constants():
    c = {n: np.zeros((P, k), np.float32) for n, k in CON}
    c["ones"][:] = 1
    c["ident"][:] = np.eye(P)
    c["b64"][:64, :64] = c["b64"][64:, 64:] = 1
    for b in (0, 64):
        for j in range(32):
            c["rot"][b + j + 32, b + j] = -1
            c["rot"][b + j, b + j + 32] = 1
    i = np.arange(P)
    c["causal"][:] = np.where(i[None, :] <= i[:, None], 0, NEG)
    for cb in range(4):
        q = cb * 16 + i % 16
        lo = np.clip(q - 8, 0, 48)
        kc = KCS[cb] + np.arange(32)
        c["winmask"][:, cb * 32:(cb + 1) * 32] = np.where((kc >= lo[:, None]) & (kc < lo[:, None] + 16), 0, NEG)
    c["scan"][:] = (np.arange(T) % P != 0)
    for l in range(7):
        h = 64 >> l
        t = np.arange(64)
        c["lvl"][:, 64 * l:64 * l + 64] = i[:, None] // h == 2 * (t // h)[None, :]
    c["inv"][:, 0] = np.float32(10000.0) ** (-(i % 32).astype(np.float32) / np.float32(32))
    c["e1"][:], c["e64"][:], c["e192"][:] = EPS, 64 * EPS, 192 * EPS
    return np.concatenate([c[n] for n, _ in CON], axis=1)


def layout(i):
    d = {"x": i["x"], "mem": i["mem"], "pos": i["positions"], "ctx": i["ctx_2"]}
    mk, z = i["w_mem_kv"], slots(i["hg_w_in"][0], 8, 256)
    d["w0"] = np.concatenate([z[:6], slots(mk[0], 8, 256), slots(mk[1], 8, 256), z[6:]])

    def out_up(l):
        return [slots(i["w_out"][l], 8, 256), paired(i["w_up"][l], 0, FF, FC)]
    d["w0b"] = np.concatenate(out_up(0))
    d["wd0"], d["wd1"] = down(i["w_down"][0]), down(i["w_down"][1])
    win = i["mla_w_in"][0]
    z = np.concatenate([win[:, 0:704], win[:, 640:704], win[:, 704:960]], axis=1)
    uq = i["mla_w_uq"][0].reshape(384, 3, 2, 192)
    uq = np.concatenate([uq[:, :, :, 0:128].reshape(384, 3, 256), uq[:, :, :, 128:192].reshape(384, 3, 128)], axis=2)
    ukv = i["mla_w_ukv"][0].reshape(256, 3, 2, 2, 128).transpose(0, 1, 3, 2, 4)
    d["w1"] = np.concatenate([slots(z, 8, 256), padded(slots(uq.reshape(384, 1152), 3, 384)),
                              padded(slots(ukv.reshape(256, 1536), 2, 512))] + out_up(1))
    w2 = i["w_in_2"][0]
    br = lambda n: slots(i[n][0], 4, 512)
    conv = np.stack([paired(w2, 1024, 0, 4), paired(w2, 512, 1536, 4)], axis=1).reshape(8, P, SLOT)
    d["w2"] = np.concatenate([*(slots(w2[:, a:a + 512], 8, 256) for a in (3072, 4608, 4096, 3584)), slots(w2[:, 7168:8192], 8, 256), br("w_br_c_2"),
                              conv, slots(w2[:, 5120:6144], 8, 256), br("w_br_a_2"),
                              slots(w2[:, 2048:3072], 8, 256), slots(w2[:, 6144:7168], 8, 256), br("w_br_f_2"),
                              slots(i["w_out_2"][0], 8, 256)])
    d["wada"] = slots(i["w_ada_2"][0], 8, 256)
    r = i["rpb_2"][0].transpose(1, 0, 2)
    r = np.pad(r, ((0, 0), (0, 0), (16, 17))).reshape(120, 64)
    d["rpb"] = np.stack([r[:, 15 - q:63 - q] for q in range(16)])
    twice = lambda v: np.concatenate([v, v]).reshape(P, 1)
    v = {}
    for l in range(2):
        v[f"mix{l}"], v[f"ffn{l}"], v[f"mem{l}"] = (columns(i[n][l]) for n in ("mix_norm_g", "ffn_norm_g", "mem_norm_g"))
        v[f"cw{l}"], v[f"cb{l}"] = columns(i["conv_w"][l]), columns(i["conv_b"][l])
        v[f"mq{l}"], v[f"mk{l}"] = twice(i["mem_q_norm_g"][l]), twice(i["mem_k_norm_g"][l])
    v["bin"], v["bada"], v["ng2"], v["fin"] = columns(i["b_in_2"][0]), columns(i["b_ada_2"][0]), columns(i["norm_g_2"][0]), columns(i["final_g_2"])
    v["wc2"], v["bc2"] = columns(i["w_conv_2"][0]), columns(i["b_conv_2"][0])
    v["cc"] = np.stack([columns(i["c_2"][0]), columns(i["c_ctx_2"])], axis=2).reshape(P, 16)
    v["lb"], v["hgo"] = columns(i["hg_lb_logits"]), columns(i["hg_out_norm_g"][0])
    v["qa"], v["kva"] = columns(i["mla_qa_norm_g"][0]), columns(i["mla_kva_norm_g"][0])
    for n, k in (("qn", "mla_q_norm_g"), ("kn", "mla_k_norm_g")):
        v[n + "n"], v[n + "r"] = i[k][0][0:128].reshape(P, 1), twice(i[k][0][128:192])
    d["vec"] = np.ascontiguousarray(np.concatenate([v[n] for n, _ in VEC], axis=1))
    d["con"] = constants()
    t = np.arange(T)
    a = (t[:, None] * t[None, :] % T) * (TWO_PI / T)
    c = np.arange(P)
    b = (c[:, None] * c[None, :] % P) * (TWO_PI / P)
    d["dft"] = np.stack([np.cos(a), np.sin(a)]).astype(np.float32)
    d["dcc"] = np.concatenate([np.cos(b), -np.sin(b)], axis=1).astype(np.float32)
    return d


def kernel(**inputs):
    import concourse.bacc as bacc
    from concourse.bass_utils import run_bass_kernel_spmd as run

    nc = bacc.Bacc("TRN2", target_bir_lowering=False, num_devices=1)
    arrays, dr = {}, {}
    for name, a in layout({k: np.asarray(v) for k, v in inputs.items()}).items():
        a = np.ascontiguousarray(a)
        arrays["in_" + name] = a
        dr[name] = nc.dram_tensor("in_" + name, a.shape, mybir.dt.from_np(a.dtype), kind="ExternalInput").ap()
    out = nc.dram_tensor("out_0", (1, T, D), F32, kind="ExternalOutput").ap()
    build(nc, dr, out)
    return run(nc, [arrays], core_ids=[0]).results[0]["out_0"]
```
